# Optimizing a Trainium2 kernel written in Bass

```python
import math
import jax, jax.numpy as jnp
from jax import lax
import numpy as np

D_MODEL = 1024
BATCH = 1
SEQ = 256
DEPTH = 2

HG_HEADS = 4
HG_DK = 128
HG_DV = 128
HG_K = HG_HEADS * HG_DK
HG_V = HG_HEADS * HG_DV
HG_CHUNK = 64
SG_GROUPS = 4
SG_WIDTH = 512
SG_GROUP_DIM = SG_WIDTH // SG_GROUPS
SG_CHUNK = 128
D_FF = 2816
ALPHA = (2 * DEPTH) ** 0.25
BETA = (8 * DEPTH) ** -0.25
LN_EPS = 1e-5
RMS_EPS = 1e-6
D_IN = 2 * HG_K + 2 * HG_V + 2 * SG_WIDTH + 2 * D_MODEL
IN_SPLITS = (HG_K,
             2 * HG_K,
             2 * HG_K + HG_V,
             2 * HG_K + 2 * HG_V,
             2 * HG_K + 2 * HG_V + SG_WIDTH,
             2 * HG_K + 2 * HG_V + 2 * SG_WIDTH,
             2 * HG_K + 2 * HG_V + 2 * SG_WIDTH + D_MODEL)


def layer_norm(x, g, b):
    xf = x.astype(jnp.float32)
    mu = jnp.mean(xf, axis=-1, keepdims=True)
    var = jnp.mean(jnp.square(xf - mu), axis=-1, keepdims=True)
    y = (xf - mu) * lax.rsqrt(var + LN_EPS) * g.astype(jnp.float32) + b.astype(jnp.float32)
    return y.astype(x.dtype)

def swiglu(x, w13, w2):
    a, b = jnp.split(x @ w13, 2, axis=-1)
    return (jax.nn.silu(a) * b) @ w2

def hgrn2_chunkwise(q, k, i, log_f):
    B, T, H, _ = q.shape
    n_chunks = T // HG_CHUNK

    def to_chunks(a):
        return a.reshape(B, n_chunks, HG_CHUNK, H, a.shape[-1]).transpose(1, 0, 3, 2, 4)

    causal = jnp.tril(jnp.ones((HG_CHUNK, HG_CHUNK), dtype=bool))[:, :, None]

    def step(S, inp):
        q_c, k_c, i_c, lf_c = inp
        b = jnp.cumsum(lf_c, axis=-2)
        o_inter = jnp.einsum('bhtk,bhkv->bhtv', q_c * jnp.exp(b), S)
        diff = b[:, :, :, None, :] - b[:, :, None, :, :]
        decay = jnp.where(causal, jnp.exp(jnp.where(causal, diff, 0.0)), 0.0)
        scores = jnp.einsum('bhtk,bhtsk,bhsk->bhts', q_c, decay, k_c)
        o_intra = jnp.einsum('bhts,bhsv->bhtv', scores, i_c)
        b_last = b[:, :, -1:, :]
        S_new = jnp.exp(b_last[:, :, 0, :])[..., None] * S + jnp.einsum(
            'bhsk,bhsv->bhkv', k_c * jnp.exp(b_last - b), i_c)
        return S_new, o_inter + o_intra

    S0 = jnp.zeros((B, H, q.shape[-1], i.shape[-1]), jnp.float32)
    _, o = lax.scan(step, S0, (to_chunks(q), to_chunks(k), to_chunks(i), to_chunks(log_f)))
    return o.transpose(1, 0, 3, 2, 4).reshape(B, T, H, i.shape[-1])

def mixer(x, w_in, lb, hg_norm_g, sg_ln_g, sg_ln_b, sg_ws, sg_bs, w_branch_a, w_branch_b, w_out):
    B, T, _ = x.shape
    zq, zf, zi, zg, zu, zv, za, zb = jnp.split(x @ w_in, IN_SPLITS, axis=-1)

    f32 = jnp.float32
    lbf = lb.astype(f32)
    zff = zf.astype(f32)
    f = lbf + (1.0 - lbf) * jax.nn.sigmoid(zff)
    log_f = jnp.log(f)
    k = (1.0 - lbf) * jax.nn.sigmoid(-zff)
    hs = lambda a, d: a.reshape(B, T, HG_HEADS, d)
    o = hgrn2_chunkwise(hs(zq.astype(f32), HG_DK), hs(k, HG_DK),
                        hs(zi.astype(f32), HG_DV), hs(log_f, HG_DK))
    o = o * lax.rsqrt(jnp.mean(jnp.square(o), axis=-1, keepdims=True) + RMS_EPS)
    o = o * hg_norm_g.astype(f32).reshape(HG_HEADS, HG_DV)
    o = o.reshape(B, T, HG_V).astype(x.dtype) * jax.nn.silu(zg)
    y_a = o @ w_branch_a

    u = jax.nn.gelu(zu)
    v = layer_norm(jax.nn.gelu(zv), sg_ln_g, sg_ln_b)
    n_chunks = T // SG_CHUNK
    v = v.reshape(B, n_chunks, SG_CHUNK, SG_GROUPS, SG_GROUP_DIM)
    ws = sg_ws * jnp.tril(jnp.ones((SG_CHUNK, SG_CHUNK), sg_ws.dtype))
    mixed = jnp.einsum('gts,bnsgc->bntgc', ws, v) + sg_bs.T[None, None, :, :, None]
    y_b = (u * mixed.reshape(B, T, SG_WIDTH)) @ w_branch_b

    y = jax.nn.sigmoid(za) * y_a + jax.nn.sigmoid(zb) * y_b
    return y @ w_out

def first_inputs(seed: int = 0) -> dict:
    key = jax.random.key(seed)
    ks = jax.random.split(key, 20)
    n = jax.random.normal
    f32 = jnp.float32
    return {
        "x": n(ks[0], (BATCH, SEQ, D_MODEL), f32),
        "ffn1_w13": n(ks[1], (DEPTH, D_MODEL, 2 * D_FF), f32) * D_MODEL ** -0.5,
        "ffn1_w2": n(ks[2], (DEPTH, D_FF, D_MODEL), f32) * (D_FF ** -0.5 * BETA),
        "ffn2_w13": n(ks[3], (DEPTH, D_MODEL, 2 * D_FF), f32) * D_MODEL ** -0.5,
        "ffn2_w2": n(ks[4], (DEPTH, D_FF, D_MODEL), f32) * (D_FF ** -0.5 * BETA),
        "ln_g": 1.0 + 0.02 * n(ks[5], (DEPTH, 3, D_MODEL), f32),
        "ln_b": 0.02 * n(ks[6], (DEPTH, 3, D_MODEL), f32),
        "w_in": n(ks[7], (DEPTH, D_MODEL, D_IN), f32) * D_MODEL ** -0.5,
        "hg_lb": 0.5 * n(ks[8], (DEPTH, HG_K), f32),
        "hg_norm_g": 1.0 + 0.02 * n(ks[9], (DEPTH, HG_V), f32),
        "sg_ln_g": 1.0 + 0.02 * n(ks[10], (DEPTH, SG_WIDTH), f32),
        "sg_ln_b": 0.02 * n(ks[11], (DEPTH, SG_WIDTH), f32),
        "sg_ws": n(ks[12], (DEPTH, SG_GROUPS, SG_CHUNK, SG_CHUNK), f32) * SG_CHUNK ** -0.5,
        "sg_bs": 1.0 + 0.1 * n(ks[13], (DEPTH, SG_GROUPS, SG_CHUNK), f32),
        "w_branch_a": n(ks[14], (DEPTH, HG_V, D_MODEL), f32) * (HG_V ** -0.5 * BETA),
        "w_branch_b": n(ks[15], (DEPTH, SG_WIDTH, D_MODEL), f32) * (SG_WIDTH ** -0.5 * BETA),
        "w_out": n(ks[16], (DEPTH, D_MODEL, D_MODEL), f32) * (D_MODEL ** -0.5 * BETA),
    }

def first_block(x, ffn1_w13, ffn1_w2, ffn2_w13, ffn2_w2, ln_g, ln_b, w_in, hg_lb, hg_norm_g,
              sg_ln_g, sg_ln_b, sg_ws, sg_bs, w_branch_a, w_branch_b, w_out):
    lb_soft = jax.nn.softmax(hg_lb.astype(jnp.float32), axis=0)
    lower_bounds = jnp.cumsum(lb_soft, axis=0) - lb_soft[0]
    for l in range(DEPTH):
        x = layer_norm(ALPHA * x + 0.5 * swiglu(x, ffn1_w13[l], ffn1_w2[l]), ln_g[l, 0], ln_b[l, 0])
        m = mixer(x, w_in[l], lower_bounds[l], hg_norm_g[l], sg_ln_g[l], sg_ln_b[l], sg_ws[l],
                  sg_bs[l], w_branch_a[l], w_branch_b[l], w_out[l])
        x = layer_norm(ALPHA * x + m, ln_g[l, 1], ln_b[l, 1])
        x = layer_norm(ALPHA * x + 0.5 * swiglu(x, ffn2_w13[l], ffn2_w2[l]), ln_g[l, 2], ln_b[l, 2])
    return x


D_MIX = D_MODEL
ATT_HEAD_DIM = 64
ATT_WIDTH = D_MIX // 2
ATT_HEADS = ATT_WIDTH // ATT_HEAD_DIM
DILATED_GROUPS = ((128, 1), (512, 4), (2048, 16))
ROPE_THETA = 500000.0
ROPE_DIM = ATT_HEAD_DIM // 4
MLSTM_WIDTH = D_MIX - ATT_WIDTH
MLSTM_HEADS = 4
MLSTM_HEAD_DIM = MLSTM_WIDTH // MLSTM_HEADS
MLSTM_CHUNK = 64
CONV_WIDTH = 5
N_GATES = 4
IN_WIDTH = 3 * ATT_WIDTH + 4 * MLSTM_WIDTH + N_GATES * MLSTM_HEADS
D_FF_2 = ((8 * D_MODEL // 3 + 127) // 128) * 128
N_NORMS = 6
NORM_EPS = 1e-6
NEG_BIG = -1e30


def rms_norm(x, gain):
    xf = x.astype(jnp.float32)
    y = xf * lax.rsqrt(jnp.mean(xf * xf, axis=-1, keepdims=True) + NORM_EPS)
    return (y * gain).astype(x.dtype)

def swiglu_2(h, w_in, w_out):
    gu = h @ w_in
    g, u = jnp.split(gu, 2, axis=-1)
    return (jax.nn.silu(g) * u) @ w_out

def split_heads(t, n_heads):
    b, s, w = t.shape
    return t.reshape(b, s, n_heads, w // n_heads).transpose(0, 2, 1, 3)

def merge_heads(t):
    b, h, s, dh = t.shape
    return t.transpose(0, 2, 1, 3).reshape(b, s, h * dh)

def partial_rotary(t, positions):
    half = ROPE_DIM // 2
    inv_freq = ROPE_THETA ** (-jnp.arange(half, dtype=jnp.float32) / half)
    ang = positions.astype(jnp.float32)[:, None] * inv_freq[None, :]
    cos, sin = jnp.cos(ang), jnp.sin(ang)
    t1 = t[..., :half].astype(jnp.float32)
    t2 = t[..., half:ROPE_DIM].astype(jnp.float32)
    rot = jnp.concatenate([t1 * cos - t2 * sin, t2 * cos + t1 * sin], axis=-1).astype(t.dtype)
    return jnp.concatenate([rot, t[..., ROPE_DIM:]], axis=-1)

def dilated_window_attention(q, k, v, window, dilation):
    b, h, s, dh = q.shape
    n_side = (window // 2) // dilation
    blk = n_side
    unit = dilation * blk
    s_pad = -(-s // unit) * unit
    n_blk = s_pad // unit
    sub_len = s_pad // dilation

    def to_blocks(t):
        t = jnp.pad(t, ((0, 0), (0, 0), (0, s_pad - s), (0, 0)))
        t = t.reshape(b, h, sub_len, dilation, dh).transpose(0, 1, 3, 2, 4)
        return t.reshape(b, h, dilation, n_blk, blk, dh)

    def neighbours(t):
        tp = jnp.pad(t, ((0, 0), (0, 0), (0, 0), (1, 1), (0, 0), (0, 0)))
        return jnp.concatenate([tp[:, :, :, :-2], tp[:, :, :, 1:-1], tp[:, :, :, 2:]], axis=4)

    qb = to_blocks(q)
    kn = neighbours(to_blocks(k))
    vn = neighbours(to_blocks(v))

    r = jnp.arange(dilation)[:, None, None, None]
    bi = jnp.arange(n_blk)[None, :, None, None]
    qi = jnp.arange(blk)[None, None, :, None]
    kj = jnp.arange(3 * blk)[None, None, None, :]
    m_q = bi * blk + qi
    m_k = bi * blk - blk + kj
    valid = (m_k >= 0) & (m_k * dilation + r < s) & (jnp.abs(m_q - m_k) <= n_side)

    scores = jnp.einsum('bhrnid,bhrnjd->bhrnij', qb, kn).astype(jnp.float32)
    scores = jnp.where(valid, scores, NEG_BIG)
    lse = jax.nn.logsumexp(scores, axis=-1)
    p = jnp.exp(scores - lse[..., None])
    out = jnp.einsum('bhrnij,bhrnjd->bhrnid', p, vn.astype(jnp.float32))

    def from_blocks(t):
        rest = t.shape[5:]
        t = t.reshape((b, h, dilation, sub_len) + rest)
        t = jnp.moveaxis(t, 2, 3).reshape((b, h, s_pad) + rest)
        return t[:, :, :s]

    return from_blocks(out), from_blocks(lse)

def dilated_attention_mixture(q, k, v):
    outs, lses = [], []
    for window, dilation in DILATED_GROUPS:
        o, l = dilated_window_attention(q, k, v, window, dilation)
        outs.append(o)
        lses.append(l)
    weights = jax.nn.softmax(jnp.stack(lses, axis=0), axis=0)
    return jnp.sum(weights[..., None] * jnp.stack(outs, axis=0), axis=0)

def mlstm_direction(q, k, v, i_pre, f_pre):
    b, h, s, dh = q.shape
    n_chunks = s // MLSTM_CHUNK
    log_f = jax.nn.log_sigmoid(f_pre)
    tril = jnp.tril(jnp.ones((MLSTM_CHUNK, MLSTM_CHUNK), dtype=bool))

    def chunks(t):
        return jnp.moveaxis(t.reshape((b, h, n_chunks, MLSTM_CHUNK) + t.shape[3:]), 2, 0)

    def step(carry, inp):
        c_mat, n_vec, m_prev = carry
        qc, kc, vc, ic, lfc = inp
        cum = jnp.cumsum(lfc, axis=-1)
        decay = cum[..., :, None] - cum[..., None, :] + ic[..., None, :]
        decay = jnp.where(tril, decay, -jnp.inf)
        inter = cum + m_prev[..., None]
        m_t = jnp.maximum(inter, jnp.max(decay, axis=-1))
        w_intra = jnp.exp(decay - m_t[..., None])
        w_inter = jnp.exp(inter - m_t)
        qk = jnp.einsum('bhtd,bhsd->bhts', qc, kc) * w_intra
        num = (jnp.einsum('bhts,bhse->bhte', qk, vc)
               + w_inter[..., None] * jnp.einsum('bhed,bhtd->bhte', c_mat, qc))
        den = jnp.sum(qk, axis=-1) + w_inter * jnp.einsum('bhd,bhtd->bht', n_vec, qc)
        h_out = num / jnp.maximum(jnp.abs(den), jnp.exp(-m_t))[..., None]
        total = cum[..., -1]
        w_src = total[..., None] - cum + ic
        m_new = jnp.maximum(total + m_prev, jnp.max(w_src, axis=-1))
        carry_scale = jnp.exp(total + m_prev - m_new)
        w_src = jnp.exp(w_src - m_new[..., None])
        c_new = carry_scale[..., None, None] * c_mat + jnp.einsum('bhs,bhse,bhsd->bhed', w_src, vc, kc)
        n_new = carry_scale[..., None] * n_vec + jnp.einsum('bhs,bhsd->bhd', w_src, kc)
        return (c_new, n_new, m_new), h_out

    init = (jnp.zeros((b, h, dh, dh), jnp.float32),
            jnp.zeros((b, h, dh), jnp.float32),
            jnp.full((b, h), NEG_BIG, jnp.float32))
    _, hs = lax.scan(step, init, (chunks(q), chunks(k), chunks(v), chunks(i_pre), chunks(log_f)))
    return jnp.moveaxis(hs, 0, 2).reshape(b, h, s, dh)

def token_mixer(h, w_in, conv_w, conv_b, gate_bias, mlstm_norm_gain, w_out):
    b, s, _ = h.shape
    proj = h @ w_in
    sizes = [ATT_WIDTH] * 3 + [MLSTM_WIDTH] * 4 + [N_GATES * MLSTM_HEADS]
    cuts = np.cumsum(sizes)[:-1].tolist()
    aq, ak, av, mq, mk, mv, mo, mg = jnp.split(proj, cuts, axis=-1)

    positions = jnp.arange(s)
    aq = partial_rotary(split_heads(aq, ATT_HEADS), positions) * (ATT_HEAD_DIM ** -0.5)
    ak = partial_rotary(split_heads(ak, ATT_HEADS), positions)
    av = split_heads(av, ATT_HEADS)
    attn_out = merge_heads(dilated_attention_mixture(aq, ak, av))

    qk = jnp.concatenate([mq, mk], axis=-1)
    qk = lax.conv_general_dilated(qk, conv_w.reshape(CONV_WIDTH, 1, 2 * MLSTM_WIDTH).astype(qk.dtype),
                                  window_strides=(1,), padding='SAME',
                                  dimension_numbers=('NWC', 'WIO', 'NWC'),
                                  feature_group_count=2 * MLSTM_WIDTH)
    qk = jax.nn.silu(qk + conv_b)
    mq, mk = jnp.split(qk, 2, axis=-1)
    mq = split_heads(mq, MLSTM_HEADS).astype(jnp.float32)
    mk = split_heads(mk, MLSTM_HEADS).astype(jnp.float32) * (MLSTM_HEAD_DIM ** -0.5)
    mv = split_heads(mv, MLSTM_HEADS).astype(jnp.float32)
    gates = mg.astype(jnp.float32).reshape(b, s, N_GATES, MLSTM_HEADS) + gate_bias
    gates = gates.transpose(2, 0, 3, 1)
    h_fwd = mlstm_direction(mq, mk, mv, gates[0], gates[1])
    flip = lambda t: jnp.flip(t, axis=2)
    h_bwd = flip(mlstm_direction(flip(mq), flip(mk), flip(mv), flip(gates[2]), flip(gates[3])))
    cell = h_fwd + h_bwd
    cell = cell * lax.rsqrt(jnp.mean(cell * cell, axis=-1, keepdims=True) + NORM_EPS)
    mlstm_out = jax.nn.sigmoid(mo.astype(jnp.float32)) * (merge_heads(cell) * mlstm_norm_gain)

    merged = jnp.concatenate([attn_out, mlstm_out], axis=-1).astype(h.dtype)
    return merged @ w_out

def second_inputs(seed: int = 0) -> dict:
    key = jax.random.key(seed)
    ks = jax.random.split(key, 12)
    f32 = jnp.float32
    x = jax.random.normal(ks[0], (BATCH, SEQ, D_MODEL), f32)
    norm_gain = 1.0 + 0.05 * jax.random.normal(ks[1], (DEPTH, N_NORMS, D_MODEL), f32)
    ffn_w_in = jax.random.normal(ks[2], (DEPTH, 2, D_MODEL, 2 * D_FF_2), f32) * D_MODEL ** -0.5
    ffn_w_out = jax.random.normal(ks[3], (DEPTH, 2, D_FF_2, D_MODEL), f32) * D_FF_2 ** -0.5
    mix_w_in = jax.random.normal(ks[4], (DEPTH, D_MODEL, IN_WIDTH), f32) * D_MODEL ** -0.5
    conv_w = jax.random.normal(ks[5], (DEPTH, CONV_WIDTH, 2 * MLSTM_WIDTH), f32) * CONV_WIDTH ** -0.5
    conv_b = 0.01 * jax.random.normal(ks[6], (DEPTH, 2 * MLSTM_WIDTH), f32)
    i_bias = 0.1 * jax.random.normal(ks[7], (DEPTH, 2, MLSTM_HEADS), f32)
    f_bias = (jnp.linspace(3.0, 6.0, MLSTM_HEADS, dtype=f32)[None, None, :]
              + 0.1 * jax.random.normal(ks[8], (DEPTH, 2, MLSTM_HEADS), f32))
    gate_bias = jnp.stack([i_bias[:, 0], f_bias[:, 0], i_bias[:, 1], f_bias[:, 1]], axis=1)
    mlstm_norm_gain = 1.0 + 0.05 * jax.random.normal(ks[9], (DEPTH, MLSTM_WIDTH), f32)
    mix_w_out = jax.random.normal(ks[10], (DEPTH, D_MIX, D_MODEL), f32) * D_MIX ** -0.5
    return {"x": x, "norm_gain": norm_gain, "ffn_w_in": ffn_w_in, "ffn_w_out": ffn_w_out,
            "mix_w_in": mix_w_in, "conv_w": conv_w, "conv_b": conv_b, "gate_bias": gate_bias,
            "mlstm_norm_gain": mlstm_norm_gain, "mix_w_out": mix_w_out}

def second_block(x, norm_gain, ffn_w_in, ffn_w_out, mix_w_in, conv_w, conv_b, gate_bias,
              mlstm_norm_gain, mix_w_out):
    for layer in range(DEPTH):
        g = norm_gain[layer]
        h = swiglu_2(rms_norm(x, g[0]), ffn_w_in[layer, 0], ffn_w_out[layer, 0])
        x = x + 0.5 * rms_norm(h, g[1])
        h = token_mixer(rms_norm(x, g[2]), mix_w_in[layer], conv_w[layer], conv_b[layer],
                        gate_bias[layer], mlstm_norm_gain[layer], mix_w_out[layer])
        x = x + rms_norm(h, g[3])
        h = swiglu_2(rms_norm(x, g[4]), ffn_w_in[layer, 1], ffn_w_out[layer, 1])
        x = x + 0.5 * rms_norm(h, g[5])
    return x


def setup_inputs(seed=0):
    out = dict(first_inputs(seed))
    for name, value in second_inputs(seed + 1).items():
        if name != "x":
            out[name + "_2"] = value
    return out


def reference(
    x, ffn1_w13, ffn1_w2, ffn2_w13, ffn2_w2, ln_g, ln_b, w_in, hg_lb, hg_norm_g, sg_ln_g,
    sg_ln_b, sg_ws, sg_bs, w_branch_a, w_branch_b, w_out, norm_gain_2, ffn_w_in_2, ffn_w_out_2,
    mix_w_in_2, conv_w_2, conv_b_2, gate_bias_2, mlstm_norm_gain_2, mix_w_out_2,
):
    x = first_block(
        x, ffn1_w13, ffn1_w2, ffn2_w13, ffn2_w2, ln_g, ln_b, w_in, hg_lb, hg_norm_g, sg_ln_g,
        sg_ln_b, sg_ws, sg_bs, w_branch_a, w_branch_b, w_out,
    )
    return second_block(
        x, norm_gain_2, ffn_w_in_2, ffn_w_out_2, mix_w_in_2, conv_w_2, conv_b_2, gate_bias_2,
        mlstm_norm_gain_2, mix_w_out_2,
    )


_drawn_inputs = setup_inputs


def setup_inputs(seed=0):
    import zlib

    import numpy as np

    out = dict(_drawn_inputs(seed))
    spreads = {}
    factors = {'hg_norm_g': 22.792,
     'sg_ln_g': 31.261,
     'sg_ln_b': 30.067,
     'sg_bs': 3.69,
     'conv_b_2': 7.493}
    for name, (base, spread) in spreads.items():
        noise = np.random.default_rng([zlib.crc32(name.encode()), seed]).standard_normal(out[name].shape)
        drawn = base * np.exp(spread * noise) if base else spread * noise
        out[name] = __import__('jax').numpy.asarray(drawn.astype(out[name].dtype))
    for name, factor in factors.items():
        out[name] = (out[name] * factor).astype(out[name].dtype)
    return out
```

```python
from contextlib import ExitStack

import concourse.bass as bass
from concourse import mybir

ALU = mybir.AluOpType
ACT = mybir.ActivationFunctionType
F32 = mybir.dt.float32
F32R = mybir.dt.float32r
I32 = mybir.dt.int32

P = 128
T = 256
NT = T // P
D = 1024
KD = D // P
DEPTH = 2
D_FF = 2816
FB = 256
STEPS = D_FF // FB
RING = 6
UNIT = 1024
FFN_UNITS = 6 * STEPS
MIX1_UNITS = 60
MIX2_UNITS = 36
LAYER1_TURNS = (2 * FFN_UNITS + MIX1_UNITS) // RING
LAYER2_TURNS = (2 * FFN_UNITS + MIX2_UNITS) // RING
FFN_TURNS = FFN_UNITS // RING

ALPHA = (2 * DEPTH) ** 0.25
LN_EPS = 1e-5
RMS_EPS = 1e-6
NORM_EPS = 1e-6
H = 4
AH = 8
DH = 64
ROT = 8
NG = 16
CONV = 5
LEVELS = [0, 1, 2, 4, 8, 16, 32, 64]

PER = dict(
    silu=1, gated=1, h_hi=1, h_lo=1,
    x_turned=2, xt_f32a=4, xt_f32v=4, xt_hi_a=1, xt_hi_v=1, xt_lo=2,
    ln_resid=2, ln_stats=4, ln_aggr=2, ln_var=2, ln_rstd=2, ln_xhat=2, x_scaled=2, x_ready=2,
    now1=5, rows=32, mixrows1=48,
    hg_sig=2, hg_fk=8, hg_q=1, hg_qf=1, hg_scores=9, hg_t=7, hg_qp=7, hg_ks=7, hg_sel=10,
    zi_out=1, zg_out=1, hg_gain=1, za_out=1, hg_o=1, o_ss=8, o_var=1, o_rstd=1, o_norm=1, o_gated=1,
    o_turned=1, o_hi=1, o_lo=1,
    zuv_out=2, v_stats=2, v_aggr=2, v_var=1, v_rstd=1, v_hat=2, v_scaled=1, v_ready=1,
    ws_in=16, ws_turned=1, ws_out=1, ws_low=4, mixed=1, ub=4, ub_turned=1, ub_hi=1, ub_lo=1,
    zb_out=1, ya=1, yb=2, y_sum=2, y_hi=2, y_lo=2,
    pre_ss=2, pre_var=1, pre_rstd=1, pre_xhat=2,
    post_ss=2, post_var=1, post_rstd=1, post_scaled=2,
    now2=2, margins=3, mixrows2=32, wg_in=16, wg_hi=1, wg_lo=1,
    gates=1, g_biased=2, g_min=2, g_exp=1, g_ln=1, g_logf=1, g_turned=1, g_rows=1,
    g_cum=2, g_a=2, g_max=2, g_neg=2, g_nm=2, g_cols_turned=1, g_cols=1, g_em=1,
    mqk_out=1, conv=40, conv_silu=1, k_scaled=1, mv_out=1, mo_out=1, mo_gain=1,
    m_scores=4, m_arg=16, m_exp=8, m_p=16, m_num=8, m_den=8, m_abs=8, m_rden=4, m_fwd=8, m_cell=8,
    m_ss=8, m_var=1, m_rstd=1, m_norm=1, m_out=1,
    aqk_out=1, av_out=1, rot=12, a_turned=1, a_t_out=1,
    a_scores=8, a_masked=16, a_exp=16, a_p_turned=8, a_p_out=8, a_o=8, a_rden=1, a_out=1,
    merged_turned=1,
    m_hi=2, m_lo=2,
)


def at(name, turn, which=None):
    return turn * PER[name] + (PER[name] if which is None else which)


def build(nc, A, out):
    ctx = ExitStack()
    with ctx:
        def sb(name, shape, dt=F32):
            return ctx.enter_context(nc.sbuf_tensor(name, shape, dt))

        S = {n: ctx.enter_context(nc.semaphore(n)) for n in PER}
        for n in ("hi_ready", "lo_ready", "weights_used", "x_in", "const_in", "ones_set", "tables_in",
                  "tables_turned", "tables_out", "lb_step", "lb_exp", "x_out", "gate_dve", "gate_pe", "gate_pool", "gate_sp"):
            S[n] = ctx.enter_context(nc.semaphore(n))
        staged = [ctx.enter_context(nc.semaphore(f"staged{i}")) for i in range(RING)]

        stage = sb("stage", [P, RING, UNIT])
        w_hi = sb("w_hi", [P, RING, UNIT], F32R)
        w_lo = sb("w_lo", [P, RING, UNIT], F32R)
        x = sb("x", [P, NT, D])
        xh = sb("xh", [P, NT, D])
        r = sb("r", [P, NT, D])
        xt32 = sb("xt32", [P, KD, T])
        xt_hi = sb("xt_hi", [P, KD, T], F32R)
        xt_lo = sb("xt_lo", [P, KD, T], F32R)
        hidden = sb("hidden", [P, 2, NT, FB])
        sil, h32 = hidden[:, 0], hidden[:, 1]
        h_hi = sb("h_hi", [P, NT, FB], F32R)
        h_lo = sb("h_lo", [P, NT, FB], F32R)
        rows = sb("rows", [P, 2, D])
        mt_hi = sb("mt_hi", [P, KD, T], F32R)
        mt_lo = sb("mt_lo", [P, KD, T], F32R)
        const = sb("const", [P, A["shape_constants"].shape[1]])
        sel = sb("sel", [2 * H, 2 * H, P])
        ones8 = sb("ones8", [2 * H, T])
        neg_half = sb("neg_half", [P, 2 * H])
        small = sb("small", [P, 756])
        small_at = [0]

        def few(n):
            small_at[0] += n
            return small[:, small_at[0] - n:small_at[0]]

        scratch = sb("scratch", [P, 10240])
        scratch_at = [0]

        def part(n):
            scratch_at[0] += n
            assert scratch_at[0] <= 10240, scratch_at[0]
            return scratch[:, scratch_at[0] - n:scratch_at[0]]

        bank = ctx.enter_context(nc.psum_tensor("bank", [P, 8, 512], F32))
        acc = bank[:, 0:4, :].rearrange("p (t b) n -> p t (b n)", t=NT)
        turned = bank[:, 4:8, :].rearrange("p b (k t) -> p (b k) t", k=2)
        low8 = bank[:, 0:4, :].rearrange("p b (k t) -> p (b k) t", k=2)
        gu = bank[:, 4:6, :].rearrange("p j (g t) -> p j g t", g=2)

        ident = const[:, 0:128]
        hg_mask = const[:, 128:128 + 6 * 128].rearrange("p (l t) -> p l t", l=6)
        at_mask = const[:, 896:896 + 512].rearrange("p (i j) -> p i j", i=NT)
        fwd_mask = const[:, 1408:1664]
        bwd_mask = const[:, 1664:1920]
        cos = const[:, 1920:1936].rearrange("p (i r) -> p i r", i=NT)
        sin = const[:, 1936:1952].rearrange("p (i r) -> p i r", i=NT)

        t_rows = r[:, :, :].rearrange("p a b -> p (a b)")[:, 0:512].rearrange("p (a b) -> p a b", a=4)
        ln_tab = few(2 * 7 * KD).rearrange("p (g e k) -> p g e k", g=2, e=7)
        gain_tab = few(2 * 6 * KD).rearrange("p (l j k) -> p l j k", l=2, j=6)
        conv_tab = few(2 * 6 * KD).rearrange("p (l j k) -> p l j k", l=2, j=6)
        sgb_tab = few(2 * H).rearrange("p (l h) -> p l h", l=2)
        lbr_tab = few(2 * H).rearrange("p (l h) -> p l h", l=2)
        lb_tab = few(2 * H).rearrange("p (l h) -> p l h", l=2)
        om_tab = few(2 * H).rearrange("p (l h) -> p l h", l=2)
        lb_tmp = few(6 * H).rearrange("p (l h) -> p l h", l=6)
        ln_now = few(2 * 3 * KD).rearrange("p (g e k) -> p g e k", g=2, e=3)
        sgb_now = few(H)
        lb_now = few(H)
        om_now = few(H)
        gain_now = few(6 * KD).rearrange("p (j k) -> p j k", j=6)
        conv_now = few(6 * KD).rearrange("p (j k) -> p j k", j=6)
        stats = sb("stats", [P, NT, 2, 6])
        mv_ = sb("mv_", [P, NT, 2])
        var = sb("var", [P, 2 * H])
        rstd = sb("rstd", [P, 2 * H])
        ss = sb("ss", [P, 2 * H])

        sig_f = part(1024).rearrange("p (h t) -> p h t", h=H)
        ks = part(1024).rearrange("p (h t) -> p h t", h=H)
        q = part(1024).rearrange("p (h t) -> p h t", h=H)
        qp = part(1024).rearrange("p (h t) -> p h t", h=H)
        tot = part(1024)
        sc = part(1024).rearrange("p (b t) -> p b t", b=2 * H)
        hidden_flat = hidden[:, :, :, :].rearrange("p a b c -> p (a b c)")
        ws_nat = hidden_flat[:, 0:512].rearrange("p (g s) -> p g s", g=H)
        ws_t = hidden_flat[:, 512:1024].rearrange("p (g t) -> p g t", g=H)
        scx = rows[:, 1, 512:1024].rearrange("p (h t) -> p h t", h=H)
        zi = part(1024).rearrange("p (i v) -> p i v", i=NT)
        gz = part(1024).rearrange("p (i v) -> p i v", i=NT)
        tb = part(2048).rearrange("p (k t) -> p k t", k=KD)
        ta = xh[:, :, :].rearrange("p i d -> p (i d)").rearrange("p (k t) -> p k t", k=KD)
        u_ = r[:, 0, :].rearrange("p (i v) -> p i v", i=NT)
        v_ = r[:, 1, :].rearrange("p (i v) -> p i v", i=NT)
        og = qp.rearrange("p h t -> p (h t)").rearrange("p (i v) -> p i v", i=NT)
        sq_junk = q.rearrange("p h t -> p (h t)")
        y32 = xt32

        scratch_at[0] = 0
        xp = part(KD * (T + 4)).rearrange("p (k t) -> p k t", k=KD)
        va = part(2 * H * 129).rearrange("p (i h e) -> p i h e", i=NT, h=H)
        gm = part(1024).rearrange("p (i v) -> p i v", i=NT)
        m_e = hidden_flat[:, 0:768].rearrange("p (d n) -> p d n", d=2)
        m_w = part(768).rearrange("p (d n) -> p d n", d=2)
        m_pt = part(2 * 384).rearrange("p (d n) -> p d n", d=2)
        cell = part(1024).rearrange("p (i v) -> p i v", i=NT)
        mlout = part(1024).rearrange("p (i v) -> p i v", i=NT)
        av = part(1024).rearrange("p (i v) -> p i v", i=NT)
        a_s = part(2 * 512).rearrange("p (b i j) -> p b i j", b=2, i=NT)
        conv_y = xt32
        aqk = r
        aqk_t = xh[:, :, :].rearrange("p i d -> p (i d)").rearrange("p (k t) -> p k t", k=KD)
        xp_flat = xp.rearrange("p k t -> p (k t)")
        a_p = xp_flat[:, 0:1024].rearrange("p (b i j) -> p b i j", b=2, i=NT)
        a_pt = xp_flat[:, 1024:2048].rearrange("p (b i j) -> p b i j", b=2, i=NT)
        a_out = gm
        rot_t = m_e.rearrange("p d n -> p (d n)")
        rot_u = m_w.rearrange("p d n -> p (d n)")
        g_i = few(NT * 8).rearrange("p (i r) -> p i r", i=NT)
        g_f = few(NT * 8).rearrange("p (i r) -> p i r", i=NT)
        g_n = few(NT * 8).rearrange("p (i r) -> p i r", i=NT)
        g_lf = few(NT * 8).rearrange("p (i r) -> p i r", i=NT)
        g_cols = few(NT * 2 * 2 * 8).rearrange("p (m d i r) -> p m d i r", m=2, d=2, i=NT)
        g_em = few(2 * NT * 8).rearrange("p (d i r) -> p d i r", d=2, i=NT)
        a_mx = few(16).rearrange("p (h i) -> p h i", h=AH)
        a_sum = few(16).rearrange("p (h i) -> p h i", h=AH)
        a_rs = few(16).rearrange("p (h i) -> p h i", h=AH)
        m_den = few(16).rearrange("p (h d i) -> p h d i", h=H, d=2)
        m_rd = few(16).rearrange("p (h d i) -> p h d i", h=H, d=2)
        grow = xh[0:2 * H, :, :].rearrange("p i d -> p (i d)")[:, 0:8 * T].rearrange("p (a t) -> p a t", t=T)
        wg32 = part(KD * NG).rearrange("p (k g) -> p k g", k=KD)
        wg_hi, wg_lo = (m[:, 0, 0:KD * NG].rearrange("p (k g) -> p k g", k=KD) for m in (mt_hi, mt_lo))

        def f32(ap):
            return ap.bitcast(F32)

        def place(turn, c):
            return turn + c // RING, c % RING

        def load(sp, turn, c, src, k):
            t, s = place(turn, c)
            sp.wait_ge(S["lo_ready"], t * RING + (s + 1))
            sp.sem_inc(S["gate_sp"], 1)
            sp.dma_start(stage[:, s, :][:, 0:k * src.shape[-1]].rearrange("p (k c) -> p k c", k=k), src)\
              .then_inc(staged[s], 16)

        def split_hi(act, turn, cs, n=UNIT):
            for c in cs:
                t, s = place(turn, c)
                act.wait_ge(staged[s], t * 16 + 16)
                act.wait_ge(S["weights_used"], t * RING + (s + 1))
                act.activation(w_hi[:, s, 0:n], stage[:, s, 0:n], ACT.Copy).then_inc(S["hi_ready"], 1)

        def split_lo(dve, turn, cs, n=UNIT):
            for c in cs:
                t, s = place(turn, c)
                dve.wait_ge(S["hi_ready"], t * RING + (s + 1))
                dve.tensor_tensor(w_lo[:, s, 0:n], stage[:, s, 0:n], f32(w_hi[:, s, 0:n]), ALU.subtract)\
                   .then_inc(S["lo_ready"], 1)

        def used_after(turn, c):
            t, s = place(turn, c)
            return t * RING + (s + 1 + RING)

        def unit(pe, turn, c):
            t, s = place(turn, c)
            pe.wait_ge(S["lo_ready"], t * RING + (s + 1 + RING))
            return w_hi[:, s, :], w_lo[:, s, :]

        def by_feature(pe, o, hi, lo, m_hi, m_lo, first, last):
            pe.matmul(o, hi, m_hi, start=first, stop=False)
            pe.matmul(o, hi, m_lo, start=False, stop=False)
            return pe.matmul(o, lo, m_hi, start=False, stop=last)

        def by_token(pe, o, hi, lo, m_hi, m_lo, first, last):
            pe.matmul(o, m_hi, hi, start=first, stop=False)
            pe.matmul(o, m_hi, lo, start=False, stop=False)
            return pe.matmul(o, m_lo, hi, start=False, stop=last)

        def token_unit(pe, turn, c, m_hi, m_lo, o, first, last):
            hi, lo = unit(pe, turn, c)
            for i in range(NT):
                for b in range(2):
                    mm = by_token(pe, o[:, i, b * 512:(b + 1) * 512], hi[:, b * 512:(b + 1) * 512],
                                  lo[:, b * 512:(b + 1) * 512], m_hi[:, i * P:(i + 1) * P],
                                  m_lo[:, i * P:(i + 1) * P], first, last)
            mm.then_inc(S["weights_used"], 1)

        def feature_unit(pe, turn, c, nk, m_hi, m_lo, outs, k0, k1):
            hi, lo = unit(pe, turn, c)
            w = P * len(outs)
            hi = hi[:, 0:nk * w].rearrange("p (k c) -> p k c", k=nk)
            lo = lo[:, 0:nk * w].rearrange("p (k c) -> p k c", k=nk)
            for j, o in enumerate(outs):
                for k in range(nk):
                    mm = by_feature(pe, o, hi[:, k, j * P:(j + 1) * P], lo[:, k, j * P:(j + 1) * P],
                                    m_hi[:, k0 + k, :], m_lo[:, k0 + k, :], k0 + k == 0, k0 + k == k1 - 1)
            mm.then_inc(S["weights_used"], 1)

        def dve_hold(dve, sem, value):
            dve.wait_ge(sem, value)
            dve.sem_inc(S["gate_dve"], 1)

        def pe_hold(pe, sem, value):
            pe.wait_ge(sem, value)
            pe.sem_inc(S["gate_pe"], 1)

        def pool_hold(pool, sem, value):
            pool.wait_ge(sem, value)
            pool.sem_inc(S["gate_pool"], 1)

        def norm_done(n, which=None):
            return at("x_ready", n + 1, which)

        def xhat_done(n, which=None):
            return at("ln_xhat", n + 1, which)

        def sp_ffn(sp, turn, w13, w2):
            def load_gu(turn, i, cs):
                for n, c in enumerate(cs):
                    g, kh = n // 2, n % 2
                    src = w13[kh * 512:(kh + 1) * 512, bass.ds(g * D_FF + i * FB, FB)] if not isinstance(i, int) \
                        else w13[kh * 512:(kh + 1) * 512, g * D_FF + i * FB:g * D_FF + (i + 1) * FB]
                    load(sp, turn, c, src.rearrange("(k p) c -> p k c", p=P), 4)

            def load_w2(turn, i, cs):
                for n, c in enumerate(cs):
                    src = w2[bass.ds(i * FB + n * P, P), :] if not isinstance(i, int) \
                        else w2[i * FB + n * P:i * FB + (n + 1) * P, :]
                    load(sp, turn, c, src.rearrange("p (k c) -> p k c", k=1), 1)

            load_gu(turn, 0, [0, 1, 2, 3])
            load_gu(turn, 1, [4, 5, 6, 7])
            with sp.Fori(1, STEPS - 1) as i:
                load_w2(turn + i, i - 1, [2, 3])
                load_gu(turn + i, i + 1, [4, 5, 6, 7])
            load_w2(turn, STEPS - 2, [FFN_UNITS - 4, FFN_UNITS - 3])
            load_w2(turn, STEPS - 1, [FFN_UNITS - 2, FFN_UNITS - 1])

        def act_silu(act, turn, c, n):
            act.wait_ge(S["weights_used"], used_after(turn, c))
            act.activation(sil[:, :, :], gu[:, :, 0, :], ACT.Silu).then_inc(S["silu"], 1)

        def act_h(act, n):
            act.wait_ge(S["gated"], n)
            act.activation(h_hi[:, :, :], h32[:, :, :], ACT.Copy).then_inc(S["h_hi"], 1)

        def act_ffn(act, turn, step0):
            split_hi(act, turn, [4, 5, 6, 7])
            act_silu(act, turn, 3, step0)
            with act.Fori(1, STEPS - 1) as i:
                split_hi(act, turn + i, [2, 3])
                act_h(act, step0 + i)
                split_hi(act, turn + i, [4, 5, 6, 7])
                act_silu(act, turn + i, 1, step0 + i)
            split_hi(act, turn, [FFN_UNITS - 4, FFN_UNITS - 3])
            act_h(act, step0 + (STEPS - 1))
            split_hi(act, turn, [FFN_UNITS - 2, FFN_UNITS - 1])
            act_silu(act, turn, FFN_UNITS - 5, step0 + (STEPS - 1))
            act.wait_ge(S["weights_used"], used_after(turn, FFN_UNITS - 3))
            act_h(act, step0 + STEPS)

        def dve_gate(dve, n):
            dve.wait_ge(S["silu"], n)
            dve.tensor_tensor(h32[:, :, :], sil[:, :, :], gu[:, :, 1, :], ALU.mult).then_inc(S["gated"], 1)

        def dve_h(dve, n):
            dve.wait_ge(S["h_hi"], n)
            dve.tensor_tensor(h_lo[:, :, :], h32[:, :, :], f32(h_hi[:, :, :]), ALU.subtract)\
               .then_inc(S["h_lo"], 1)

        def dve_ffn(dve, turn, step0):
            split_lo(dve, turn, [4, 5, 6, 7])
            dve_gate(dve, step0 + 1)
            with dve.Fori(1, STEPS - 1) as i:
                split_lo(dve, turn + i, [2, 3])
                dve_h(dve, step0 + i)
                split_lo(dve, turn + i, [4, 5, 6, 7])
                dve.wait_ge(S["h_lo"], step0 + i)
                dve_gate(dve, step0 + i + 1)
            split_lo(dve, turn, [FFN_UNITS - 4, FFN_UNITS - 3])
            dve_h(dve, step0 + (STEPS - 1))
            split_lo(dve, turn, [FFN_UNITS - 2, FFN_UNITS - 1])
            dve.wait_ge(S["h_lo"], step0 + (STEPS - 1))
            dve_gate(dve, step0 + STEPS)
            dve_h(dve, step0 + STEPS)

        def pe_ffn(pe, turn, step0, xt):
            def gate_up(turn, cs, first=False):
                outs = [[gu[:, j, g, :] for j in range(2)] for g in range(2)]
                for n, c in enumerate(cs):
                    g, kh = n // 2, n % 2
                    if first and g == 0:
                        pe.wait_ge(S["xt_lo"], at("xt_lo", xt, kh + 1))
                    feature_unit(pe, turn, c, 4, xt_hi, xt_lo, outs[g], 4 * kh, KD)

            def down(turn, cs, n, first, last):
                pe.wait_ge(S["h_lo"], n)
                for j, c in enumerate(cs):
                    token_unit(pe, turn, c, h_hi[:, j, :], h_lo[:, j, :], acc, first and j == 0, last and j == 1)

            gate_up(turn, [0, 1, 2, 3], True)
            pe.wait_ge(S["gated"], step0 + 1)
            gate_up(turn, [4, 5, 6, 7])
            down(turn, [8, 9], step0 + 1, True, False)
            with pe.Fori(2, STEPS) as i:
                pe.wait_ge(S["gated"], step0 + i)
                gate_up(turn + i, [-2, -1, 0, 1])
                down(turn + i, [2, 3], step0 + i, False, False)
            down(turn, [FFN_UNITS - 2, FFN_UNITS - 1], step0 + STEPS, False, True)

        def pe_turn(pe, ready, ready_at):
            for i in range(NT):
                pe.wait_ge(ready, ready_at(i))
                for k in range(KD):
                    mm = pe.transpose(turned[:, k, i * P:(i + 1) * P], xh[:, i, k * P:(k + 1) * P], ident)
                    if i == NT - 1 and k % 4 == 3:
                        mm.then_inc(S["x_turned"], 1)

        def dve_turn(dve, n, g, b):
            dve.wait_ge(S["x_turned"], at("x_turned", n, 1))
            for k in range(4):
                dve.tensor_scalar(xt32[:, k, :], turned[:, k, :], g[:, k:k + 1],
                                  0.0 if b is None else b[:, k:k + 1], ALU.mult, ALU.add)\
                   .then_inc(S["xt_f32v"], 1)
            dve.wait_ge(S["xt_f32v"], at("xt_f32v", n))
            dve.tensor_copy(xt_hi[:, 0:4, :], xt32[:, 0:4, :]).then_inc(S["xt_hi_v"], 1)
            dve.wait_ge(S["xt_hi_v"], at("xt_hi_v", n))
            dve.tensor_tensor(xt_lo[:, 0:4, :], xt32[:, 0:4, :], f32(xt_hi[:, 0:4, :]), ALU.subtract)\
               .then_inc(S["xt_lo"], 1)
            dve.wait_ge(S["xt_hi_a"], at("xt_hi_a", n))
            dve.tensor_tensor(xt_lo[:, 4:8, :], xt32[:, 4:8, :], f32(xt_hi[:, 4:8, :]), ALU.subtract)\
               .then_inc(S["xt_lo"], 1)

        def act_turn(act, n, g, b):
            act.wait_ge(S["x_turned"], at("x_turned", n, 2))
            for k in range(4, 8):
                act.activation(xt32[:, k, :], turned[:, k, :], ACT.Identity, scale=g[:, k:k + 1],
                               bias=0.0 if b is None else b[:, k:k + 1]).then_inc(S["xt_f32a"], 1)
            act.wait_ge(S["xt_f32a"], at("xt_f32a", n))
            act.activation(xt_hi[:, 4:8, :], xt32[:, 4:8, :], ACT.Copy).then_inc(S["xt_hi_a"], 1)

        def dve_layer_norm(dve, n, out_at):
            for i in range(NT):
                if i == 0:
                    dve.wait_ge(S["weights_used"], out_at)
                dve.scalar_tensor_tensor(r[:, i, :], x[:, i, :], 2 * ALPHA, acc[:, i, :], ALU.mult, ALU.add)\
                   .then_inc(S["ln_resid"], 1)
                dve.wait_ge(S["ln_resid"], at("ln_resid", n, i + 1))
                for b in range(2):
                    dve.bn_stats(stats[:, i, b, :], r[:, i, b * 512:(b + 1) * 512]).then_inc(S["ln_stats"], 1)
                dve_hold(dve, S["ln_stats"], at("ln_stats", n, 2 * i + 2))
                dve.bn_aggr(mv_[:, i, :], stats[:, i, :, :]).then_inc(S["ln_aggr"], 1)
                dve.wait_ge(S["ln_aggr"], at("ln_aggr", n, i + 1))
                dve.tensor_scalar(var[:, i:i + 1], mv_[:, i, 1:2], 4 * LN_EPS, None, ALU.add).then_inc(S["ln_var"], 1)
            for i in range(NT):
                dve.wait_ge(S["ln_rstd"], at("ln_rstd", n, i + 1))
                dve.tensor_scalar(xh[:, i, :], r[:, i, :], mv_[:, i, 0:1], rstd[:, i:i + 1], ALU.subtract,
                                  ALU.mult).then_inc(S["ln_xhat"], 1)

        def pool_layer_norm(pool, n):
            for i in range(NT):
                pool.wait_ge(S["ln_var"], at("ln_var", n, i + 1))
                pool.tensor_tensor(rstd[:, i:i + 1], var[:, i:i + 1], neg_half[:, 0:1], ALU.pow)\
                    .then_inc(S["ln_rstd"], 1)

        def dve_residual(dve, n):
            dve.wait_ge(S["rows"], at("rows", n))
            dve.wait_ge(S["ln_xhat"], xhat_done(n))
            for i in range(NT):
                dve.tensor_tensor(x[:, i, :], xh[:, i, :], rows[:, 0, :], ALU.mult).then_inc(S["x_scaled"], 1)
            for i in range(NT):
                dve.wait_ge(S["x_scaled"], at("x_scaled", n, i + 1))
                dve.tensor_tensor(x[:, i, :], x[:, i, :], rows[:, 1, :], ALU.add).then_inc(S["x_ready"], 1)

        def w_cols(w, c0, n, k0=0, nk=KD):
            return w[k0 * P:(k0 + nk) * P, c0:c0 + n].rearrange("(k p) c -> p k c", p=P)

        def sp_mix1(sp, turn, w_in, wa, wb, wo):
            for j in range(4):
                load(sp, turn, j, w_cols(w_in, 512 + j * P, P), KD)
            for j in range(4):
                load(sp, turn, 4 + j, w_cols(w_in, j * P, P), KD)
            for k in range(KD):
                load(sp, turn, 8 + k, w_cols(w_in, 1024, 1024, k, 1), 1)
            for j in range(8):
                load(sp, turn, 16 + j, w_cols(w_in, 3072 + j * P, P), KD)
            for k in range(KD):
                load(sp, turn, 24 + k, w_cols(w_in, 2048, 1024, k, 1), 1)
            for j in range(8):
                load(sp, turn, 32 + j, w_cols(w_in, 4096 + j * P, P), KD)
            for j in range(8):
                load(sp, turn, 40 + j, w_cols(wa, j * P, P, 0, 4), 4)
            for j in range(4):
                load(sp, turn, 48 + j, w_cols(wb, j * 2 * P, 2 * P, 0, 4), 4)
            for k in range(KD):
                load(sp, turn, 52 + k, w_cols(wo, 0, 1024, k, 1), 1)

        def pe_mix1(pe, L, turn, xt):
            def project(c0, n, base):
                for j in range(n):
                    feature_unit(pe, turn, c0 + j, KD, xt_hi, xt_lo, [base[:, j, :]], 0, KD)

            pe.wait_ge(S["xt_lo"], at("xt_lo", xt))
            project(0, 4, turned)
            project(4, 4, turned[:, 4:8, :])
            for k in range(KD):
                token_unit(pe, turn, 8 + k, xt_hi[:, k, :], xt_lo[:, k, :], acc, k == 0, k == KD - 1)

            def scores(n, size):
                o = bank[:, 2 * (n % 2):2 * (n % 2) + 2, :].rearrange("p b (c t) -> p (b c) t", c=4)
                if n == 0:
                    pe.wait_ge(S["zi_out"], at("zi_out", L))
                    pe.wait_ge(S["zg_out"], at("zg_out", L))
                    pe.wait_ge(S["hg_qf"], at("hg_qf", L))
                if n >= 2:
                    pe.wait_ge(S["hg_sel"], at("hg_sel", L, SEL_AFTER[n - 2]))
                if n >= 2:
                    pe.wait_ge(S["hg_qp"], at("hg_qp", L, n - 1))
                    pe.wait_ge(S["hg_ks"], at("hg_ks", L, n - 1))
                qq = q if n == 0 else qp
                if size < P:
                    for h in range(H):
                        for a in range(NT):
                            mm = pe.matmul(o[:, 2 * h + a, :], ks[:, h, a * P:(a + 1) * P],
                                           qq[:, h, a * P:(a + 1) * P], start=True, stop=True)
                else:
                    for h in range(H):
                        mm = pe.matmul(o[:, h, :], ks[:, h, 0:P], qq[:, h, P:2 * P], start=True, stop=True)
                mm.then_inc(S["hg_scores"], 1)

            for j in range(8):
                if j == 0:
                    pe.wait_ge(S["hg_q"], at("hg_q", L))
                feature_unit(pe, turn, 16 + j, KD, xt_hi, xt_lo, [turned[:, j, :]], 0, KD)
                scores(j, LEVELS[j])
            scores(8, P)
            for k in range(KD):
                if k == 0:
                    pe.wait_ge(S["hg_sel"], at("hg_sel", L))
                token_unit(pe, turn, 24 + k, xt_hi[:, k, :], xt_lo[:, k, :], acc, k == 0, k == KD - 1)
                if k == 2:
                    pe.wait_ge(S["za_out"], at("za_out", L))
                    for h in range(H):
                        c = slice(h * P, (h + 1) * P)
                        pe.matmul(bank[:, 4, c], sc[:, 2 * h, :], zi[:, 0, c], start=True, stop=True)
                        pe.matmul(bank[:, 5, c], sc[:, 2 * h + 1, :], zi[:, 1, c], start=True, stop=False)
                        mm = pe.matmul(bank[:, 5, c], scx[:, h, :], zi[:, 0, c], start=False, stop=True)
                    mm.then_inc(S["hg_o"], 1)
                if k == 4:
                    pe.wait_ge(S["ws_in"], at("ws_in", L))
                    for g in range(H):
                        mm = pe.transpose(bank[:, 6, g * P:(g + 1) * P], ws_nat[:, g, :], ident)
                    mm.then_inc(S["ws_turned"], 1)
            for j in range(8):
                if j == 0:
                    pe.wait_ge(S["o_norm"], at("o_norm", L))
                    pe.wait_ge(S["ws_out"], at("ws_out", L))
                feature_unit(pe, turn, 32 + j, KD, xt_hi, xt_lo, [turned[:, j, :]], 0, KD)
                if j == 3:
                    pe.wait_ge(S["zuv_out"], at("zuv_out", L))
                    pe.wait_ge(S["o_gated"], at("o_gated", L))
                    for k in range(4):
                        for i in range(NT):
                            mm = pe.transpose(low8[:, 4 + k, i * P:(i + 1) * P], og[:, i, k * P:(k + 1) * P], ident)
                    mm.then_inc(S["o_turned"], 1)
                if j == 5:
                    pe.wait_ge(S["v_ready"], at("v_ready", L))
                    pe.wait_ge(S["ws_low"], at("ws_low", L))
                    for g in range(H):
                        mm = pe.matmul(low8[:, g, :].rearrange("p (i c) -> p i c", i=NT), ws_t[:, g, :],
                                       v_[:, :, g * P:(g + 1) * P], start=True, stop=True)
                    mm.then_inc(S["mixed"], 1)
            pe.wait_ge(S["ub"], at("ub", L))
            pe.wait_ge(S["o_lo"], at("o_lo", L))
            for k in range(4):
                for i in range(NT):
                    mm = pe.transpose(low8[:, 4 + k, i * P:(i + 1) * P], u_[:, i, k * P:(k + 1) * P], ident)
            mm.then_inc(S["ub_turned"], 1)
            pe.wait_ge(S["zb_out"], at("zb_out", L))
            for j in range(8):
                feature_unit(pe, turn, 40 + j, 4, mt_hi, mt_lo, [turned[:, j, :]], 0, 4)
            pe.wait_ge(S["ub_lo"], at("ub_lo", L))
            for j in range(4):
                feature_unit(pe, turn, 48 + j, 4, mt_hi[:, 4:8, :], mt_lo[:, 4:8, :],
                             [low8[:, 2 * j, :], low8[:, 2 * j + 1, :]], 0, 4)
            pe.wait_ge(S["yb"], at("yb", L))
            for k in range(KD):
                if k % 4 == 0:
                    pe.wait_ge(S["y_lo"], at("y_lo", L, k // 4 + 1))
                token_unit(pe, turn, 52 + k, xt_hi[:, k, :], xt_lo[:, k, :], acc, k == 0, k == KD - 1)

        SEL_AFTER = [1, 2, 3, 4, 5, 6, 8, 9, 10]

        def act_mix1(act, L, turn):
            split_hi(act, turn, range(4, 10))
            act.wait_ge(S["weights_used"], used_after(turn, 3))
            act.activation(sig_f, turned[:, 0:4, :], ACT.Sigmoid).then_inc(S["hg_sig"], 1)
            act.activation(ks, turned[:, 0:4, :], ACT.Sigmoid, scale=-1.0).then_inc(S["hg_sig"], 1)
            split_hi(act, turn, range(10, 14))
            act.wait_ge(S["weights_used"], used_after(turn, 7))
            act.activation(q, turned[:, 4:8, :], ACT.Copy).then_inc(S["hg_q"], 1)
            split_hi(act, turn, range(14, 22))
            act.wait_ge(S["weights_used"], used_after(turn, 15))
            act.activation(zi, acc[:, :, 0:512], ACT.Copy).then_inc(S["zi_out"], 1)
            act.activation(gz, acc[:, :, 512:1024], ACT.Silu).then_inc(S["zg_out"], 1)
            split_hi(act, turn, range(22, 30))
            act.wait_ge(S["weights_used"], used_after(turn, 23))
            act.wait_ge(S["x_ready"], norm_done(3 * L))
            act.activation(ta, turned, ACT.Tanh, scale=0.5).then_inc(S["za_out"], 1)
            split_hi(act, turn, range(30, 33))
            act.wait_ge(S["hg_o"], at("hg_o", L))
            for h in range(H):
                for i in range(NT):
                    n = 2 * h + i
                    act.activation(sq_junk[:, n * P:(n + 1) * P], bank[:, 4 + i, h * P:(h + 1) * P], ACT.Square,
                                   accum_out=ss[:, i * H + h:i * H + h + 1]).then_inc(S["o_ss"], 1)
            split_hi(act, turn, range(33, 35))
            act.wait_ge(S["ws_turned"], at("ws_turned", L))
            act.activation(ws_t, bank[:, 6, :].rearrange("p (g t) -> p g t", g=H), ACT.Copy).then_inc(S["ws_out"], 1)
            split_hi(act, turn, range(35, 38))
            act.wait_ge(S["weights_used"], used_after(turn, 31))
            act.activation(v_, acc[:, :, 512:1024], ACT.Gelu_apprx_tanh).then_inc(S["zuv_out"], 1)
            act.activation(u_, acc[:, :, 0:512], ACT.Gelu_apprx_tanh).then_inc(S["zuv_out"], 1)
            split_hi(act, turn, range(38, 40))
            split_hi(act, turn, range(40, 42), 512)
            act.wait_ge(S["o_turned"], at("o_turned", L))
            act.activation(mt_hi[:, 0:4, :], low8[:, 4:8, :], ACT.Copy).then_inc(S["o_hi"], 1)
            split_hi(act, turn, range(42, 46), 512)
            act.wait_ge(S["weights_used"], used_after(turn, 39))
            act.activation(tb, turned, ACT.Tanh, scale=0.5).then_inc(S["zb_out"], 1)
            act.wait_ge(S["ub_turned"], at("ub_turned", L))
            act.activation(mt_hi[:, 4:8, :], low8[:, 4:8, :], ACT.Copy).then_inc(S["ub_hi"], 1)
            split_hi(act, turn, range(46, 48), 512)
            split_hi(act, turn, range(48, 56))
            for a in range(2):
                act.wait_ge(S["y_sum"], at("y_sum", L, a + 1))
                act.activation(xt_hi[:, 4 * a:4 * a + 4, :], y32[:, 4 * a:4 * a + 4, :], ACT.Copy)\
                   .then_inc(S["y_hi"], 1)
            split_hi(act, turn, range(56, 60))

        def dve_mix1(dve, L, turn):
            split_lo(dve, turn, range(4, 10))
            dve.wait_ge(S["now1"], at("now1", L))
            dve.wait_ge(S["hg_sig"], at("hg_sig", L))
            for h in range(H):
                dve.tensor_scalar(sig_f[:, h, :], sig_f[:, h, :], om_now[:, h:h + 1], lb_now[:, h:h + 1],
                                  ALU.mult, ALU.add).then_inc(S["hg_fk"], 1)
            for h in range(H):
                dve.tensor_scalar(ks[:, h, :], ks[:, h, :], om_now[:, h:h + 1], None, ALU.mult)\
                   .then_inc(S["hg_fk"], 1)
            split_lo(dve, turn, range(10, 14))
            dve.wait_ge(S["hg_q"], at("hg_q", L))
            dve.wait_ge(S["hg_fk"], at("hg_fk", L))
            dve.tensor_tensor(qp, q, sig_f, ALU.mult).then_inc(S["hg_qf"], 1)
            split_lo(dve, turn, range(14, 22))
            dve.wait_ge(S["mixrows1"], at("mixrows1", L))
            dve.wait_ge(S["zg_out"], at("zg_out", L))
            dve.tensor_tensor(gz, gz, rows[:, 0, 0:512].unsqueeze(1).broadcast_to([P, NT, 512]), ALU.mult)\
               .then_inc(S["hg_gain"], 1)

            qpf, ksf = (a.rearrange("p h t -> p (h t)") for a in (qp, ks))
            block_total = [sig_f.rearrange("p h t -> p (h t)")]
            at_ = 0
            for n in range(1, 8):
                size = 1024 >> n
                block_total.append(tot[:, at_:at_ + size])
                at_ += size
            selected = 0
            for n in range(9):
                size = LEVELS[n] if n < 8 else P
                o = bank[:, 2 * (n % 2):2 * (n % 2) + 2, :].rearrange("p b (c t) -> p (b c) t", c=4)
                dve_hold(dve, S["hg_scores"], at("hg_scores", L, n + 1))
                if 1 <= n < 8:
                    if n > 1:
                        dve.wait_ge(S["hg_t"], at("hg_t", L, n - 1))
                    b, nb = size, 1024 // (2 * size)
                    t2 = block_total[n - 1].rearrange("p (n two) -> p n two", two=2)
                    qv = qpf.rearrange("p (n two b) -> p n two b", two=2, b=b)
                    kv = ksf.rearrange("p (n two b) -> p n two b", two=2, b=b)
                    dve.tensor_tensor(qv[:, :, 1, :], qv[:, :, 1, :],
                                      t2[:, :, 0:1].broadcast_to([P, nb, b]), ALU.mult).then_inc(S["hg_qp"], 1)
                    dve.tensor_tensor(kv[:, :, 0, :], kv[:, :, 0, :],
                                      t2[:, :, 1:2].broadcast_to([P, nb, b]), ALU.mult).then_inc(S["hg_ks"], 1)
                    dve.tensor_tensor(block_total[n], t2[:, :, 0], t2[:, :, 1], ALU.mult).then_inc(S["hg_t"], 1)
                if selected and n < 8:
                    dve_hold(dve, S["hg_sel"], at("hg_sel", L, selected))
                if n == 0:
                    dve.tensor_tensor(sc, o, hg_mask[:, 0:1, :].broadcast_to([P, 8, P]), ALU.mult)\
                       .then_inc(S["hg_sel"], 1)
                elif size <= 16:
                    dve.copy_predicated(sc, hg_mask[:, n:n + 1, :].bitcast(I32).broadcast_to([P, 8, P]), o)\
                       .then_inc(S["hg_sel"], 1)
                elif size == 32:
                    for s in (0, 64):
                        dve.tensor_copy(sc[s:s + 32, :, s + 32:s + 64], o[s:s + 32, :, s + 32:s + 64])\
                           .then_inc(S["hg_sel"], 1)
                elif size == 64:
                    dve.tensor_copy(sc[0:64, :, 64:128], o[0:64, :, 64:128]).then_inc(S["hg_sel"], 1)
                else:
                    dve.tensor_copy(scx, o[:, 0:4, :]).then_inc(S["hg_sel"], 1)
                selected = SEL_AFTER[n]
                if n < 8:
                    split_lo(dve, turn, [22 + n])
            split_lo(dve, turn, range(30, 33))
            dve.wait_ge(S["o_ss"], at("o_ss", L))
            dve.tensor_scalar(var[:, 0:8], ss[:, 0:8], 1.0 / P, RMS_EPS, ALU.mult, ALU.add).then_inc(S["o_var"], 1)
            split_lo(dve, turn, range(33, 34))
            dve.wait_ge(S["o_rstd"], at("o_rstd", L))
            ogv = og.rearrange("p i (h v) -> p i h v", h=H)
            for_o = bank[:, 4:6, :].rearrange("p i (h v) -> p (i h) v", h=H)
            dve.tensor_tensor(og.rearrange("p i (h v) -> p (i h) v", h=H), for_o,
                              rstd[:, 0:8].unsqueeze(2).broadcast_to([P, 8, P]), ALU.mult).then_inc(S["o_norm"], 1)
            dve.wait_ge(S["o_norm"], at("o_norm", L))
            dve.wait_ge(S["hg_gain"], at("hg_gain", L))
            dve.tensor_tensor(og, og, gz, ALU.mult).then_inc(S["o_gated"], 1)
            split_lo(dve, turn, range(34, 38))
            dve.wait_ge(S["zuv_out"], at("zuv_out", L, 1))
            for i in range(NT):
                dve.bn_stats(stats[:, i, 0, :], v_[:, i, :]).then_inc(S["v_stats"], 1)
            for i in range(NT):
                dve_hold(dve, S["v_stats"], at("v_stats", L, i + 1))
                dve.bn_aggr(mv_[:, i, :], stats[:, i, 0, :]).then_inc(S["v_aggr"], 1)
            dve.wait_ge(S["v_aggr"], at("v_aggr", L))
            dve.tensor_scalar(var[:, 0:2], mv_[:, :, 1], LN_EPS, None, ALU.add).then_inc(S["v_var"], 1)
            split_lo(dve, turn, range(38, 39))
            dve.wait_ge(S["v_rstd"], at("v_rstd", L))
            for i in range(NT):
                dve.tensor_scalar(v_[:, i, :], v_[:, i, :], mv_[:, i, 0:1], rstd[:, i:i + 1], ALU.subtract,
                                  ALU.mult).then_inc(S["v_hat"], 1)
            dve.wait_ge(S["v_hat"], at("v_hat", L))
            dve.tensor_tensor(v_, v_, rows[:, 0, 512:1024].unsqueeze(1).broadcast_to([P, NT, 512]), ALU.mult)\
               .then_inc(S["v_scaled"], 1)
            dve.wait_ge(S["v_scaled"], at("v_scaled", L))
            dve.tensor_tensor(v_, v_, rows[:, 1, 0:512].unsqueeze(1).broadcast_to([P, NT, 512]), ALU.add)\
               .then_inc(S["v_ready"], 1)
            split_lo(dve, turn, range(39, 40))
            split_lo(dve, turn, range(40, 42), 512)
            dve.wait_ge(S["o_hi"], at("o_hi", L))
            dve.tensor_tensor(mt_lo[:, 0:4, :], low8[:, 4:8, :], f32(mt_hi[:, 0:4, :]), ALU.subtract)\
               .then_inc(S["o_lo"], 1)
            split_lo(dve, turn, range(42, 44), 512)
            dve.wait_ge(S["mixed"], at("mixed", L))
            dve.wait_ge(S["zuv_out"], at("zuv_out", L))
            for g in range(H):
                c = slice(g * P, (g + 1) * P)
                dve.scalar_tensor_tensor(u_[:, :, c], low8[:, g, :].rearrange("p (i c) -> p i c", i=NT),
                                         sgb_now[:, g:g + 1], u_[:, :, c], ALU.add, ALU.mult).then_inc(S["ub"], 1)
            split_lo(dve, turn, range(44, 46), 512)
            dve.wait_ge(S["ub_hi"], at("ub_hi", L))
            dve.tensor_tensor(mt_lo[:, 4:8, :], low8[:, 4:8, :], f32(mt_hi[:, 4:8, :]), ALU.subtract)\
               .then_inc(S["ub_lo"], 1)
            split_lo(dve, turn, range(46, 48), 512)
            split_lo(dve, turn, range(48, 54))
            dve.wait_ge(S["weights_used"], used_after(turn, 47))
            dve.wait_ge(S["zb_out"], at("zb_out", L))
            dve.scalar_tensor_tensor(ta, ta, 1.0, turned, ALU.add, ALU.mult).then_inc(S["ya"], 1)
            split_lo(dve, turn, range(54, 56))
            dve.wait_ge(S["ya"], at("ya", L))
            for a in range(2):
                c = slice(4 * a, 4 * a + 4)
                dve.wait_ge(S["weights_used"], used_after(turn, 49 + 2 * a))
                dve.scalar_tensor_tensor(tb[:, c, :], tb[:, c, :], 1.0, low8[:, c, :], ALU.add, ALU.mult)\
                   .then_inc(S["yb"], 1)
                dve.wait_ge(S["yb"], at("yb", L, a + 1))
                dve.tensor_tensor(y32[:, c, :], ta[:, c, :], tb[:, c, :], ALU.add).then_inc(S["y_sum"], 1)
            for a in range(2):
                c = slice(4 * a, 4 * a + 4)
                dve.wait_ge(S["y_hi"], at("y_hi", L, a + 1))
                dve.tensor_tensor(xt_lo[:, c, :], y32[:, c, :], f32(xt_hi[:, c, :]), ALU.subtract)\
                   .then_inc(S["y_lo"], 1)
            split_lo(dve, turn, range(56, 60))

        def pool_mix1(pool, L):
            pool_hold(pool, S["x_ready"], norm_done(3 * L))
            for src, dst in ((A["hg_norm_g"], rows[:, 0, 0:512]), (A["sg_ln_g"], rows[:, 0, 512:1024]),
                             (A["sg_ln_b"], rows[:, 1, 0:512])):
                pool.dma_start(dst, src[bass.ds(L, 1), :].rearrange("a n -> (a n)").partition_broadcast(P))\
                    .then_inc(S["mixrows1"], 16)
            pool.dma_start(ws_nat, A["sg_ws"][bass.ds(L, 1), :, :, :].rearrange("l g t s -> t (l g) s"))\
                .then_inc(S["ws_in"], 16)
            pool.wait_ge(S["o_var"], at("o_var", L))
            pool.tensor_tensor(rstd[:, 0:8], var[:, 0:8], neg_half[:, :], ALU.pow).then_inc(S["o_rstd"], 1)
            pool_hold(pool, S["ws_out"], at("ws_out", L))
            for g in range(H):
                pool.affine_select(ws_t[:, g, :], ws_t[:, g, :], [[1, P]], ALU.is_ge, 0.0, base=0,
                                   channel_multiplier=-1).then_inc(S["ws_low"], 1)
            pool.wait_ge(S["v_var"], at("v_var", L))
            pool.tensor_tensor(rstd[:, 0:2], var[:, 0:2], neg_half[:, 0:2], ALU.pow).then_inc(S["v_rstd"], 1)
            pool_hold(pool, S["v_ready"], at("v_ready", L))

        def load_ln_rows(pool, L, j):
            for g, src in enumerate((A["ln_g"], A["ln_b"])):
                pool.dma_start(rows[:, g, :], src[bass.ds(L, 1), j, :].rearrange("a n -> (a n)")
                               .partition_broadcast(P)).then_inc(S["rows"], 16)

        def act_pre(act, n, before):
            for i in range(NT):
                act.wait_ge(S["x_ready"], norm_done(before, i + 1))
                act.activation(xh[:, i, :], x[:, i, :], ACT.Square, accum_out=ss[:, i:i + 1])\
                   .then_inc(S["pre_ss"], 1)

        def dve_pre(dve, n):
            dve.wait_ge(S["pre_ss"], at("pre_ss", n))
            dve.tensor_scalar(var[:, 0:2], ss[:, 0:2], 1.0 / D, NORM_EPS, ALU.mult, ALU.add).then_inc(S["pre_var"], 1)
            dve.wait_ge(S["pre_rstd"], at("pre_rstd", n))
            for i in range(NT):
                dve.tensor_scalar(xh[:, i, :], x[:, i, :], rstd[:, i:i + 1], None, ALU.mult).then_inc(S["pre_xhat"], 1)

        def pool_pre(pool, n):
            pool.wait_ge(S["pre_var"], at("pre_var", n))
            pool.tensor_tensor(rstd[:, 0:2], var[:, 0:2], neg_half[:, 0:2], ALU.pow).then_inc(S["pre_rstd"], 1)

        def act_post(act, n, out_at):
            act.wait_ge(S["weights_used"], out_at)
            for i in range(NT):
                act.activation(r[:, i, :], acc[:, i, :], ACT.Square, accum_out=ss[:, i:i + 1])\
                   .then_inc(S["post_ss"], 1)

        def dve_post(dve, n, factor):
            dve.wait_ge(S["post_ss"], at("post_ss", n))
            dve.tensor_scalar(var[:, 0:2], ss[:, 0:2], 1.0 / D, NORM_EPS, ALU.mult, ALU.add).then_inc(S["post_var"], 1)
            dve.wait_ge(S["rows"], n * 16 + (3 * DEPTH * PER["rows"] + 16))
            dve.wait_ge(S["post_rstd"], at("post_rstd", n))
            for i in range(NT):
                dve.scalar_tensor_tensor(r[:, i, :], acc[:, i, :], rstd[:, i:i + 1], rows[:, 0, :], ALU.mult,
                                         ALU.mult).then_inc(S["post_scaled"], 1)
                dve.wait_ge(S["post_scaled"], at("post_scaled", n, i + 1))
                dve.scalar_tensor_tensor(x[:, i, :], r[:, i, :], factor, x[:, i, :], ALU.mult, ALU.add)\
                   .then_inc(S["x_ready"], 1)

        def pool_post(pool, n):
            pool.wait_ge(S["post_var"], at("post_var", n))
            pool.tensor_tensor(rstd[:, 0:2], var[:, 0:2], neg_half[:, 0:2], ALU.pow).then_inc(S["post_rstd"], 1)

        def load_post_row(pool, L, j):
            pool.dma_start(rows[:, 0, :], A["norm_gain_2"][bass.ds(L, 1), j, :].rearrange("a n -> (a n)")
                           .partition_broadcast(P)).then_inc(S["rows"], 16)

        def sp_mix2(sp, turn, w, wo):
            for j in range(8):
                load(sp, turn, j, w_cols(w, 1536 + j * P, P), KD)
            for k in range(KD):
                load(sp, turn, 8 + k, w_cols(w, 2560, 1024, k, 1), 1)
            for k in range(KD):
                load(sp, turn, 16 + k, w_cols(w, 0, 1024, k, 1), 1)
            for k in range(4):
                load(sp, turn, 24 + k, w_cols(w, 1024, 512, 2 * k, 2), 2)
            for k in range(KD):
                load(sp, turn, 28 + k, w_cols(wo, 0, 1024, k, 1), 1)

        g_bank = bank[:, 0, 0:2 * NG].rearrange("p (i g) -> p i g", i=NT)
        m_s = bank[:, 0, :].rearrange("p (s t) -> p s t", s=NT)
        m_bc = bank[:, 1, :].rearrange("p (d t) -> p d t", d=2)

        def m_cols(d, s):
            if d == 0:
                return (0, 256, 0) if s == 0 else (128, 256, 256)
            return (0, 128, 0) if s == 0 else (0, 256, 128)

        def pe_mix2(pe, L, turn, xt):
            pe.wait_ge(S["xt_lo"], at("xt_lo", xt))
            pe.wait_ge(S["wg_lo"], at("wg_lo", L))
            for i in range(NT):
                for k in range(KD):
                    mm = by_token(pe, g_bank[:, i, :], wg_hi[:, k, :], wg_lo[:, k, :],
                                  xt_hi[:, k, i * P:(i + 1) * P], xt_lo[:, k, i * P:(i + 1) * P],
                                  k == 0, k == KD - 1)
            mm.then_inc(S["gates"], 1)
            for j in range(8):
                feature_unit(pe, turn, j, KD, xt_hi, xt_lo, [turned[:, j, :]], 0, KD)
                if j == 3:
                    pe.wait_ge(S["g_logf"], at("g_logf", L))
                    for m, src in enumerate((g_i, g_lf)):
                        for i in range(NT):
                            mm = pe.transpose(bank[0:8, 1, m * T + i * P:m * T + (i + 1) * P], src[:, i, :], ident)
                    mm.then_inc(S["g_turned"], 1)
            for k in range(KD):
                if k == 0:
                    pe.wait_ge(S["g_rows"], at("g_rows", L))
                token_unit(pe, turn, 8 + k, xt_hi[:, k, :], xt_lo[:, k, :], acc, k == 0, k == KD - 1)
                if k == 4:
                    pe.wait_ge(S["mqk_out"], at("mqk_out", L))
                    pe_hold(pe, S["g_nm"], at("g_nm", L))
                    for m, which in enumerate((GA, GNM)):
                        for d in range(2):
                            for i in range(NT):
                                at_ = ((m * 2 + d) * 2 + i) * 8
                                mm = pe.transpose(bank[:, 4, at_:at_ + 8], grow[:, which[d], i * P:(i + 1) * P],
                                                  ident[0:8, 0:8])
                    mm.then_inc(S["g_cols_turned"], 1)

            def m_pair(h):
                if h == 0:
                    pe.wait_ge(S["mv_out"], at("mv_out", L))
                    pe.wait_ge(S["mo_out"], at("mo_out", L))
                    pe.wait_ge(S["k_scaled"], at("k_scaled", L))
                else:
                    pe_hold(pe, S["m_p"], at("m_p", L, 4 * h))
                for s in range(NT):
                    pe.matmul(m_s[:, s, :], conv_y[:, 4 + h, s * P:(s + 1) * P], conv_y[:, h, :],
                              start=True, stop=True)
                for d in range(2):
                    mm = pe.matmul(m_bc[:, d, :], sel[:, d * H + h, :], grow[:, GNEG[d], :], start=True, stop=True)
                mm.then_inc(S["m_scores"], 1)

            def m_out(h):
                for d in range(2):
                    pe.wait_ge(S["m_p"], at("m_p", L, 4 * h + 2 * d + 2))
                    if h:
                        pe.wait_ge(S["m_cell"], at("m_cell", L, 2 * h))
                    else:
                        pe.wait_ge(S["margins"], at("margins", L))
                    for i in range(NT):
                        o = bank[:, 2 + d, i * 129:(i + 1) * 129]
                        ss_ = [s for s in range(NT) if (s <= i if d == 0 else s >= i)]
                        for s in ss_:
                            c0, c1, p0 = m_cols(d, s)
                            lhs = m_pt[:, d, p0 + i * P - c0:p0 + (i + 1) * P - c0]
                            mm = pe.matmul(o, lhs, va[:, s, h, :], start=s == ss_[0], stop=s == ss_[-1])
                    mm.then_inc(S["m_num"], 1)

            for k in range(KD):
                if k == 0:
                    pe.wait_ge(S["g_cols"], at("g_cols", L))
                token_unit(pe, turn, 16 + k, xt_hi[:, k, :], xt_lo[:, k, :],
                           bank[:, 4:8, :].rearrange("p (t b) n -> p t (b n)", t=NT), k == 0, k == KD - 1)
                if k % 2 == 0:
                    m_pair(k // 2)
                else:
                    m_out(k // 2)
            pe.wait_ge(S["m_cell"], at("m_cell", L))
            for k in range(4):
                hi, lo = unit(pe, turn, 24 + k)
                for i in range(NT):
                    for kk in range(2):
                        kt = 2 * k + kk
                        mm = by_token(pe, bank[:, i, :], hi[:, kk * 512:(kk + 1) * 512],
                                      lo[:, kk * 512:(kk + 1) * 512], xt_hi[:, kt, i * P:(i + 1) * P],
                                      xt_lo[:, kt, i * P:(i + 1) * P], kt == 0, kt == KD - 1)
                mm.then_inc(S["weights_used"], 1)
            pe.wait_ge(S["rot"], at("rot", L))
            for k in range(KD):
                for i in range(NT):
                    mm = pe.transpose(turned[:, k, i * P:(i + 1) * P], aqk[:, i, k * P:(k + 1) * P], ident)
            mm.then_inc(S["a_turned"], 1)

            def a_scores(h):
                if h == 0:
                    pe.wait_ge(S["a_t_out"], at("a_t_out", L))
                    pe.wait_ge(S["av_out"], at("av_out", L))
                if h >= 2:
                    pe.wait_ge(S["a_masked"], at("a_masked", L, 2 * (h - 1)))
                p0 = 64 * (h % 2)
                for i in range(NT):
                    mm = pe.matmul(bank[:, 4 + h % 2, i * T:(i + 1) * T],
                                   aqk_t[p0:p0 + 64, h // 2, i * P:(i + 1) * P],
                                   aqk_t[p0:p0 + 64, 4 + h // 2, :], start=True, stop=True)
                mm.then_inc(S["a_scores"], 1)

            def a_turn(h):
                pe.wait_ge(S["a_exp"], at("a_exp", L, 2 * h + 2))
                if h >= 2:
                    pe.wait_ge(S["a_p_out"], at("a_p_out", L, h - 1))
                for j in range(NT):
                    for i in range(NT):
                        mm = pe.transpose(bank[:, 6 + h % 2, j * T + i * P:j * T + (i + 1) * P],
                                          a_p[:, h % 2, i, j * P:(j + 1) * P], ident)
                mm.then_inc(S["a_p_turned"], 1)

            def a_values(h):
                pe.wait_ge(S["a_p_out"], at("a_p_out", L, h + 1))
                for i in range(NT):
                    for j in range(NT):
                        mm = pe.matmul(bank[:, 2 + i, h * DH:(h + 1) * DH], a_pt[:, h % 2, j, i * P:(i + 1) * P],
                                       av[:, j, h * DH:(h + 1) * DH], start=j == 0, stop=j == NT - 1)
                mm.then_inc(S["a_o"], 1)

            for h in range(AH + 2):
                if h < AH:
                    a_scores(h)
                if 1 <= h <= AH:
                    a_turn(h - 1)
                if h >= 2:
                    a_values(h - 2)
            pe.wait_ge(S["a_out"], at("a_out", L))
            pe.wait_ge(S["m_out"], at("m_out", L))
            for k in range(KD):
                src = a_out if k < 4 else mlout
                for i in range(NT):
                    mm = pe.transpose(turned[:, k, i * P:(i + 1) * P], src[:, i, (k % 4) * P:(k % 4 + 1) * P], ident)
            mm.then_inc(S["merged_turned"], 1)
            for k in range(KD):
                if k % 4 == 0:
                    pe.wait_ge(S["m_lo"], at("m_lo", L, k // 4 + 1))
                token_unit(pe, turn, 28 + k, xt_hi[:, k, :], xt_lo[:, k, :], acc, k == 0, k == KD - 1)

        GI, GLF = 0, 1
        GCUM, GA, GNEG = (2, 3), (4, 5), (6, 7)
        GNM = GCUM

        def act_mix2(act, L, turn):
            act.wait_ge(S["wg_in"], at("wg_in", L))
            act.activation(wg_hi[:, :, :], wg32[:, :, :], ACT.Copy).then_inc(S["wg_hi"], 1)
            split_hi(act, turn, range(4, 6))
            act.wait_ge(S["g_min"], at("g_min", L))
            act.activation(g_n, g_n, ACT.Exp).then_inc(S["g_exp"], 1)
            act.wait_ge(S["g_exp"], at("g_exp", L))
            act.activation(g_n, g_n, ACT.Ln, bias=1.0).then_inc(S["g_ln"], 1)
            split_hi(act, turn, range(6, 14))
            act.wait_ge(S["weights_used"], used_after(turn, 7))
            act.activation(xp[:, :, 2:2 + T], turned, ACT.Copy).then_inc(S["mqk_out"], 1)
            split_hi(act, turn, range(14, 22))
            act.wait_ge(S["g_cols_turned"], at("g_cols_turned", L))
            act.activation(g_cols, bank[:, 4, 0:64].rearrange("p (m d i r) -> p m d i r", m=2, d=2, i=NT), ACT.Copy)\
               .then_inc(S["g_cols"], 1)
            act.wait_ge(S["weights_used"], used_after(turn, 15))
            act.activation(va[:, :, :, 0:P], acc[:, :, 0:512].rearrange("p i (h e) -> p i h e", h=H), ACT.Copy)\
               .then_inc(S["mv_out"], 1)
            act.activation(gm, acc[:, :, 512:1024], ACT.Tanh, scale=0.5).then_inc(S["mo_out"], 1)
            act.wait_ge(S["conv"], at("conv", L))
            act.activation(conv_y[:, :, :], conv_y[:, :, :], ACT.Silu).then_inc(S["conv_silu"], 1)
            act.wait_ge(S["g_cols"], at("g_cols", L))
            act.activation(g_em, g_cols[:, 1], ACT.Exp).then_inc(S["g_em"], 1)
            for h in range(H):
                for d in range(2):
                    act.wait_ge(S["m_arg"], at("m_arg", L, 4 * h + 2 * d + 2))
                    act.activation(m_w[:, d, :], m_e[:, d, :], ACT.Exp).then_inc(S["m_exp"], 1)
                split_hi(act, turn, [22 + 2 * h, 23 + 2 * h])
            act.wait_ge(S["m_cell"], at("m_cell", L))
            for i in range(NT):
                for h in range(H):
                    n = i * H + h
                    act.activation(m_e[:, 0, 0:P] if n % 2 else m_e[:, 0, P:2 * P], cell[:, i, h * P:(h + 1) * P],
                                   ACT.Square, accum_out=ss[:, n:n + 1]).then_inc(S["m_ss"], 1)
                    act.wait_ge(S["m_ss"], at("m_ss", L, n + 1))
            act.wait_ge(S["weights_used"], used_after(turn, 23))
            act.activation(aqk[:, :, :], bank[:, 4:8, :].rearrange("p (t b) n -> p t (b n)", t=NT), ACT.Copy)\
               .then_inc(S["aqk_out"], 1)
            split_hi(act, turn, range(30, 34))
            act.wait_ge(S["weights_used"], used_after(turn, 27))
            act.activation(av, bank[:, 0:2, :], ACT.Copy).then_inc(S["av_out"], 1)
            act.wait_ge(S["a_turned"], at("a_turned", L))
            act.activation(aqk_t, turned, ACT.Copy).then_inc(S["a_t_out"], 1)
            for h in range(AH + 1):
                if h < AH:
                    for i in range(NT):
                        act.wait_ge(S["a_masked"], at("a_masked", L, 2 * h + i + 1))
                        if h >= 2:
                            act.wait_ge(S["a_p_turned"], at("a_p_turned", L, h - 1))
                        act.activation(a_p[:, h % 2, i, :], a_s[:, h % 2, i, :], ACT.Exp, scale=-1.0,
                                       bias=a_mx[:, h, i:i + 1], accum_out=a_sum[:, h, i:i + 1])\
                           .then_inc(S["a_exp"], 1)
                if h >= 1:
                    act.wait_ge(S["a_p_turned"], at("a_p_turned", L, h))
                    if h >= 3:
                        act.wait_ge(S["a_o"], at("a_o", L, h - 2))
                    act.activation(a_pt[:, (h - 1) % 2], bank[:, 6 + (h - 1) % 2, :]
                                   .rearrange("p (j i) -> p j i", j=NT), ACT.Copy).then_inc(S["a_p_out"], 1)
            act.wait_ge(S["merged_turned"], at("merged_turned", L))
            for a in range(2):
                act.activation(xt_hi[:, 4 * a:4 * a + 4, :], turned[:, 4 * a:4 * a + 4, :], ACT.Copy)\
                   .then_inc(S["m_hi"], 1)
            split_hi(act, turn, range(34, 36))

        def dve_mix2(dve, L, turn):
            dve.wait_ge(S["wg_hi"], at("wg_hi", L))
            dve.tensor_tensor(wg_lo[:, :, :], wg32[:, :, :], f32(wg_hi[:, :, :]), ALU.subtract).then_inc(S["wg_lo"], 1)
            split_lo(dve, turn, range(4, 6))
            dve.wait_ge(S["mixrows2"], at("mixrows2", L))
            dve.wait_ge(S["gates"], at("gates", L))
            gb = g_bank.rearrange("p i (d g r) -> p i d g r", d=2, g=2)
            bias = rows[:, 1, 512:512 + NG].rearrange("p (d g r) -> p d g r", d=2, g=2)
            for g, dst in enumerate((g_i, g_f)):
                for i in range(NT):
                    ins = dve.tensor_tensor(dst[:, i, :].rearrange("p (d r) -> p d r", d=2), gb[:, i, :, g, :],
                                            bias[:, :, g, :], ALU.add)
                ins.then_inc(S["g_biased"], 1)
            dve.wait_ge(S["g_biased"], at("g_biased", L))
            dve.scalar_tensor_tensor(g_n, g_f, -1.0, g_f, ALU.mult, ALU.min).then_inc(S["g_min"], 1)
            dve.tensor_scalar(g_lf, g_f, 0.0, None, ALU.min).then_inc(S["g_min"], 1)
            dve.wait_ge(S["g_min"], at("g_min", L))
            dve.wait_ge(S["g_ln"], at("g_ln", L))
            dve.tensor_tensor(g_lf, g_lf, g_n, ALU.subtract).then_inc(S["g_logf"], 1)
            split_lo(dve, turn, range(6, 10))
            dve.wait_ge(S["g_turned"], at("g_turned", L))
            dve.tensor_copy(grow[:, 0:2, :], bank[0:8, 1, :].rearrange("p (m t) -> p m t", m=2)).then_inc(S["g_rows"], 1)
            dve.wait_ge(S["g_rows"], at("g_rows", L))
            lf = grow[:, GLF, :]
            rev = (slice(None), slice(None, None, -1))
            dve.tensor_tensor_scan(grow[:, GCUM[0], :], ones8[:, :], lf, 0.0, ALU.mult, ALU.add).then_inc(S["g_cum"], 1)
            dve.tensor_tensor_scan(grow[:, GCUM[1], :][rev], ones8[:, :], lf[rev], 0.0, ALU.mult, ALU.add)\
               .then_inc(S["g_cum"], 1)
            for d in range(2):
                dve.wait_ge(S["g_cum"], at("g_cum", L, d + 1))
                dve.tensor_tensor(grow[:, GA[d], :], grow[:, GI, :], grow[:, GCUM[d], :], ALU.subtract)\
                   .then_inc(S["g_a"], 1)
            for d in range(2):
                o, a = grow[:, GNEG[d], :], grow[:, GA[d], :]
                if d:
                    o, a = o[rev], a[rev]
                dve.wait_ge(S["g_a"], at("g_a", L, d + 1))
                dve.tensor_tensor_scan(o, ones8[:, :], a, -1e30, ALU.mult, ALU.max).then_inc(S["g_max"], 1)
            for d in range(2):
                dve.wait_ge(S["g_max"], at("g_max", L, d + 1))
                dve.tensor_scalar(grow[:, GNEG[d], :], grow[:, GNEG[d], :], -1.0, None, ALU.mult).then_inc(S["g_neg"], 1)
            for d in range(2):
                dve.wait_ge(S["g_neg"], at("g_neg", L, d + 1))
                dve.tensor_tensor(grow[:, GNM[d], :], grow[:, GNEG[d], :], grow[:, GCUM[d], :], ALU.subtract)\
                   .then_inc(S["g_nm"], 1)
            split_lo(dve, turn, range(10, 14))
            dve.wait_ge(S["mqk_out"], at("mqk_out", L))
            dve.wait_ge(S["now2"], at("now2", L))
            dve.wait_ge(S["margins"], at("margins", L))
            for tap in range(CONV):
                for k in range(KD):
                    if tap == 0:
                        dve.tensor_scalar(conv_y[:, k, :], xp[:, k, 0:T], conv_now[:, 0, k:k + 1],
                                          conv_now[:, CONV, k:k + 1], ALU.mult, ALU.add).then_inc(S["conv"], 1)
                    else:
                        dve.wait_ge(S["conv"], at("conv", L, 8 * (tap - 1) + k + 1))
                        dve.scalar_tensor_tensor(conv_y[:, k, :], xp[:, k, tap:tap + T], conv_now[:, tap, k:k + 1],
                                                 conv_y[:, k, :], ALU.mult, ALU.add).then_inc(S["conv"], 1)
                split_lo(dve, turn, [14 + tap])
            split_lo(dve, turn, range(19, 22))
            dve.wait_ge(S["conv_silu"], at("conv_silu", L))
            dve.tensor_scalar(conv_y[:, 4:8, :], conv_y[:, 4:8, :], float(P) ** -0.5, None, ALU.mult)\
               .then_inc(S["k_scaled"], 1)
            dve.wait_ge(S["mo_out"], at("mo_out", L))
            dve.scalar_tensor_tensor(gm, gm, 1.0, rows[:, 1, 0:512].unsqueeze(1).broadcast_to([P, NT, 512]),
                                     ALU.add, ALU.mult).then_inc(S["mo_gain"], 1)
            dve.wait_ge(S["g_em"], at("g_em", L))
            for h in range(H):
                dve.wait_ge(S["m_scores"], at("m_scores", L, h + 1))
                for d in range(2):
                    mask = (fwd_mask, bwd_mask)[d]
                    for s in range(NT):
                        c0, c1, p0 = m_cols(d, s)
                        if d == 0:
                            mk = mask if s == 0 else mask[:, 0:P]
                        else:
                            mk = mask[:, P:2 * P] if s == 0 else mask
                        dve.scalar_tensor_tensor(m_e[:, d, p0:p0 + c1 - c0], m_bc[:, d, c0:c1],
                                                 g_cols[:, 0, d, s, d * H + h:d * H + h + 1], mk, ALU.add, ALU.min)\
                           .then_inc(S["m_arg"], 1)
                for d in range(2):
                    dve.wait_ge(S["m_exp"], at("m_exp", L, 2 * h + d + 1))
                    if h:
                        dve.wait_ge(S["m_num"], at("m_num", L, 2 * h - 1 + d))
                    for s in range(NT):
                        c0, c1, p0 = m_cols(d, s)
                        dve.tensor_tensor(m_pt[:, d, p0:p0 + c1 - c0], m_w[:, d, p0:p0 + c1 - c0],
                                          m_s[:, s, c0:c1], ALU.mult).then_inc(S["m_p"], 1)
                split_lo(dve, turn, [22 + 2 * h, 23 + 2 * h])
                nums = [bank[:, 2 + d, 0:258].rearrange("p (i e) -> p i e", i=NT) for d in range(2)]
                for d in range(2):
                    dve.wait_ge(S["m_num"], at("m_num", L, 2 * h + d + 1))
                    dve.tensor_tensor(m_den[:, h, d, :], nums[d][:, :, P], g_em[:, d, :, d * H + h], ALU.max)\
                       .then_inc(S["m_abs"], 1)
                for d in range(2):
                    dve.wait_ge(S["m_abs"], at("m_abs", L, 2 * h + d + 1))
                    dve.scalar_tensor_tensor(m_den[:, h, d, :], nums[d][:, :, P], -1.0, m_den[:, h, d, :],
                                             ALU.mult, ALU.max).then_inc(S["m_den"], 1)
                dve.wait_ge(S["m_den"], at("m_den", L, 2 * h + 2))
                dve.reciprocal(m_rd[:, h], m_den[:, h]).then_inc(S["m_rden"], 1)
                dve.wait_ge(S["m_rden"], at("m_rden", L, h + 1))
                for i in range(NT):
                    dve.tensor_scalar(cell[:, i, h * P:(h + 1) * P], nums[0][:, i, 0:P], m_rd[:, h, 0, i:i + 1], None,
                                      ALU.mult).then_inc(S["m_fwd"], 1)
                for i in range(NT):
                    dve.wait_ge(S["m_fwd"], at("m_fwd", L, 2 * h + i + 1))
                    dve.scalar_tensor_tensor(cell[:, i, h * P:(h + 1) * P], nums[1][:, i, 0:P],
                                             m_rd[:, h, 1, i:i + 1], cell[:, i, h * P:(h + 1) * P], ALU.mult, ALU.add)\
                       .then_inc(S["m_cell"], 1)
            dve.wait_ge(S["m_ss"], at("m_ss", L))
            dve.tensor_scalar(var[:, 0:8], ss[:, 0:8], 1.0 / P, NORM_EPS, ALU.mult, ALU.add).then_inc(S["m_var"], 1)
            dve.wait_ge(S["m_rstd"], at("m_rstd", L))
            dve.tensor_tensor(cell.rearrange("p i (h v) -> p (i h) v", h=H), cell.rearrange("p i (h v) -> p (i h) v", h=H),
                              rstd[:, 0:8].unsqueeze(2).broadcast_to([P, 8, P]), ALU.mult).then_inc(S["m_norm"], 1)
            dve.wait_ge(S["m_norm"], at("m_norm", L))
            dve.wait_ge(S["mo_gain"], at("mo_gain", L))
            dve.scalar_tensor_tensor(mlout, cell, 0.5, gm, ALU.mult, ALU.mult).then_inc(S["m_out"], 1)
            dve.wait_ge(S["aqk_out"], at("aqk_out", L))
            heads = 2 * AH
            n = 0
            for i in range(NT):
                v = aqk[:, i, :].rearrange("p (h c) -> p h c", c=DH)
                t1, t2 = v[:, :, 0:ROT], v[:, :, ROT:2 * ROT]
                cb, sb_ = (a[:, i:i + 1, :].broadcast_to([P, heads, ROT]) for a in (cos, sin))
                ra, rb, rc, rd = (b_[:, 0 + o * 128:128 + o * 128].rearrange("p (h c) -> p h c", c=ROT)
                                  for b_ in (rot_t, rot_u) for o in (2 * i, 2 * i + 1))
                for o, a, b in ((ra, t1, cb), (rb, t2, sb_), (rc, t2, cb), (rd, t1, sb_)):
                    dve.tensor_tensor(o, a, b, ALU.mult).then_inc(S["rot"], 1)
                    n += 1
                dve.wait_ge(S["rot"], at("rot", L, n))
                dve.tensor_tensor(t1, ra, rb, ALU.subtract).then_inc(S["rot"], 1)
                dve.tensor_tensor(t2, rc, rd, ALU.add).then_inc(S["rot"], 1)
                n += 2
            split_lo(dve, turn, range(30, 34))
            for h in range(AH):
                for i in range(NT):
                    dve_hold(dve, S["a_scores"], at("a_scores", L, h + 1))
                    if h >= 2:
                        dve_hold(dve, S["a_exp"], at("a_exp", L, 2 * h - 3 + i))
                    dve.tensor_tensor_reduce(a_s[:, h % 2, i, :], bank[:, 4 + h % 2, i * T:(i + 1) * T],
                                             at_mask[:, i, :], -float(DH) ** -0.5, 1e30, ALU.add, ALU.min,
                                             a_mx[:, h, i:i + 1]).then_inc(S["a_masked"], 1)
            dve.wait_ge(S["a_exp"], at("a_exp", L))
            dve.reciprocal(a_rs, a_sum).then_inc(S["a_rden"], 1)
            dve.wait_ge(S["a_rden"], at("a_rden", L))
            dve.wait_ge(S["m_out"], at("m_out", L))
            dve.wait_ge(S["a_o"], at("a_o", L))
            for i in range(NT):
                ins = dve.tensor_tensor(a_out[:, i, :].rearrange("p (h c) -> p h c", h=AH),
                                        bank[:, 2 + i, :].rearrange("p (h c) -> p h c", h=AH),
                                        a_rs[:, :, i:i + 1].broadcast_to([P, AH, DH]), ALU.mult)
            ins.then_inc(S["a_out"], 1)
            for a in range(2):
                dve.wait_ge(S["m_hi"], at("m_hi", L, a + 1))
                dve.tensor_tensor(xt_lo[:, 4 * a:4 * a + 4, :], turned[:, 4 * a:4 * a + 4, :],
                                  f32(xt_hi[:, 4 * a:4 * a + 4, :]), ALU.subtract).then_inc(S["m_lo"], 1)
            split_lo(dve, turn, range(34, 36))

        def pool_mix2(pool, L):
            pool.dma_start(rows[:, 1, 0:512], A["mlstm_norm_gain_2"][bass.ds(L, 1), :].rearrange("a n -> (a n)")
                           .partition_broadcast(P)).then_inc(S["mixrows2"], 16)
            pool.dma_start(rows[:, 1, 512:512 + NG], A["gate_bias_2"][bass.ds(L, 1), :, :]
                           .rearrange("a k h -> (a k h)").partition_broadcast(P)).then_inc(S["mixrows2"], 16)
            pool.memset(xp[:, :, 0:2], 0.0).then_inc(S["margins"], 1)
            pool.memset(xp[:, :, T + 2:T + 4], 0.0).then_inc(S["margins"], 1)
            pool.memset(va[:, :, :, P:P + 1], 1.0).then_inc(S["margins"], 1)
            pool.wait_ge(S["m_var"], at("m_var", L))
            pool.tensor_tensor(rstd[:, 0:8], var[:, 0:8], neg_half[:, :], ALU.pow).then_inc(S["m_rstd"], 1)

        block = ctx.enter_context(nc.Block())

        def turns1(L):
            t = L * LAYER1_TURNS
            return t, t + FFN_TURNS, t + (FFN_TURNS + MIX1_UNITS // RING)

        def turns2(L):
            t = L * LAYER2_TURNS + DEPTH * LAYER1_TURNS
            return t, t + FFN_TURNS, t + (FFN_TURNS + MIX2_UNITS // RING)

        def ln_cols(j):
            return ln_now[:, 0, j, :], ln_now[:, 1, j, :]

        def of_layer(w, L):
            return w[bass.ds(L, 1)].rearrange("l k c -> (l k) c")

        def of_half(w, L, j):
            return w[bass.ds(L, 1), j].rearrange("l k c -> (l k) c")

        @block.sync
        def _(sp):
            for i in range(NT):
                sp.dma_start(xh[:, i, :], A["x"][0, i * P:(i + 1) * P, :]).then_inc(S["x_in"], 16)
            sp.dma_start(const[:, :], A["shape_constants"]).then_inc(S["const_in"], 16)
            with sp.Fori(0, DEPTH) as L:
                t_ffn1, t_mix, t_ffn2 = turns1(L)
                sp_ffn(sp, t_ffn1, of_layer(A["ffn1_w13"], L), of_layer(A["ffn1_w2"], L))
                sp_mix1(sp, t_mix, of_layer(A["w_in"], L), of_layer(A["w_branch_a"], L),
                        of_layer(A["w_branch_b"], L), of_layer(A["w_out"], L))
                sp_ffn(sp, t_ffn2, of_layer(A["ffn2_w13"], L), of_layer(A["ffn2_w2"], L))
            with sp.Fori(0, DEPTH) as L:
                t_ffn1, t_mix, t_ffn2 = turns2(L)
                sp_ffn(sp, t_ffn1, of_half(A["ffn_w_in_2"], L, 0), of_half(A["ffn_w_out_2"], L, 0))
                sp_mix2(sp, t_mix, of_layer(A["mix_w_in_2"], L), of_layer(A["mix_w_out_2"], L))
                sp_ffn(sp, t_ffn2, of_half(A["ffn_w_in_2"], L, 1), of_half(A["ffn_w_out_2"], L, 1))
            for i in range(NT):
                sp.wait_ge(S["x_ready"], norm_done(6 * DEPTH - 1, i + 1))
                sp.dma_start(out[0, i * P:(i + 1) * P, :], x[:, i, :]).then_inc(S["x_out"], 16)
            sp.wait_ge(S["x_out"], 32)

        @block.gpsimd
        def _(pool):
            tab = lambda name, pat: A[name].rearrange(pat, p=P)
            for dst, src in ((t_rows[0:48, 0, :], tab("ln_g", "l j (k p) -> (l j k) p")),
                             (t_rows[48:96, 0, :], tab("ln_b", "l j (k p) -> (l j k) p")),
                             (t_rows[0:96, 1, :], tab("norm_gain_2", "l j (k p) -> (l j k) p")),
                             (t_rows[0:40, 2, :], tab("conv_w_2", "l j (k p) -> l (j k) p")[0]),
                             (t_rows[40:48, 2, :], tab("conv_b_2", "l (k p) -> l k p")[0]),
                             (t_rows[48:88, 2, :], tab("conv_w_2", "l j (k p) -> l (j k) p")[1]),
                             (t_rows[88:96, 2, :], tab("conv_b_2", "l (k p) -> l k p")[1]),
                             (t_rows[0:8, 3, :], tab("sg_bs", "l g p -> (l g) p")),
                             (t_rows[8:16, 3, :], tab("hg_lb", "l (k p) -> (l k) p"))):
                pool.dma_start(dst, src).then_inc(S["tables_in"], 16)
            for i in range(NT):
                pool.dma_start(x[:, i, :], A["x"][0, i * P:(i + 1) * P, :]).then_inc(S["tables_in"], 16)
            pool.dma_start(sel[:, :, :], A["row_selectors"]).then_inc(S["tables_in"], 16)
            pool.memset(neg_half[:, :], -0.5).then_inc(S["ones_set"], 1)
            pool.memset(ones8[:, :], 1.0).then_inc(S["ones_set"], 1)
            pool.memset(ln_tab[:, 0, 0, :], 1.0).then_inc(S["ones_set"], 1)
            pool.memset(ln_tab[:, 1, 0, :], 0.0).then_inc(S["ones_set"], 1)
            pool.wait_ge(S["ones_set"], 2)
            with pool.Fori(0, DEPTH) as L:
                pool_hold(pool, S["x_ready"], norm_done(3 * L - 1))
                load_ln_rows(pool, L, 0)
                pool_layer_norm(pool, 3 * L)
                pool_mix1(pool, L)
                load_ln_rows(pool, L, 1)
                pool_layer_norm(pool, 3 * L + 1)
                pool_hold(pool, S["x_ready"], norm_done(3 * L + 1))
                load_ln_rows(pool, L, 2)
                pool_layer_norm(pool, 3 * L + 2)
            with pool.Fori(0, DEPTH) as L:
                pool_hold(pool, S["x_ready"], norm_done(3 * L + 5))
                pool_pre(pool, 3 * L)
                load_post_row(pool, L, 1)
                pool.dma_start(wg32[:, :, :], A["mix_w_in_2"][bass.ds(L, 1), :, 3584:3600]
                               .rearrange("l (k p) c -> p (l k) c", p=P)).then_inc(S["wg_in"], 16)
                pool_post(pool, 3 * L)
                pool_hold(pool, S["x_ready"], norm_done(3 * L + 6))
                pool_pre(pool, 3 * L + 1)
                load_post_row(pool, L, 3)
                pool_mix2(pool, L)
                pool_post(pool, 3 * L + 1)
                pool_hold(pool, S["x_ready"], norm_done(3 * L + 7))
                pool_pre(pool, 3 * L + 2)
                load_post_row(pool, L, 5)
                pool_post(pool, 3 * L + 2)

        @block.scalar
        def _(act):
            act.wait_ge(S["lb_step"], 3)
            act.activation(lb_tmp[:, 3:5, :], lb_tmp[:, 1:3, :], ACT.Exp).then_inc(S["lb_exp"], 1)
            with act.Fori(0, DEPTH) as L:
                t_ffn1, t_mix, t_ffn2 = turns1(L)
                split_hi(act, t_ffn1, range(4))
                act.wait_ge(S["now1"], at("now1", L))
                act_turn(act, 3 * L, *ln_cols(0))
                act_ffn(act, t_ffn1, L * 2 * STEPS)
                split_hi(act, t_mix, range(4))
                act_turn(act, 3 * L + 1, *ln_cols(1))
                act_mix1(act, L, t_mix)
                split_hi(act, t_ffn2, range(4))
                act_turn(act, 3 * L + 2, *ln_cols(2))
                act_ffn(act, t_ffn2, L * 2 * STEPS + STEPS)
            with act.Fori(0, DEPTH) as L:
                t_ffn1, t_mix, t_ffn2 = turns2(L)
                split_hi(act, t_ffn1, range(4))
                act_pre(act, 3 * L, 3 * L + 5)
                act.wait_ge(S["now2"], at("now2", L))
                act_turn(act, 3 * L + 6, gain_now[:, 0, :], None)
                act_ffn(act, t_ffn1, L * 2 * STEPS + 2 * DEPTH * STEPS)
                split_hi(act, t_mix, range(4))
                act_post(act, 3 * L, used_after(t_ffn1, FFN_UNITS - 1))
                act_pre(act, 3 * L + 1, 3 * L + 6)
                act_turn(act, 3 * L + 7, gain_now[:, 2, :], None)
                act_mix2(act, L, t_mix)
                split_hi(act, t_ffn2, range(4))
                act_post(act, 3 * L + 1, used_after(t_mix, MIX2_UNITS - 1))
                act_pre(act, 3 * L + 2, 3 * L + 7)
                act_turn(act, 3 * L + 8, gain_now[:, 4, :], None)
                act_ffn(act, t_ffn2, L * 2 * STEPS + (2 * DEPTH + 1) * STEPS)
                act_post(act, 3 * L + 2, used_after(t_ffn2, FFN_UNITS - 1))

        @block.vector
        def _(dve):
            dve.sem_inc(S["lo_ready"], RING)
            dve.wait_ge(S["tables_turned"], 1)
            c = [bank[:, 0, j * P:(j + 1) * P] for j in range(4)]
            for n, (dst, src) in enumerate((
                    (ln_tab[:, 0, 1:7, :], c[0][:, 0:48]), (ln_tab[:, 1, 1:7, :], c[0][:, 48:96]),
                    (gain_tab, c[1][:, 0:96]), (conv_tab, c[2][:, 0:96]),
                    (sgb_tab, c[3][:, 0:8]), (lbr_tab, c[3][:, 8:16]))):
                pat = {3: "p (a k) -> p a k", 4: "p (l j k) -> p l j k"}[len(dst.shape)]
                src = src.rearrange(pat, k=dst.shape[-1]) if len(dst.shape) == 3 else \
                    src.rearrange(pat, k=dst.shape[-1], j=dst.shape[-2])
                dve.tensor_copy(dst, src).then_inc(S["tables_out"], 1)
            dve.wait_ge(S["tables_out"], 6)
            mx, e = lb_tmp[:, 0, :], lb_tmp[:, 3:5, :]
            dve.tensor_tensor(mx, lbr_tab[:, 0, :], lbr_tab[:, 1, :], ALU.max).then_inc(S["lb_step"], 1)
            dve.wait_ge(S["lb_step"], 1)
            for l in range(2):
                dve.tensor_tensor(lb_tmp[:, 1 + l, :], lbr_tab[:, l, :], mx, ALU.subtract).then_inc(S["lb_step"], 1)
            dve.wait_ge(S["lb_exp"], 1)
            dve.tensor_tensor(lb_tmp[:, 5, :], e[:, 0, :], e[:, 1, :], ALU.add).then_inc(S["lb_step"], 1)
            dve.wait_ge(S["lb_step"], 4)
            dve.reciprocal(mx, lb_tmp[:, 5, :]).then_inc(S["lb_step"], 1)
            dve.wait_ge(S["lb_step"], 5)
            dve.tensor_tensor(lb_tab[:, 1, :], e[:, 1, :], mx, ALU.mult).then_inc(S["lb_step"], 1)
            dve.memset(lb_tab[:, 0, :], 0.0).then_inc(S["lb_step"], 1)
            dve.wait_ge(S["lb_step"], 7)
            dve.tensor_scalar(om_tab, lb_tab, -1.0, 1.0, ALU.mult, ALU.add).then_inc(S["lb_step"], 1)
            dve.wait_ge(S["lb_step"], 8)
            dve.wait_ge(S["ones_set"], 4)
            dve.wait_ge(S["const_in"], 16)
            dve.wait_ge(S["x_in"], 16 * NT)
            dve.wait_ge(S["tables_in"], 16 * 12)
            dve.sem_inc(S["ln_xhat"], NT)
            dve.sem_inc(S["x_ready"], NT)
            with dve.Fori(0, DEPTH) as L:
                t_ffn1, t_mix, t_ffn2 = turns1(L)
                for g in range(2):
                    dve.tensor_copy(ln_now[:, g, :, :], ln_tab[:, g, bass.ds(3 * L, 3), :]).then_inc(S["now1"], 1)
                for dst, src in ((sgb_now, sgb_tab), (lb_now, lb_tab), (om_now, om_tab)):
                    dve.tensor_copy(dst.unsqueeze(1), src[:, bass.ds(L, 1), :]).then_inc(S["now1"], 1)
                split_lo(dve, t_ffn1, range(4))
                dve_hold(dve, S["now1"], at("now1", L))
                dve_turn(dve, 3 * L, *ln_cols(0))
                dve_ffn(dve, t_ffn1, L * 2 * STEPS)
                split_lo(dve, t_mix, range(4))
                dve_layer_norm(dve, 3 * L, used_after(t_ffn1, FFN_UNITS - 1))
                dve_turn(dve, 3 * L + 1, *ln_cols(1))
                dve_residual(dve, 3 * L)
                dve_mix1(dve, L, t_mix)
                split_lo(dve, t_ffn2, range(4))
                dve_layer_norm(dve, 3 * L + 1, used_after(t_mix, MIX1_UNITS - 1))
                dve_turn(dve, 3 * L + 2, *ln_cols(2))
                dve_residual(dve, 3 * L + 1)
                dve_ffn(dve, t_ffn2, L * 2 * STEPS + STEPS)
                dve_layer_norm(dve, 3 * L + 2, used_after(t_ffn2, FFN_UNITS - 1))
                dve_residual(dve, 3 * L + 2)
            with dve.Fori(0, DEPTH) as L:
                t_ffn1, t_mix, t_ffn2 = turns2(L)
                dve_hold(dve, S["x_ready"], norm_done(3 * L + 5))
                for dst, src in ((gain_now, gain_tab), (conv_now, conv_tab)):
                    dve.tensor_copy(dst.unsqueeze(1), src[:, bass.ds(L, 1), :, :]).then_inc(S["now2"], 1)
                split_lo(dve, t_ffn1, range(4))
                dve_pre(dve, 3 * L)
                dve.wait_ge(S["now2"], at("now2", L))
                dve_turn(dve, 3 * L + 6, gain_now[:, 0, :], None)
                dve_ffn(dve, t_ffn1, L * 2 * STEPS + 2 * DEPTH * STEPS)
                split_lo(dve, t_mix, range(4))
                dve_post(dve, 3 * L, 0.5)
                dve_pre(dve, 3 * L + 1)
                dve_turn(dve, 3 * L + 7, gain_now[:, 2, :], None)
                dve_mix2(dve, L, t_mix)
                split_lo(dve, t_ffn2, range(4))
                dve_post(dve, 3 * L + 1, 1.0)
                dve_pre(dve, 3 * L + 2)
                dve_turn(dve, 3 * L + 8, gain_now[:, 4, :], None)
                dve_ffn(dve, t_ffn2, L * 2 * STEPS + (2 * DEPTH + 1) * STEPS)
                dve_post(dve, 3 * L + 2, 0.5)

        @block.tensor
        def _(pe):
            pe.sem_inc(S["weights_used"], RING)
            pe.wait_ge(S["const_in"], 16)
            pe.wait_ge(S["tables_in"], 16 * 12)
            for j in range(3):
                pe.transpose(bank[:, 0, j * P:j * P + 96], t_rows[0:96, j, :], ident[0:96, 0:96])
            pe.transpose(bank[:, 0, 3 * P:3 * P + 16], t_rows[0:16, 3, :], ident[0:16, 0:16])\
              .then_inc(S["tables_turned"], 1)
            with pe.Fori(0, DEPTH) as L:
                t_ffn1, t_mix, t_ffn2 = turns1(L)
                pe_turn(pe, S["ln_xhat"], lambda i: xhat_done(3 * L - 1, i + 1))
                pe_ffn(pe, t_ffn1, L * 2 * STEPS, 3 * L)
                pe_turn(pe, S["ln_xhat"], lambda i: xhat_done(3 * L, i + 1))
                pe_mix1(pe, L, t_mix, 3 * L + 1)
                pe_turn(pe, S["ln_xhat"], lambda i: xhat_done(3 * L + 1, i + 1))
                pe_ffn(pe, t_ffn2, L * 2 * STEPS + STEPS, 3 * L + 2)
            with pe.Fori(0, DEPTH) as L:
                t_ffn1, t_mix, t_ffn2 = turns2(L)
                pe_turn(pe, S["pre_xhat"], lambda i: at("pre_xhat", 3 * L, i + 1))
                pe_ffn(pe, t_ffn1, L * 2 * STEPS + 2 * DEPTH * STEPS, 3 * L + 6)
                pe_turn(pe, S["pre_xhat"], lambda i: at("pre_xhat", 3 * L + 1, i + 1))
                pe_mix2(pe, L, t_mix, 3 * L + 7)
                pe_turn(pe, S["pre_xhat"], lambda i: at("pre_xhat", 3 * L + 2, i + 1))
                pe_ffn(pe, t_ffn2, L * 2 * STEPS + (2 * DEPTH + 1) * STEPS, 3 * L + 8)


def shape_constants():
    import numpy as np
    s = np.arange(P)[:, None]
    t = np.arange(P)[None, :]
    hg = [(s == t)]
    for b in LEVELS[1:6]:
        hg.append((s // (2 * b) == t // (2 * b)) & (s % (2 * b) < b) & (t % (2 * b) >= b))
    i = np.arange(T)[:, None]
    j = np.arange(T)[None, :]
    count = np.zeros((T, T))
    for window, dilation in ((128, 1), (512, 4), (2048, 16)):
        side = (window // 2) // dilation
        count += ((i - j) % dilation == 0) & (np.abs(i // dilation - j // dilation) <= side)
    logs = np.where(count > 0, np.log(np.maximum(count, 1)) * DH ** 0.5, -1e30)
    logs = logs.reshape(NT, P, T).transpose(1, 0, 2).reshape(P, NT * T)
    none = np.zeros((P, P))
    fwd = np.concatenate([np.where(s <= t, 0.0, -1e30), none], 1)
    bwd = np.concatenate([none, np.where(s >= t, 0.0, -1e30)], 1)
    freq = np.float32(500000.0) ** (-np.arange(ROT, dtype=np.float32) / np.float32(ROT))
    ang = (np.arange(T, dtype=np.float32)[:, None] * freq[None, :]).astype(np.float32)
    turn = [f(ang).reshape(NT, P, ROT).transpose(1, 0, 2).reshape(P, NT * ROT) for f in (np.cos, np.sin)]
    table = np.concatenate([np.eye(P), *[m.astype(float) for m in hg], logs, fwd, bwd, *turn], 1).astype(np.float32)
    rows = np.zeros((2 * H, 2 * H, P), np.float32)
    for k in range(2 * H):
        rows[k, k, :] = 1.0
    return table, rows


_INS = ["x", "ffn1_w13", "ffn1_w2", "ffn2_w13", "ffn2_w2", "ln_g", "ln_b", "w_in", "hg_lb", "hg_norm_g",
        "sg_ln_g", "sg_ln_b", "sg_ws", "sg_bs", "w_branch_a", "w_branch_b", "w_out", "norm_gain_2",
        "ffn_w_in_2", "ffn_w_out_2", "mix_w_in_2", "conv_w_2", "conv_b_2", "gate_bias_2",
        "mlstm_norm_gain_2", "mix_w_out_2"]


def kernel(**inputs):
    import numpy as _np
    import concourse.bacc as _bacc
    from concourse import mybir as _mybir
    from concourse.bass_utils import run_bass_kernel_spmd as _run

    nc = _bacc.Bacc("TRN2", target_bir_lowering=False, num_devices=1)
    arrays = {name: _np.ascontiguousarray(inputs[name]) for name in _INS}
    arrays["shape_constants"], arrays["row_selectors"] = shape_constants()
    aps = {name: nc.dram_tensor("in_" + name, a.shape, _mybir.dt.from_np(a.dtype), kind="ExternalInput").ap()
           for name, a in arrays.items()}
    out = nc.dram_tensor("out", (1, T, D), F32, kind="ExternalOutput").ap()
    build(nc, aps, out)
    r = _run(nc, [{"in_" + name: a for name, a in arrays.items()}], core_ids=[0])
    return r.results[0]["out"]
```

```python
from contextlib import ExitStack

import concourse.bass as bass
from concourse import mybir

ALU = mybir.AluOpType
ACT = mybir.ActivationFunctionType
F32 = mybir.dt.float32
F32R = mybir.dt.float32r
I32 = mybir.dt.int32

P = 128
T = 256
NT = T // P
D = 1024
KD = D // P
DEPTH = 2
D_FF = 2816
FB = 256
STEPS = D_FF // FB
RING = 6
UNIT = 1024
FFN_UNITS = 6 * STEPS
MIX1_UNITS = 60
MIX2_UNITS = 36
LAYER1_TURNS = (2 * FFN_UNITS + MIX1_UNITS) // RING
LAYER2_TURNS = (2 * FFN_UNITS + MIX2_UNITS) // RING
FFN_TURNS = FFN_UNITS // RING

ALPHA = (2 * DEPTH) ** 0.25
LN_EPS = 1e-5
RMS_EPS = 1e-6
NORM_EPS = 1e-6
H = 4
AH = 8
DH = 64
ROT = 8
NG = 16
CONV = 5
LEVELS = [0, 1, 2, 4, 8, 16, 32, 64]

PER = dict(
    silu=1, gated=1, h_hi=1, h_lo=1,
    x_turned=4, xt_f32a=8, xt_f32v=8, xt_hi_a=2, xt_hi_v=2, xt_lo=3, xt_lo_p=1, tile0_out=1,
    ln_resid=2, ln_mean=2, ln_ss=2, ln_var=2, ln_rstd=2, ln_xhat=2, x_scaled=2, x_ready=2,
    now1=5, rows=32, mixrows1=48,
    hg_sig=2, hg_fk=8, hg_q=1, hg_qf=1, hg_scores=9, hg_t=7, hg_qp=7, hg_ks=7, hg_sel=10,
    zg_out=2, hg_gain=1, za_out=1, hg_o=1, o_ss=8, o_var=1, o_rstd=1, o_norm=1, o_gated=1,
    o_turned=1, o_hi=1, o_lo=1,
    zuv_out=2, v_stats=2, v_aggr=2, v_var=1, v_rstd=1, v_hat=2, v_scaled=1, v_ready=1,
    ws_in=16, ws_turned=1, ws_out=1, ws_low=4, mixed=1, ub=4, ub_turned=1, ub_hi=1, ub_lo=1,
    zb_out=1, ya=1, yb=2, y_sum=2, y_hi=2, y_lo=2,
    pre_ss=2, pre_var=2, pre_rstd=2, pre_xhat=2,
    post_ss=4, post_sum=2, post_var=2, post_rstd=2, post_scaled=4,
    now2=2, margins=3, mixrows2=32, wg_in=16, wg_hi=1, wg_lo=1,
    gates=1, gates_out=1, gates_turned=1, g_biased=2, g_min=2, g_exp=1, g_ln=1, g_logf=1, g_turned=1, g_rows=1,
    g_cum=2, g_a=2, g_max=2, g_neg=2, g_nm=2, g_cols_turned=1, g_cols=1, g_em=1,
    mqk_out=1, conv=40, conv_silu=1, k_scaled=1, mo_out=2, mo_gain=1,
    m_scores=4, m_arg=16, m_exp=8, m_p=16, m_num=8, m_den=8, m_abs=8, m_rden=4, m_fwd=8, m_cell=8,
    m_ss=8, m_var=1, m_rstd=1, m_norm=1, m_out=1,
    aqk_out=1, av_out=1, rot=12, a_turned=1, a_t_out=1,
    a_scores=8, a_masked=16, a_exp=16, a_p_turned=8, a_p_out=8, a_o=8, a_rden=1, a_out=1,
    merged_turned=1,
    m_hi=2, m_lo=2,
)


def at(name, turn, which=None):
    return turn * PER[name] + (PER[name] if which is None else which)


def build(nc, A, out):
    ctx = ExitStack()
    with ctx:
        def sb(name, shape, dt=F32):
            return ctx.enter_context(nc.sbuf_tensor(name, shape, dt))

        S = {n: ctx.enter_context(nc.semaphore(n)) for n in PER}
        for n in ("hi_ready", "lo_ready", "weights_used", "x_in", "const_in", "rest_in", "ones_set", "tables_in",
                  "tables_turned", "tables_out", "lb_step", "lb_exp", "x_out", "held"):
            S[n] = ctx.enter_context(nc.semaphore(n))
        staged = [ctx.enter_context(nc.semaphore(f"staged{i}")) for i in range(RING)]

        stage = sb("stage", [P, RING, UNIT])
        w_hi = sb("w_hi", [P, RING, UNIT], F32R)
        w_lo = sb("w_lo", [P, RING, UNIT], F32R)
        x = sb("x", [P, NT, D])
        xh = sb("xh", [P, NT, D])
        r = sb("r", [P, NT, D])
        xt32 = sb("xt32", [P, KD, T])
        xt_hi = sb("xt_hi", [P, KD, T], F32R)
        xt_lo = sb("xt_lo", [P, KD, T], F32R)
        hidden = sb("hidden", [P, 2, NT, FB])
        sil, h32 = hidden[:, 0], hidden[:, 1]
        h_hi = sb("h_hi", [P, NT, FB], F32R)
        h_lo = sb("h_lo", [P, NT, FB], F32R)
        rows = sb("rows", [P, 2, D])
        mt_hi = sb("mt_hi", [P, KD, T], F32R)
        mt_lo = sb("mt_lo", [P, KD, T], F32R)
        const = sb("const", [P, A["shape_constants"].shape[1]])
        sel = sb("sel", [2 * H, 2 * H, P])
        ones8 = sb("ones8", [2 * H, T])
        neg_half = sb("neg_half", [P, 2 * H])
        small = sb("small", [P, 756])
        small_at = [0]

        def few(n):
            small_at[0] += n
            return small[:, small_at[0] - n:small_at[0]]

        scratch = sb("scratch", [P, 10240])
        scratch_at = [0]

        def part(n):
            scratch_at[0] += n
            assert scratch_at[0] <= 10240, scratch_at[0]
            return scratch[:, scratch_at[0] - n:scratch_at[0]]

        bank = ctx.enter_context(nc.psum_tensor("bank", [P, 8, 512], F32))
        acc = bank[:, 0:4, :].rearrange("p (t b) n -> p t (b n)", t=NT)
        turned = bank[:, 4:8, :].rearrange("p b (k t) -> p (b k) t", k=2)
        turned_x = bank[:, 4:8, :].rearrange("p (i b) (k t) -> p i (b k) t", i=NT, k=4)
        low8 = bank[:, 0:4, :].rearrange("p b (k t) -> p (b k) t", k=2)
        gu = bank[:, 4:6, :].rearrange("p j (g t) -> p j g t", g=2)
        gu0 = bank[:, 6:8, :].rearrange("p j (g t) -> p j g t", g=2)

        ident = const[:, 0:128]
        hg_mask = const[:, 128:128 + 6 * 128].rearrange("p (l t) -> p l t", l=6)
        at_mask = const[:, 896:896 + 512].rearrange("p (i j) -> p i j", i=NT)
        fwd_mask = const[:, 1408:1664]
        bwd_mask = const[:, 1664:1920]
        cos = const[:, 1920:1936].rearrange("p (i r) -> p i r", i=NT)
        sin = const[:, 1936:1952].rearrange("p (i r) -> p i r", i=NT)

        t_rows = r[:, :, :].rearrange("p a b -> p (a b)")[:, 0:512].rearrange("p (a b) -> p a b", a=4)
        ln_tab = few(2 * 7 * KD).rearrange("p (g e k) -> p g e k", g=2, e=7)
        gain_tab = few(2 * 6 * KD).rearrange("p (l j k) -> p l j k", l=2, j=6)
        conv_tab = few(2 * 6 * KD).rearrange("p (l j k) -> p l j k", l=2, j=6)
        sgb_tab = few(2 * H).rearrange("p (l h) -> p l h", l=2)
        lbr_tab = few(2 * H).rearrange("p (l h) -> p l h", l=2)
        lb_tab = few(2 * H).rearrange("p (l h) -> p l h", l=2)
        om_tab = few(2 * H).rearrange("p (l h) -> p l h", l=2)
        lb_tmp = few(6 * H).rearrange("p (l h) -> p l h", l=6)
        ln_now = few(2 * 3 * KD).rearrange("p (g e k) -> p g e k", g=2, e=3)
        sgb_now = few(H)
        lb_now = few(H)
        om_now = few(H)
        gain_now = few(6 * KD).rearrange("p (j k) -> p j k", j=6)
        conv_now = few(6 * KD).rearrange("p (j k) -> p j k", j=6)
        stats = sb("stats", [P, NT, 2, 6])
        mv_ = sb("mv_", [P, NT, 2])
        var = sb("var", [P, 2 * H])
        mean = mv_[:, :, 0]
        rstd = sb("rstd", [P, 2 * H])
        ss = sb("ss", [P, 2 * H])

        sig_f = part(1024).rearrange("p (h t) -> p h t", h=H)
        ks = part(1024).rearrange("p (h t) -> p h t", h=H)
        q = part(1024).rearrange("p (h t) -> p h t", h=H)
        qp = part(1024).rearrange("p (h t) -> p h t", h=H)
        tot = part(1024)
        sc = part(1024).rearrange("p (b t) -> p b t", b=2 * H)
        hidden_flat = hidden[:, :, :, :].rearrange("p a b c -> p (a b c)")
        ws_nat = hidden_flat[:, 0:512].rearrange("p (g s) -> p g s", g=H)
        ws_t = hidden_flat[:, 512:1024].rearrange("p (g t) -> p g t", g=H)
        scx = rows[:, 1, 512:1024].rearrange("p (h t) -> p h t", h=H)
        zi = part(1024).rearrange("p (i v) -> p i v", i=NT)
        gz = part(1024).rearrange("p (i v) -> p i v", i=NT)
        tb = part(2048).rearrange("p (k t) -> p k t", k=KD)
        ta = xh[:, :, :].rearrange("p i d -> p (i d)").rearrange("p (k t) -> p k t", k=KD)
        u_ = r[:, 0, :].rearrange("p (i v) -> p i v", i=NT)
        v_ = r[:, 1, :].rearrange("p (i v) -> p i v", i=NT)
        og = qp.rearrange("p h t -> p (h t)").rearrange("p (i v) -> p i v", i=NT)
        sq_junk = q.rearrange("p h t -> p (h t)")
        y32 = xt32

        scratch_at[0] = 0
        xp = part(KD * (T + 4)).rearrange("p (k t) -> p k t", k=KD)
        va = part(2 * H * 129).rearrange("p (i h e) -> p i h e", i=NT, h=H)
        gm = part(1024).rearrange("p (i v) -> p i v", i=NT)
        m_e = hidden_flat[:, 0:768].rearrange("p (d n) -> p d n", d=2)
        m_w = part(768).rearrange("p (d n) -> p d n", d=2)
        m_pt = part(2 * 384).rearrange("p (d n) -> p d n", d=2)
        cell = part(1024).rearrange("p (i v) -> p i v", i=NT)
        mlout = part(1024).rearrange("p (i v) -> p i v", i=NT)
        av = part(1024).rearrange("p (i v) -> p i v", i=NT)
        a_s = part(2 * 512).rearrange("p (b i j) -> p b i j", b=2, i=NT)
        conv_y = xt32
        aqk = r
        aqk_t = xh[:, :, :].rearrange("p i d -> p (i d)").rearrange("p (k t) -> p k t", k=KD)
        xp_flat = xp.rearrange("p k t -> p (k t)")
        a_p = xp_flat[:, 0:1024].rearrange("p (b i j) -> p b i j", b=2, i=NT)
        a_pt = xp_flat[:, 1024:2048].rearrange("p (b i j) -> p b i j", b=2, i=NT)
        a_out = gm
        rot_t = m_e.rearrange("p d n -> p (d n)")
        rot_u = m_w.rearrange("p d n -> p (d n)")
        g_i = few(NT * 8).rearrange("p (i r) -> p i r", i=NT)
        g_f = few(NT * 8).rearrange("p (i r) -> p i r", i=NT)
        g_n = few(NT * 8).rearrange("p (i r) -> p i r", i=NT)
        g_lf = few(NT * 8).rearrange("p (i r) -> p i r", i=NT)
        g_cols = few(NT * 2 * 2 * 8).rearrange("p (m d i r) -> p m d i r", m=2, d=2, i=NT)
        g_em = few(2 * NT * 8).rearrange("p (d i r) -> p d i r", d=2, i=NT)
        a_mx = few(16).rearrange("p (h i) -> p h i", h=AH)
        a_sum = few(16).rearrange("p (h i) -> p h i", h=AH)
        a_rs = few(16).rearrange("p (h i) -> p h i", h=AH)
        m_den = few(16).rearrange("p (h d i) -> p h d i", h=H, d=2)
        m_rd = few(16).rearrange("p (h d i) -> p h d i", h=H, d=2)
        grow = xh[0:2 * H, :, :].rearrange("p i d -> p (i d)")[:, 0:8 * T].rearrange("p (a t) -> p a t", t=T)
        wg32 = part(KD * NG).rearrange("p (k g) -> p k g", k=KD)
        wg_hi, wg_lo = (m[:, 0, 0:KD * NG].rearrange("p (k g) -> p k g", k=KD) for m in (mt_hi, mt_lo))

        def f32(ap):
            return ap.bitcast(F32)

        def place(turn, c):
            return turn + c // RING, c % RING

        def load(sp, turn, c, src, k):
            t, s = place(turn, c)
            sp.wait_ge(S["lo_ready"], t * RING + (s + 1))
            sp.sem_inc(S["held"], 1)
            sp.dma_start(stage[:, s, :][:, 0:k * src.shape[-1]].rearrange("p (k c) -> p k c", k=k), src)\
              .then_inc(staged[s], 16)

        def split_hi(act, turn, cs, n=UNIT):
            for c in cs:
                t, s = place(turn, c)
                act.wait_ge(staged[s], t * 16 + 16)
                act.wait_ge(S["weights_used"], t * RING + (s + 1))
                act.activation(w_hi[:, s, 0:n], stage[:, s, 0:n], ACT.Copy).then_inc(S["hi_ready"], 1)

        def split_lo(dve, turn, cs, n=UNIT):
            for c in cs:
                t, s = place(turn, c)
                dve.wait_ge(S["hi_ready"], t * RING + (s + 1))
                dve.tensor_tensor(w_lo[:, s, 0:n], stage[:, s, 0:n], f32(w_hi[:, s, 0:n]), ALU.subtract)\
                   .then_inc(S["lo_ready"], 1)

        def used_after(turn, c):
            t, s = place(turn, c)
            return t * RING + (s + 1 + RING)

        def unit(pe, turn, c):
            t, s = place(turn, c)
            pe.wait_ge(S["lo_ready"], t * RING + (s + 1 + RING))
            return w_hi[:, s, :], w_lo[:, s, :]

        def by_feature(pe, o, hi, lo, m_hi, m_lo, first, last):
            pe.matmul(o, hi, m_hi, start=first, stop=False)
            pe.matmul(o, hi, m_lo, start=False, stop=False)
            return pe.matmul(o, lo, m_hi, start=False, stop=last)

        def by_token(pe, o, hi, lo, m_hi, m_lo, first, last):
            pe.matmul(o, m_hi, hi, start=first, stop=False)
            pe.matmul(o, m_hi, lo, start=False, stop=False)
            return pe.matmul(o, m_lo, hi, start=False, stop=last)

        def token_unit(pe, turn, c, m_hi, m_lo, o, first, last):
            hi, lo = unit(pe, turn, c)
            for i in range(NT):
                for b in range(2):
                    mm = by_token(pe, o[:, i, b * 512:(b + 1) * 512], hi[:, b * 512:(b + 1) * 512],
                                  lo[:, b * 512:(b + 1) * 512], m_hi[:, i * P:(i + 1) * P],
                                  m_lo[:, i * P:(i + 1) * P], first, last)
            mm.then_inc(S["weights_used"], 1)

        def token_units_by_tile(pe, turn, cs, parts, o, ready):
            for i in range(NT):
                for n, c in enumerate(cs):
                    if i == 0:
                        if n in ready:
                            pe.wait_ge(*ready[n])
                        unit(pe, turn, c)
                    s = place(turn, c)[1]
                    hi, lo = w_hi[:, s, :], w_lo[:, s, :]
                    m_hi, m_lo = parts[n]
                    for b in range(2):
                        mm = by_token(pe, o[:, i, b * 512:(b + 1) * 512], hi[:, b * 512:(b + 1) * 512],
                                      lo[:, b * 512:(b + 1) * 512], m_hi[:, i * P:(i + 1) * P],
                                      m_lo[:, i * P:(i + 1) * P], False, n == len(cs) - 1)
                    if i == NT - 1:
                        mm.then_inc(S["weights_used"], 1)
                    elif n == len(cs) - 1:
                        mm.then_inc(S["tile0_out"], 1)

        def feature_unit(pe, turn, c, nk, m_hi, m_lo, outs, k0, k1):
            hi, lo = unit(pe, turn, c)
            w = P * len(outs)
            hi = hi[:, 0:nk * w].rearrange("p (k c) -> p k c", k=nk)
            lo = lo[:, 0:nk * w].rearrange("p (k c) -> p k c", k=nk)
            for j, o in enumerate(outs):
                for k in range(nk):
                    mm = by_feature(pe, o, hi[:, k, j * P:(j + 1) * P], lo[:, k, j * P:(j + 1) * P],
                                    m_hi[:, k0 + k, :], m_lo[:, k0 + k, :], k0 + k == 0, k0 + k == k1 - 1)
            mm.then_inc(S["weights_used"], 1)

        def dve_hold(dve, sem, value):
            dve.wait_ge(sem, value)
            dve.sem_inc(S["held"], 1)

        def pe_hold(pe, sem, value):
            pe.wait_ge(sem, value)
            pe.sem_inc(S["held"], 1)

        def pool_hold(pool, sem, value):
            pool.wait_ge(sem, value)
            pool.sem_inc(S["held"], 1)

        def norm_done(n, which=None):
            return at("x_ready", n + 1, which)

        def xhat_done(n, which=None):
            return at("ln_xhat", n + 1, which)

        def sp_ffn(sp, turn, w13, w2):
            def load_gu(turn, i, cs):
                for n, c in enumerate(cs):
                    g, kh = n // 2, n % 2
                    src = w13[kh * 512:(kh + 1) * 512, bass.ds(g * D_FF + i * FB, FB)] if not isinstance(i, int) \
                        else w13[kh * 512:(kh + 1) * 512, g * D_FF + i * FB:g * D_FF + (i + 1) * FB]
                    load(sp, turn, c, src.rearrange("(k p) c -> p k c", p=P), 4)

            def load_w2(turn, i, cs):
                for n, c in enumerate(cs):
                    src = w2[bass.ds(i * FB + n * P, P), :] if not isinstance(i, int) \
                        else w2[i * FB + n * P:i * FB + (n + 1) * P, :]
                    load(sp, turn, c, src.rearrange("p (k c) -> p k c", k=1), 1)

            load_gu(turn, 0, [0, 1, 2, 3])
            load_gu(turn, 1, [4, 5, 6, 7])
            with sp.Fori(1, STEPS - 1) as i:
                load_w2(turn + i, i - 1, [2, 3])
                load_gu(turn + i, i + 1, [4, 5, 6, 7])
            load_w2(turn, STEPS - 2, [FFN_UNITS - 4, FFN_UNITS - 3])
            load_w2(turn, STEPS - 1, [FFN_UNITS - 2, FFN_UNITS - 1])

        def act_silu(act, turn, c, n, gu=gu):
            act.wait_ge(S["weights_used"], used_after(turn, c))
            act.activation(sil[:, :, :], gu[:, :, 0, :], ACT.Silu).then_inc(S["silu"], 1)

        last_hi, last_lo = mt_hi[:, 0:NT, :], mt_lo[:, 0:NT, :]

        def act_h(act, n, hi=h_hi[:, :, :]):
            act.wait_ge(S["gated"], n)
            act.activation(hi, h32[:, :, :], ACT.Copy).then_inc(S["h_hi"], 1)

        def act_ffn(act, turn, step0):
            split_hi(act, turn, [4, 5, 6, 7])
            act_silu(act, turn, 3, step0, gu0)
            with act.Fori(1, STEPS - 1) as i:
                split_hi(act, turn + i, [2, 3])
                act_h(act, step0 + i)
                split_hi(act, turn + i, [4, 5, 6, 7])
                act_silu(act, turn + i, 1, step0 + i)
            split_hi(act, turn, [FFN_UNITS - 4, FFN_UNITS - 3])
            act_h(act, step0 + (STEPS - 1))
            split_hi(act, turn, [FFN_UNITS - 2, FFN_UNITS - 1])
            act_silu(act, turn, FFN_UNITS - 5, step0 + (STEPS - 1))
            act_h(act, step0 + STEPS, last_hi)

        def dve_gate(dve, n, gu=gu):
            dve.wait_ge(S["silu"], n)
            dve.tensor_tensor(h32[:, :, :], sil[:, :, :], gu[:, :, 1, :], ALU.mult).then_inc(S["gated"], 1)

        def dve_h(dve, n, hi=h_hi[:, :, :], lo=h_lo[:, :, :]):
            dve.wait_ge(S["h_hi"], n)
            dve.tensor_tensor(lo, h32[:, :, :], f32(hi), ALU.subtract)\
               .then_inc(S["h_lo"], 1)

        def dve_ffn(dve, turn, step0):
            split_lo(dve, turn, [4, 5, 6, 7])
            dve_gate(dve, step0 + 1, gu0)
            with dve.Fori(1, STEPS - 1) as i:
                split_lo(dve, turn + i, [2, 3])
                dve_h(dve, step0 + i)
                split_lo(dve, turn + i, [4, 5, 6, 7])
                dve.wait_ge(S["h_lo"], step0 + i)
                dve_gate(dve, step0 + i + 1)
            split_lo(dve, turn, [FFN_UNITS - 4, FFN_UNITS - 3])
            dve_h(dve, step0 + (STEPS - 1))
            split_lo(dve, turn, [FFN_UNITS - 2, FFN_UNITS - 1])
            dve.wait_ge(S["h_lo"], step0 + (STEPS - 1))
            dve_gate(dve, step0 + STEPS)
            dve_h(dve, step0 + STEPS, last_hi, last_lo)

        def pe_ffn(pe, turn, step0, xt):
            def gate_up(turn, cs, first=False):
                o = gu0 if first else gu
                for n, c in enumerate(cs):
                    g, kh = n // 2, n % 2
                    if first and g == 0:
                        if kh == 0:
                            pe.wait_ge(S["xt_f32a"], at("xt_f32a", xt))
                            pe.wait_ge(S["xt_lo_p"], at("xt_lo_p", xt))
                        pe.wait_ge(S["xt_lo"], at("xt_lo", xt, 2 + kh))
                    feature_unit(pe, turn, c, 4, xt_hi, xt_lo, [o[:, j, g, :] for j in range(2)], 4 * kh, KD)

            def down(turn, cs, n, first):
                pe.wait_ge(S["h_lo"], n)
                for j, c in enumerate(cs):
                    token_unit(pe, turn, c, h_hi[:, j, :], h_lo[:, j, :], acc, first and j == 0, False)

            gate_up(turn, [0, 1, 2, 3], True)
            gate_up(turn, [4, 5, 6, 7])
            down(turn, [8, 9], step0 + 1, True)
            with pe.Fori(2, STEPS - 1) as i:
                pe.wait_ge(S["gated"], step0 + i)
                gate_up(turn + i, [-2, -1, 0, 1])
                down(turn + i, [2, 3], step0 + i, False)
            pe.wait_ge(S["gated"], step0 + (STEPS - 1))
            gate_up(turn, range(FFN_UNITS - 8, FFN_UNITS - 4))
            token_units_by_tile(pe, turn, range(FFN_UNITS - 4, FFN_UNITS),
                                [(h_hi[:, j, :], h_lo[:, j, :]) for j in range(2)]
                                + [(last_hi[:, j, :], last_lo[:, j, :]) for j in range(2)], acc,
                                {0: (S["h_lo"], step0 + (STEPS - 1)), 2: (S["h_lo"], step0 + STEPS)})

        def pe_turn(pe, ready, ready_at):
            for i in range(NT):
                pe.wait_ge(ready, ready_at(i))
                for k in range(KD):
                    mm = pe.transpose(turned_x[:, i, k, :], xh[:, i, k * P:(k + 1) * P], ident)
                    if k % 4 == 3:
                        mm.then_inc(S["x_turned"], 1)

        def dve_turn(dve, n, i, g, b, alone=False):
            dve_gains(dve, n, i, g, b)
            dve_rests(dve, n, i, alone)

        def dve_gains(dve, n, i, g, b):
            t = slice(i * P, (i + 1) * P)
            dve.wait_ge(S["x_turned"], at("x_turned", n, 2 * i + 1))
            if b is None:
                dve.tensor_tensor(xt32[:, 0:4, t], turned_x[:, i, 0:4, :], g[:, 0:4].unsqueeze(2)
                                  .broadcast_to([P, 4, P]), ALU.mult).then_inc(S["xt_f32v"], 4)
            else:
                for k in range(4):
                    dve.tensor_scalar(xt32[:, k, t], turned_x[:, i, k, :], g[:, k:k + 1], b[:, k:k + 1],
                                      ALU.mult, ALU.add).then_inc(S["xt_f32v"], 1)

        def dve_rests(dve, n, i, alone=False):
            t = slice(i * P, (i + 1) * P)
            dve.wait_ge(S["xt_f32v"], at("xt_f32v", n, 4 * i + 4))
            dve.tensor_copy(xt_hi[:, 0:4, t], xt32[:, 0:4, t]).then_inc(S["xt_hi_v"], 1)
            dve.wait_ge(S["xt_hi_v"], at("xt_hi_v", n, i + 1))
            dve.tensor_tensor(xt_lo[:, 0:4, t], xt32[:, 0:4, t], f32(xt_hi[:, 0:4, t]), ALU.subtract)\
               .then_inc(S["xt_lo"], 1)
            if i == NT - 1 or alone:
                dve.wait_ge(S["xt_hi_a"], at("xt_hi_a", n, i + 1))
                dve.tensor_tensor(xt_lo[:, 4:8, t], xt32[:, 4:8, t], f32(xt_hi[:, 4:8, t]), ALU.subtract)\
                   .then_inc(S["xt_lo"] if i == NT - 1 else S["xt_lo_p"], 1)

        def pool_turn(pool, n):
            pool.wait_ge(S["xt_hi_a"], at("xt_hi_a", n, 1))
            pool.tensor_tensor(xt_lo[:, 4:8, 0:P], xt32[:, 4:8, 0:P], f32(xt_hi[:, 4:8, 0:P]), ALU.subtract)\
                .then_inc(S["xt_lo_p"], 1)

        def act_turn(act, n, i, g, b):
            t = slice(i * P, (i + 1) * P)
            act.wait_ge(S["x_turned"], at("x_turned", n, 2 * i + 2))
            for k in range(4, 8):
                act.activation(xt32[:, k, t], turned_x[:, i, k, :], ACT.Identity, scale=g[:, k:k + 1],
                               bias=0.0 if b is None else b[:, k:k + 1]).then_inc(S["xt_f32a"], 1)
            act.wait_ge(S["xt_f32a"], at("xt_f32a", n, 4 * i + 4))
            act.activation(xt_hi[:, 4:8, t], xt32[:, 4:8, t], ACT.Copy).then_inc(S["xt_hi_a"], 1)

        def act_turn_both(act, n, g, b):
            for i in range(NT):
                act_turn(act, n, i, g, b)

        def dve_layer_norm(dve, n, turn, out_at, gb):
            def residual(i):
                if i == 0:
                    dve.wait_ge(S["tile0_out"], at("tile0_out", n))
                    dve.wait_ge(S["x_ready"], norm_done(n - 1))
                else:
                    dve.wait_ge(S["weights_used"], out_at)
                dve.scalar_tensor_tensor(r[:, i, :], x[:, i, :], 2 * ALPHA, acc[:, i, :], ALU.mult, ALU.add,
                                         accum_out=mean[:, i:i + 1]).then_inc(S["ln_resid"], 1)
                dve.wait_ge(S["ln_resid"], at("ln_resid", n, i + 1))
                dve.tensor_scalar(mean[:, i:i + 1], mean[:, i:i + 1], -1.0 / D, None, ALU.mult)\
                   .then_inc(S["ln_mean"], 1)

            def variance(i):
                dve.wait_ge(S["ln_ss"], at("ln_ss", n, i + 1))
                dve.tensor_scalar(var[:, i:i + 1], ss[:, i:i + 1], 1.0 / D, 4 * LN_EPS, ALU.mult, ALU.add)\
                   .then_inc(S["ln_var"], 1)

            def normalise(i):
                dve.wait_ge(S["ln_rstd"], at("ln_rstd", n, i + 1))
                dve.tensor_scalar(xh[:, i, :], r[:, i, :], mean[:, i:i + 1], rstd[:, i:i + 1], ALU.add,
                                  ALU.mult).then_inc(S["ln_xhat"], 1)

            residual(0)
            variance(0)
            normalise(0)
            residual(1)
            if gb:
                dve_gains(dve, turn, 0, *gb)
            variance(1)
            if gb:
                dve_rests(dve, turn, 0)
            normalise(1)
            if gb:
                dve_turn(dve, turn, 1, *gb)

        def act_layer_norm(act, n):
            for i in range(NT):
                act.wait_ge(S["ln_mean"], at("ln_mean", n, i + 1))
                act.activation(xh[:, i, :], r[:, i, :], ACT.Square, bias=mean[:, i:i + 1],
                               accum_out=ss[:, i:i + 1]).then_inc(S["ln_ss"], 1)

        def pool_layer_norm(pool, n):
            for i in range(NT):
                pool.wait_ge(S["ln_var"], at("ln_var", n, i + 1))
                pool.tensor_tensor(rstd[:, i:i + 1], var[:, i:i + 1], neg_half[:, 0:1], ALU.pow)\
                    .then_inc(S["ln_rstd"], 1)

        def pool_residual(pool, n):
            pool_hold(pool, S["rows"], at("rows", n))
            for i in range(NT):
                pool.wait_ge(S["ln_xhat"], xhat_done(n, i + 1))
                pool.tensor_tensor(x[:, i, :], xh[:, i, :], rows[:, 0, :], ALU.mult).then_inc(S["x_scaled"], 1)
            for i in range(NT):
                pool.wait_ge(S["x_scaled"], at("x_scaled", n, i + 1))
                pool.tensor_tensor(x[:, i, :], x[:, i, :], rows[:, 1, :], ALU.add).then_inc(S["x_ready"], 1)

        def w_cols(w, c0, n, k0=0, nk=KD):
            return w[k0 * P:(k0 + nk) * P, c0:c0 + n].rearrange("(k p) c -> p k c", p=P)

        def sp_mix1(sp, turn, w_in, wa, wb, wo):
            for j in range(4):
                load(sp, turn, j, w_cols(w_in, 512 + j * P, P), KD)
            for j in range(4):
                load(sp, turn, 4 + j, w_cols(w_in, j * P, P), KD)
            for k in range(KD):
                load(sp, turn, 8 + k, w_cols(w_in, 1024, 1024, k, 1), 1)
            for j in range(8):
                load(sp, turn, 16 + j, w_cols(w_in, 3072 + j * P, P), KD)
            for k in range(KD):
                load(sp, turn, 24 + k, w_cols(w_in, 2048, 1024, k, 1), 1)
            for j in range(8):
                load(sp, turn, 32 + j, w_cols(w_in, 4096 + j * P, P), KD)
            for j in range(8):
                load(sp, turn, 40 + j, w_cols(wa, j * P, P, 0, 4), 4)
            for j in range(4):
                load(sp, turn, 48 + j, w_cols(wb, j * 2 * P, 2 * P, 0, 4), 4)
            for k in range(KD):
                load(sp, turn, 52 + k, w_cols(wo, 0, 1024, k, 1), 1)

        def pe_mix1(pe, L, turn, xt):
            def project(c0, n, base):
                for j in range(n):
                    feature_unit(pe, turn, c0 + j, KD, xt_hi, xt_lo, [base[:, j, :]], 0, KD)

            pe.wait_ge(S["xt_lo_p"], at("xt_lo_p", xt))
            pe.wait_ge(S["xt_lo"], at("xt_lo", xt))
            project(0, 4, turned)
            project(4, 4, turned[:, 4:8, :])
            for k in range(KD):
                token_unit(pe, turn, 8 + k, xt_hi[:, k, :], xt_lo[:, k, :], acc, k == 0, k == KD - 1)

            def scores(n, size):
                o = bank[:, 2 * (n % 2):2 * (n % 2) + 2, :].rearrange("p b (c t) -> p (b c) t", c=4)
                if n == 0:
                    pe.wait_ge(S["zg_out"], at("zg_out", L))
                    pe.wait_ge(S["hg_qf"], at("hg_qf", L))
                if n >= 2:
                    pe.wait_ge(S["hg_sel"], at("hg_sel", L, SEL_AFTER[n - 2]))
                if n >= 2:
                    pe.wait_ge(S["hg_qp"], at("hg_qp", L, n - 1))
                    pe.wait_ge(S["hg_ks"], at("hg_ks", L, n - 1))
                qq = q if n == 0 else qp
                if size < P:
                    for h in range(H):
                        for a in range(NT):
                            mm = pe.matmul(o[:, 2 * h + a, :], ks[:, h, a * P:(a + 1) * P],
                                           qq[:, h, a * P:(a + 1) * P], start=True, stop=True)
                else:
                    for h in range(H):
                        mm = pe.matmul(o[:, h, :], ks[:, h, 0:P], qq[:, h, P:2 * P], start=True, stop=True)
                mm.then_inc(S["hg_scores"], 1)

            for j in range(8):
                if j == 0:
                    pe.wait_ge(S["hg_q"], at("hg_q", L))
                feature_unit(pe, turn, 16 + j, KD, xt_hi, xt_lo, [turned[:, j, :]], 0, KD)
                scores(j, LEVELS[j])
            scores(8, P)
            for k in range(KD):
                if k == 0:
                    pe.wait_ge(S["hg_sel"], at("hg_sel", L))
                token_unit(pe, turn, 24 + k, xt_hi[:, k, :], xt_lo[:, k, :], acc, k == 0, k == KD - 1)
                if k == 2:
                    pe.wait_ge(S["za_out"], at("za_out", L))
                    for h in range(H):
                        c = slice(h * P, (h + 1) * P)
                        pe.matmul(bank[:, 4, c], sc[:, 2 * h, :], zi[:, 0, c], start=True, stop=True)
                        pe.matmul(bank[:, 5, c], sc[:, 2 * h + 1, :], zi[:, 1, c], start=True, stop=False)
                        mm = pe.matmul(bank[:, 5, c], scx[:, h, :], zi[:, 0, c], start=False, stop=True)
                    mm.then_inc(S["hg_o"], 1)
                if k == 4:
                    pe.wait_ge(S["ws_in"], at("ws_in", L))
                    for g in range(H):
                        mm = pe.transpose(bank[:, 6, g * P:(g + 1) * P], ws_nat[:, g, :], ident)
                    mm.then_inc(S["ws_turned"], 1)
            for j in range(8):
                if j == 0:
                    pe.wait_ge(S["o_norm"], at("o_norm", L))
                    pe.wait_ge(S["ws_out"], at("ws_out", L))
                feature_unit(pe, turn, 32 + j, KD, xt_hi, xt_lo, [turned[:, j, :]], 0, KD)
                if j == 3:
                    pe.wait_ge(S["zuv_out"], at("zuv_out", L))
                    pe.wait_ge(S["o_gated"], at("o_gated", L))
                    for k in range(4):
                        for i in range(NT):
                            mm = pe.transpose(low8[:, 4 + k, i * P:(i + 1) * P], og[:, i, k * P:(k + 1) * P], ident)
                    mm.then_inc(S["o_turned"], 1)
                if j == 5:
                    pe.wait_ge(S["v_ready"], at("v_ready", L))
                    pe.wait_ge(S["ws_low"], at("ws_low", L))
                    for g in range(H):
                        mm = pe.matmul(low8[:, g, :].rearrange("p (i c) -> p i c", i=NT), ws_t[:, g, :],
                                       v_[:, :, g * P:(g + 1) * P], start=True, stop=True)
                    mm.then_inc(S["mixed"], 1)
            pe.wait_ge(S["ub"], at("ub", L))
            pe.wait_ge(S["o_lo"], at("o_lo", L))
            for k in range(4):
                for i in range(NT):
                    mm = pe.transpose(low8[:, 4 + k, i * P:(i + 1) * P], u_[:, i, k * P:(k + 1) * P], ident)
            mm.then_inc(S["ub_turned"], 1)
            pe.wait_ge(S["zb_out"], at("zb_out", L))
            for j in range(8):
                feature_unit(pe, turn, 40 + j, 4, mt_hi, mt_lo, [turned[:, j, :]], 0, 4)
            pe.wait_ge(S["ub_lo"], at("ub_lo", L))
            for j in range(4):
                feature_unit(pe, turn, 48 + j, 4, mt_hi[:, 4:8, :], mt_lo[:, 4:8, :],
                             [low8[:, 2 * j, :], low8[:, 2 * j + 1, :]], 0, 4)
            pe.wait_ge(S["yb"], at("yb", L))
            pe.wait_ge(S["y_lo"], at("y_lo", L, 1))
            for k in range(4):
                token_unit(pe, turn, 52 + k, xt_hi[:, k, :], xt_lo[:, k, :], acc, k == 0, False)
            token_units_by_tile(pe, turn, range(56, 60), [(xt_hi[:, k, :], xt_lo[:, k, :]) for k in range(4, 8)],
                                acc, {0: (S["y_lo"], at("y_lo", L, 2))})

        SEL_AFTER = [1, 2, 3, 4, 5, 6, 8, 9, 10]

        def act_mix1(act, L, turn):
            split_hi(act, turn, range(4, 10))
            act.wait_ge(S["weights_used"], used_after(turn, 3))
            act.activation(sig_f, turned[:, 0:4, :], ACT.Sigmoid).then_inc(S["hg_sig"], 1)
            act.activation(ks, turned[:, 0:4, :], ACT.Sigmoid, scale=-1.0).then_inc(S["hg_sig"], 1)
            split_hi(act, turn, range(10, 14))
            act.wait_ge(S["weights_used"], used_after(turn, 7))
            act.activation(q, turned[:, 4:8, :], ACT.Copy).then_inc(S["hg_q"], 1)
            split_hi(act, turn, range(14, 22))
            act.wait_ge(S["weights_used"], used_after(turn, 15))
            act.activation(zi, acc[:, :, 0:512], ACT.Copy).then_inc(S["zg_out"], 1)
            act.activation(gz, acc[:, :, 512:1024], ACT.Silu).then_inc(S["zg_out"], 1)
            split_hi(act, turn, range(22, 30))
            act.wait_ge(S["weights_used"], used_after(turn, 23))
            act.wait_ge(S["x_ready"], norm_done(3 * L))
            act.activation(ta, turned, ACT.Tanh, scale=0.5).then_inc(S["za_out"], 1)
            split_hi(act, turn, range(30, 33))
            act.wait_ge(S["hg_o"], at("hg_o", L))
            for h in range(H):
                for i in range(NT):
                    n = 2 * h + i
                    act.activation(sq_junk[:, n * P:(n + 1) * P], bank[:, 4 + i, h * P:(h + 1) * P], ACT.Square,
                                   accum_out=ss[:, i * H + h:i * H + h + 1]).then_inc(S["o_ss"], 1)
            split_hi(act, turn, range(33, 35))
            act.wait_ge(S["ws_turned"], at("ws_turned", L))
            act.activation(ws_t, bank[:, 6, :].rearrange("p (g t) -> p g t", g=H), ACT.Copy).then_inc(S["ws_out"], 1)
            split_hi(act, turn, range(35, 38))
            act.wait_ge(S["weights_used"], used_after(turn, 31))
            act.activation(v_, acc[:, :, 512:1024], ACT.Gelu_apprx_tanh).then_inc(S["zuv_out"], 1)
            act.activation(u_, acc[:, :, 0:512], ACT.Gelu_apprx_tanh).then_inc(S["zuv_out"], 1)
            split_hi(act, turn, range(38, 40))
            split_hi(act, turn, range(40, 42), 512)
            act.wait_ge(S["o_turned"], at("o_turned", L))
            act.activation(mt_hi[:, 0:4, :], low8[:, 4:8, :], ACT.Copy).then_inc(S["o_hi"], 1)
            split_hi(act, turn, range(42, 46), 512)
            act.wait_ge(S["weights_used"], used_after(turn, 39))
            act.activation(tb, turned, ACT.Tanh, scale=0.5).then_inc(S["zb_out"], 1)
            act.wait_ge(S["ub_turned"], at("ub_turned", L))
            act.activation(mt_hi[:, 4:8, :], low8[:, 4:8, :], ACT.Copy).then_inc(S["ub_hi"], 1)
            split_hi(act, turn, range(46, 48), 512)
            split_hi(act, turn, range(48, 56))
            for a in range(2):
                act.wait_ge(S["y_sum"], at("y_sum", L, a + 1))
                act.activation(xt_hi[:, 4 * a:4 * a + 4, :], y32[:, 4 * a:4 * a + 4, :], ACT.Copy)\
                   .then_inc(S["y_hi"], 1)
            split_hi(act, turn, range(56, 60))

        def dve_mix1(dve, L, turn):
            split_lo(dve, turn, range(4, 10))
            dve.wait_ge(S["rest_in"], 16 * 2)
            dve.wait_ge(S["now1"], at("now1", L))
            dve.wait_ge(S["hg_sig"], at("hg_sig", L))
            for h in range(H):
                dve.tensor_scalar(sig_f[:, h, :], sig_f[:, h, :], om_now[:, h:h + 1], lb_now[:, h:h + 1],
                                  ALU.mult, ALU.add).then_inc(S["hg_fk"], 1)
            for h in range(H):
                dve.tensor_scalar(ks[:, h, :], ks[:, h, :], om_now[:, h:h + 1], None, ALU.mult)\
                   .then_inc(S["hg_fk"], 1)
            split_lo(dve, turn, range(10, 14))
            dve.wait_ge(S["hg_q"], at("hg_q", L))
            dve.wait_ge(S["hg_fk"], at("hg_fk", L))
            dve.tensor_tensor(qp, q, sig_f, ALU.mult).then_inc(S["hg_qf"], 1)
            split_lo(dve, turn, range(14, 22))
            dve.wait_ge(S["mixrows1"], at("mixrows1", L))
            dve.wait_ge(S["zg_out"], at("zg_out", L))
            dve.tensor_tensor(gz, gz, rows[:, 0, 0:512].unsqueeze(1).broadcast_to([P, NT, 512]), ALU.mult)\
               .then_inc(S["hg_gain"], 1)

            qpf, ksf = (a.rearrange("p h t -> p (h t)") for a in (qp, ks))
            block_total = [sig_f.rearrange("p h t -> p (h t)")]
            at_ = 0
            for n in range(1, 8):
                size = 1024 >> n
                block_total.append(tot[:, at_:at_ + size])
                at_ += size
            selected = 0
            for n in range(9):
                size = LEVELS[n] if n < 8 else P
                o = bank[:, 2 * (n % 2):2 * (n % 2) + 2, :].rearrange("p b (c t) -> p (b c) t", c=4)
                dve_hold(dve, S["hg_scores"], at("hg_scores", L, n + 1))
                if 1 <= n < 8:
                    if n > 1:
                        dve.wait_ge(S["hg_t"], at("hg_t", L, n - 1))
                    b, nb = size, 1024 // (2 * size)
                    t2 = block_total[n - 1].rearrange("p (n two) -> p n two", two=2)
                    qv = qpf.rearrange("p (n two b) -> p n two b", two=2, b=b)
                    kv = ksf.rearrange("p (n two b) -> p n two b", two=2, b=b)
                    dve.tensor_tensor(qv[:, :, 1, :], qv[:, :, 1, :],
                                      t2[:, :, 0:1].broadcast_to([P, nb, b]), ALU.mult).then_inc(S["hg_qp"], 1)
                    dve.tensor_tensor(kv[:, :, 0, :], kv[:, :, 0, :],
                                      t2[:, :, 1:2].broadcast_to([P, nb, b]), ALU.mult).then_inc(S["hg_ks"], 1)
                    dve.tensor_tensor(block_total[n], t2[:, :, 0], t2[:, :, 1], ALU.mult).then_inc(S["hg_t"], 1)
                if selected and n < 8:
                    dve_hold(dve, S["hg_sel"], at("hg_sel", L, selected))
                if n == 0:
                    dve.tensor_tensor(sc, o, hg_mask[:, 0:1, :].broadcast_to([P, 8, P]), ALU.mult)\
                       .then_inc(S["hg_sel"], 1)
                elif size <= 16:
                    dve.copy_predicated(sc, hg_mask[:, n:n + 1, :].bitcast(I32).broadcast_to([P, 8, P]), o)\
                       .then_inc(S["hg_sel"], 1)
                elif size == 32:
                    for s in (0, 64):
                        dve.tensor_copy(sc[s:s + 32, :, s + 32:s + 64], o[s:s + 32, :, s + 32:s + 64])\
                           .then_inc(S["hg_sel"], 1)
                elif size == 64:
                    dve.tensor_copy(sc[0:64, :, 64:128], o[0:64, :, 64:128]).then_inc(S["hg_sel"], 1)
                else:
                    dve.tensor_copy(scx, o[:, 0:4, :]).then_inc(S["hg_sel"], 1)
                selected = SEL_AFTER[n]
                if n < 8:
                    split_lo(dve, turn, [22 + n])
            split_lo(dve, turn, range(30, 33))
            dve.wait_ge(S["o_ss"], at("o_ss", L))
            dve.tensor_scalar(var[:, 0:8], ss[:, 0:8], 1.0 / P, RMS_EPS, ALU.mult, ALU.add).then_inc(S["o_var"], 1)
            split_lo(dve, turn, range(33, 34))
            dve.wait_ge(S["o_rstd"], at("o_rstd", L))
            o = bank[:, 4:6, :].rearrange("p i (h v) -> p (i h) v", h=H)
            dve.tensor_tensor(og.rearrange("p i (h v) -> p (i h) v", h=H), o,
                              rstd[:, 0:8].unsqueeze(2).broadcast_to([P, 8, P]), ALU.mult).then_inc(S["o_norm"], 1)
            dve.wait_ge(S["o_norm"], at("o_norm", L))
            dve.wait_ge(S["hg_gain"], at("hg_gain", L))
            dve.tensor_tensor(og, og, gz, ALU.mult).then_inc(S["o_gated"], 1)
            split_lo(dve, turn, range(34, 38))
            dve.wait_ge(S["zuv_out"], at("zuv_out", L, 1))
            for i in range(NT):
                dve.bn_stats(stats[:, i, 0, :], v_[:, i, :]).then_inc(S["v_stats"], 1)
            for i in range(NT):
                dve_hold(dve, S["v_stats"], at("v_stats", L, i + 1))
                dve.bn_aggr(mv_[:, i, :], stats[:, i, 0, :]).then_inc(S["v_aggr"], 1)
            dve.wait_ge(S["v_aggr"], at("v_aggr", L))
            dve.tensor_scalar(var[:, 0:2], mv_[:, :, 1], LN_EPS, None, ALU.add).then_inc(S["v_var"], 1)
            split_lo(dve, turn, range(38, 39))
            dve.wait_ge(S["v_rstd"], at("v_rstd", L))
            for i in range(NT):
                dve.tensor_scalar(v_[:, i, :], v_[:, i, :], mv_[:, i, 0:1], rstd[:, i:i + 1], ALU.subtract,
                                  ALU.mult).then_inc(S["v_hat"], 1)
            dve.wait_ge(S["v_hat"], at("v_hat", L))
            dve.tensor_tensor(v_, v_, rows[:, 0, 512:1024].unsqueeze(1).broadcast_to([P, NT, 512]), ALU.mult)\
               .then_inc(S["v_scaled"], 1)
            dve.wait_ge(S["v_scaled"], at("v_scaled", L))
            dve.tensor_tensor(v_, v_, rows[:, 1, 0:512].unsqueeze(1).broadcast_to([P, NT, 512]), ALU.add)\
               .then_inc(S["v_ready"], 1)
            split_lo(dve, turn, range(39, 40))
            split_lo(dve, turn, range(40, 42), 512)
            dve.wait_ge(S["o_hi"], at("o_hi", L))
            dve.tensor_tensor(mt_lo[:, 0:4, :], low8[:, 4:8, :], f32(mt_hi[:, 0:4, :]), ALU.subtract)\
               .then_inc(S["o_lo"], 1)
            split_lo(dve, turn, range(42, 44), 512)
            dve.wait_ge(S["mixed"], at("mixed", L))
            dve.wait_ge(S["zuv_out"], at("zuv_out", L))
            for g in range(H):
                c = slice(g * P, (g + 1) * P)
                dve.scalar_tensor_tensor(u_[:, :, c], low8[:, g, :].rearrange("p (i c) -> p i c", i=NT),
                                         sgb_now[:, g:g + 1], u_[:, :, c], ALU.add, ALU.mult).then_inc(S["ub"], 1)
            split_lo(dve, turn, range(44, 46), 512)
            dve.wait_ge(S["ub_hi"], at("ub_hi", L))
            dve.tensor_tensor(mt_lo[:, 4:8, :], low8[:, 4:8, :], f32(mt_hi[:, 4:8, :]), ALU.subtract)\
               .then_inc(S["ub_lo"], 1)
            split_lo(dve, turn, range(46, 48), 512)
            split_lo(dve, turn, range(48, 54))
            dve.wait_ge(S["weights_used"], used_after(turn, 47))
            dve.wait_ge(S["zb_out"], at("zb_out", L))
            dve.scalar_tensor_tensor(ta, ta, 1.0, turned, ALU.add, ALU.mult).then_inc(S["ya"], 1)
            split_lo(dve, turn, range(54, 56))
            dve.wait_ge(S["ya"], at("ya", L))
            def y_b(a):
                c = slice(4 * a, 4 * a + 4)
                dve.wait_ge(S["weights_used"], used_after(turn, 49 + 2 * a))
                dve.scalar_tensor_tensor(tb[:, c, :], tb[:, c, :], 1.0, low8[:, c, :], ALU.add, ALU.mult)\
                   .then_inc(S["yb"], 1)

            def y_sum(a):
                c = slice(4 * a, 4 * a + 4)
                dve.wait_ge(S["yb"], at("yb", L, a + 1))
                dve.tensor_tensor(y32[:, c, :], ta[:, c, :], tb[:, c, :], ALU.add).then_inc(S["y_sum"], 1)

            def y_rest(a):
                c = slice(4 * a, 4 * a + 4)
                dve.wait_ge(S["y_hi"], at("y_hi", L, a + 1))
                dve.tensor_tensor(xt_lo[:, c, :], y32[:, c, :], f32(xt_hi[:, c, :]), ALU.subtract)\
                   .then_inc(S["y_lo"], 1)

            y_b(0)
            y_sum(0)
            y_b(1)
            y_rest(0)
            y_sum(1)
            y_rest(1)
            split_lo(dve, turn, range(56, 60))

        def pool_mix1(pool, L):
            pool_hold(pool, S["x_ready"], norm_done(3 * L))
            for src, dst in ((A["hg_norm_g"], rows[:, 0, 0:512]), (A["sg_ln_g"], rows[:, 0, 512:1024]),
                             (A["sg_ln_b"], rows[:, 1, 0:512])):
                pool.dma_start(dst, src[bass.ds(L, 1), :].rearrange("a n -> (a n)").partition_broadcast(P))\
                    .then_inc(S["mixrows1"], 16)
            pool.dma_start(ws_nat, A["sg_ws"][bass.ds(L, 1), :, :, :].rearrange("l g t s -> t (l g) s"))\
                .then_inc(S["ws_in"], 16)
            pool.wait_ge(S["o_var"], at("o_var", L))
            pool.tensor_tensor(rstd[:, 0:8], var[:, 0:8], neg_half[:, :], ALU.pow).then_inc(S["o_rstd"], 1)
            pool_hold(pool, S["ws_out"], at("ws_out", L))
            for g in range(H):
                pool.affine_select(ws_t[:, g, :], ws_t[:, g, :], [[1, P]], ALU.is_ge, 0.0, base=0,
                                   channel_multiplier=-1).then_inc(S["ws_low"], 1)
            pool.wait_ge(S["v_var"], at("v_var", L))
            pool.tensor_tensor(rstd[:, 0:2], var[:, 0:2], neg_half[:, 0:2], ALU.pow).then_inc(S["v_rstd"], 1)
            pool_hold(pool, S["v_ready"], at("v_ready", L))

        def load_ln_rows(pool, L, j):
            for g, src in enumerate((A["ln_g"], A["ln_b"])):
                pool.dma_start(rows[:, g, :], src[bass.ds(L, 1), j, :].rearrange("a n -> (a n)")
                               .partition_broadcast(P)).then_inc(S["rows"], 16)

        def act_pre(act, n, before, i):
            act.wait_ge(S["x_ready"], norm_done(before, i + 1))
            act.activation(xh[:, i, :], x[:, i, :], ACT.Square, accum_out=ss[:, 4 + i:5 + i])\
               .then_inc(S["pre_ss"], 1)

        def dve_pre_var(dve, n, i):
            dve.wait_ge(S["pre_ss"], at("pre_ss", n, i + 1))
            dve.tensor_scalar(var[:, 2 + i:3 + i], ss[:, 4 + i:5 + i], 1.0 / D, NORM_EPS, ALU.mult, ALU.add)\
               .then_inc(S["pre_var"], 1)

        def dve_pre_xhat(dve, n, i):
            dve.wait_ge(S["pre_rstd"], at("pre_rstd", n, i + 1))
            dve.tensor_scalar(xh[:, i, :], x[:, i, :], rstd[:, 2 + i:3 + i], None, ALU.mult)\
               .then_inc(S["pre_xhat"], 1)

        def dve_pre(dve, n, g):
            dve_pre_var(dve, n, 0)
            dve_pre_var(dve, n, 1)
            dve_pre_xhat(dve, n, 0)
            dve_pre_xhat(dve, n, 1)
            for i in range(NT):
                dve_turn(dve, n + 3 * DEPTH, i, g, None)

        def pool_pre(pool, n, i):
            pool.wait_ge(S["pre_var"], at("pre_var", n, i + 1))
            pool.tensor_tensor(rstd[:, 2 + i:3 + i], var[:, 2 + i:3 + i], neg_half[:, 0:1], ALU.pow)\
                .then_inc(S["pre_rstd"], 1)

        def act_post(act, n, i, out_at):
            if i == 0:
                act.wait_ge(S["tile0_out"], at("tile0_out", n + 3 * DEPTH))
            else:
                act.wait_ge(S["weights_used"], out_at)
            for b in range(2):
                if b:
                    act.wait_ge(S["post_scaled"], at("post_scaled", n, 2 * i + 1))
                act.activation(xh[:, i, b * 512:(b + 1) * 512], acc[:, i, b * 512:(b + 1) * 512], ACT.Square,
                               accum_out=ss[:, 2 * i + b:2 * i + b + 1]).then_inc(S["post_ss"], 1)

        def dve_post_scale(dve, n, i, factor, out_at):
            if i == 0:
                dve.wait_ge(S["tile0_out"], at("tile0_out", n + 3 * DEPTH))
                dve.wait_ge(S["rows"], n * 16 + (3 * DEPTH * PER["rows"] + 16))
            else:
                dve.wait_ge(S["weights_used"], out_at)
            for b in (1, 0):
                if b == 0:
                    dve.wait_ge(S["post_ss"], at("post_ss", n, 2 * i + 1))
                c = slice(b * 512, (b + 1) * 512)
                dve.tensor_tensor(r[:, i, c], acc[:, i, c], rows[:, 0, c], ALU.mult).then_inc(S["post_scaled"], 1)
            dve.wait_ge(S["post_ss"], at("post_ss", n, 2 * i + 2))
            dve.tensor_tensor(ss[:, 2 * i:2 * i + 1], ss[:, 2 * i:2 * i + 1], ss[:, 2 * i + 1:2 * i + 2], ALU.add)\
               .then_inc(S["post_sum"], 1)
            dve.wait_ge(S["post_sum"], at("post_sum", n, i + 1))
            dve.tensor_scalar(var[:, i:i + 1], ss[:, 2 * i:2 * i + 1], factor ** -2 / D, factor ** -2 * NORM_EPS,
                              ALU.mult, ALU.add).then_inc(S["post_var"], 1)

        def dve_post_add(dve, n, i):
            dve.wait_ge(S["post_scaled"], at("post_scaled", n, 2 * i + 2))
            dve.wait_ge(S["post_rstd"], at("post_rstd", n, i + 1))
            dve.scalar_tensor_tensor(x[:, i, :], r[:, i, :], rstd[:, i:i + 1], x[:, i, :], ALU.mult, ALU.add)\
               .then_inc(S["x_ready"], 1)

        def pool_post(pool, n, i):
            pool.wait_ge(S["post_var"], at("post_var", n, i + 1))
            pool.tensor_tensor(rstd[:, i:i + 1], var[:, i:i + 1], neg_half[:, 0:1], ALU.pow)\
                .then_inc(S["post_rstd"], 1)

        def dve_post_pre(dve, n, factor, out_at, g):
            dve_post_scale(dve, n, 0, factor, out_at)
            dve_post_add(dve, n, 0)
            dve_post_scale(dve, n, 1, factor, out_at)
            dve_pre_var(dve, n + 1, 0)
            dve_post_add(dve, n, 1)
            dve_pre_xhat(dve, n + 1, 0)
            dve_pre_var(dve, n + 1, 1)
            dve_pre_xhat(dve, n + 1, 1)
            for i in range(NT):
                dve_turn(dve, n + 1 + 3 * DEPTH, i, g, None)

        def act_post_pre(act, n, before, out_at, g):
            act_post(act, n, 0, out_at)
            act_post(act, n, 1, out_at)
            act_pre(act, n + 1, before, 0)
            act_pre(act, n + 1, before, 1)
            act_turn_both(act, n + 1 + 3 * DEPTH, g, None)

        def pool_post_pre(pool, n):
            pool_post(pool, n, 0)
            pool_post(pool, n, 1)
            pool_pre(pool, n + 1, 0)
            pool_pre(pool, n + 1, 1)
            pool_turn(pool, n + 1 + 3 * DEPTH)

        def load_post_row(pool, L, j):
            pool.dma_start(rows[:, 0, :], A["norm_gain_2"][bass.ds(L, 1), j, :].rearrange("a n -> (a n)")
                           .partition_broadcast(P)).then_inc(S["rows"], 16)

        def sp_mix2(sp, turn, w, wo):
            for j in range(8):
                load(sp, turn, j, w_cols(w, 1536 + j * P, P), KD)
            for k in range(KD):
                load(sp, turn, 8 + k, w_cols(w, 2560, 1024, k, 1), 1)
            for k in range(KD):
                load(sp, turn, 16 + k, w_cols(w, 0, 1024, k, 1), 1)
            for k in range(4):
                load(sp, turn, 24 + k, w_cols(w, 1024, 512, 2 * k, 2), 2)
            for k in range(KD):
                load(sp, turn, 28 + k, w_cols(wo, 0, 1024, k, 1), 1)

        g_bank = bank[:, 0, T:T + 2 * NG].rearrange("p (i g) -> p i g", i=NT)
        g_feat = hidden_flat[0:NG, 768:768 + T]
        m_s = bank[:, 0, :].rearrange("p (s t) -> p s t", s=NT)
        m_bc = bank[:, 1, :].rearrange("p (d t) -> p d t", d=2)

        def m_cols(d, s):
            if d == 0:
                return (0, 256, 0) if s == 0 else (128, 256, 256)
            return (0, 128, 0) if s == 0 else (0, 256, 128)

        def pe_mix2(pe, L, turn, xt):
            pe.wait_ge(S["wg_lo"], at("wg_lo", L))
            pe.wait_ge(S["xt_lo_p"], at("xt_lo_p", xt))
            pe_hold(pe, S["xt_lo"], at("xt_lo", xt))
            for k in range(KD):
                mm = by_feature(pe, bank[0:NG, 0, 0:T], wg_hi[:, k, :], wg_lo[:, k, :], xt_hi[:, k, :],
                                xt_lo[:, k, :], k == 0, k == KD - 1)
            mm.then_inc(S["gates"], 1)
            for j in range(8):
                feature_unit(pe, turn, j, KD, xt_hi, xt_lo, [turned[:, j, :]], 0, KD)
                if j == 0:
                    pe_hold(pe, S["gates_out"], at("gates_out", L))
                    for i in range(NT):
                        mm = pe.transpose(g_bank[:, i, :], g_feat[:, i * P:(i + 1) * P], ident[0:NG, 0:NG])
                    mm.then_inc(S["gates_turned"], 1)
                if j == 3:
                    pe.wait_ge(S["g_logf"], at("g_logf", L))
                    for m, src in enumerate((g_i, g_lf)):
                        for i in range(NT):
                            mm = pe.transpose(bank[0:8, 1, m * T + i * P:m * T + (i + 1) * P], src[:, i, :], ident)
                    mm.then_inc(S["g_turned"], 1)
            for k in range(KD):
                if k == 0:
                    pe.wait_ge(S["g_rows"], at("g_rows", L))
                token_unit(pe, turn, 8 + k, xt_hi[:, k, :], xt_lo[:, k, :], acc, k == 0, k == KD - 1)
                if k == 4:
                    pe.wait_ge(S["mqk_out"], at("mqk_out", L))
                    pe_hold(pe, S["g_nm"], at("g_nm", L))
                    for m, which in enumerate((GA, GNM)):
                        for d in range(2):
                            for i in range(NT):
                                at_ = ((m * 2 + d) * 2 + i) * 8
                                mm = pe.transpose(bank[:, 4, at_:at_ + 8], grow[:, which[d], i * P:(i + 1) * P],
                                                  ident[0:8, 0:8])
                    mm.then_inc(S["g_cols_turned"], 1)

            def m_pair(h):
                if h == 0:
                    pe.wait_ge(S["rest_in"], 16 * 2)
                    pe.wait_ge(S["mo_out"], at("mo_out", L))
                    pe.wait_ge(S["k_scaled"], at("k_scaled", L))
                else:
                    pe_hold(pe, S["m_p"], at("m_p", L, 4 * h))
                for s in range(NT):
                    pe.matmul(m_s[:, s, :], conv_y[:, 4 + h, s * P:(s + 1) * P], conv_y[:, h, :],
                              start=True, stop=True)
                for d in range(2):
                    mm = pe.matmul(m_bc[:, d, :], sel[:, d * H + h, :], grow[:, GNEG[d], :], start=True, stop=True)
                mm.then_inc(S["m_scores"], 1)

            def m_out(h):
                for d in range(2):
                    pe.wait_ge(S["m_p"], at("m_p", L, 4 * h + 2 * d + 2))
                    if h:
                        pe.wait_ge(S["m_cell"], at("m_cell", L, 2 * h))
                    else:
                        pe.wait_ge(S["margins"], at("margins", L))
                    for i in range(NT):
                        o = bank[:, 2 + d, i * 129:(i + 1) * 129]
                        ss_ = [s for s in range(NT) if (s <= i if d == 0 else s >= i)]
                        for s in ss_:
                            c0, c1, p0 = m_cols(d, s)
                            lhs = m_pt[:, d, p0 + i * P - c0:p0 + (i + 1) * P - c0]
                            mm = pe.matmul(o, lhs, va[:, s, h, :], start=s == ss_[0], stop=s == ss_[-1])
                    mm.then_inc(S["m_num"], 1)

            for k in range(KD):
                if k == 0:
                    pe.wait_ge(S["g_cols"], at("g_cols", L))
                token_unit(pe, turn, 16 + k, xt_hi[:, k, :], xt_lo[:, k, :],
                           bank[:, 4:8, :].rearrange("p (t b) n -> p t (b n)", t=NT), k == 0, k == KD - 1)
                if k == 1:
                    m_pair(0)
                elif k in (2, 4, 6):
                    m_out(k // 2 - 1)
                    m_pair(k // 2)
            m_out(H - 1)
            pe_hold(pe, S["m_p"], at("m_p", L))
            for k in range(4):
                hi, lo = unit(pe, turn, 24 + k)
                for i in range(NT):
                    for kk in range(2):
                        kt = 2 * k + kk
                        mm = by_token(pe, bank[:, i, :], hi[:, kk * 512:(kk + 1) * 512],
                                      lo[:, kk * 512:(kk + 1) * 512], xt_hi[:, kt, i * P:(i + 1) * P],
                                      xt_lo[:, kt, i * P:(i + 1) * P], kt == 0, kt == KD - 1)
                mm.then_inc(S["weights_used"], 1)
            pe.wait_ge(S["rot"], at("rot", L))
            for k in range(KD):
                for i in range(NT):
                    mm = pe.transpose(turned[:, k, i * P:(i + 1) * P], aqk[:, i, k * P:(k + 1) * P], ident)
            mm.then_inc(S["a_turned"], 1)

            def a_scores(h):
                if h == 0:
                    pe.wait_ge(S["m_cell"], at("m_cell", L))
                    pe.wait_ge(S["a_t_out"], at("a_t_out", L))
                    pe.wait_ge(S["av_out"], at("av_out", L))
                if h >= 2:
                    pe.wait_ge(S["a_masked"], at("a_masked", L, 2 * (h - 1)))
                p0 = 64 * (h % 2)
                for i in range(NT):
                    mm = pe.matmul(bank[:, 4 + h % 2, i * T:(i + 1) * T],
                                   aqk_t[p0:p0 + 64, h // 2, i * P:(i + 1) * P],
                                   aqk_t[p0:p0 + 64, 4 + h // 2, :], start=True, stop=True)
                mm.then_inc(S["a_scores"], 1)

            def a_turn(h):
                pe.wait_ge(S["a_exp"], at("a_exp", L, 2 * h + 2))
                if h >= 2:
                    pe.wait_ge(S["a_p_out"], at("a_p_out", L, h - 1))
                for j in range(NT):
                    for i in range(NT):
                        mm = pe.transpose(bank[:, 6 + h % 2, j * T + i * P:j * T + (i + 1) * P],
                                          a_p[:, h % 2, i, j * P:(j + 1) * P], ident)
                mm.then_inc(S["a_p_turned"], 1)

            def a_values(h):
                pe.wait_ge(S["a_p_out"], at("a_p_out", L, h + 1))
                for i in range(NT):
                    for j in range(NT):
                        mm = pe.matmul(bank[:, 2 + i, h * DH:(h + 1) * DH], a_pt[:, h % 2, j, i * P:(i + 1) * P],
                                       av[:, j, h * DH:(h + 1) * DH], start=j == 0, stop=j == NT - 1)
                mm.then_inc(S["a_o"], 1)

            for h in range(AH + 2):
                if h < AH:
                    a_scores(h)
                if 1 <= h <= AH:
                    a_turn(h - 1)
                if h >= 2:
                    a_values(h - 2)
            pe.wait_ge(S["a_out"], at("a_out", L))
            pe.wait_ge(S["m_out"], at("m_out", L))
            for k in range(KD):
                src = a_out if k < 4 else mlout
                for i in range(NT):
                    mm = pe.transpose(turned[:, k, i * P:(i + 1) * P], src[:, i, (k % 4) * P:(k % 4 + 1) * P], ident)
            mm.then_inc(S["merged_turned"], 1)
            pe.wait_ge(S["m_lo"], at("m_lo", L, 1))
            for k in range(4):
                token_unit(pe, turn, 28 + k, xt_hi[:, k, :], xt_lo[:, k, :], acc, k == 0, False)
            token_units_by_tile(pe, turn, range(32, 36), [(xt_hi[:, k, :], xt_lo[:, k, :]) for k in range(4, 8)],
                                acc, {0: (S["m_lo"], at("m_lo", L, 2))})

        GI, GLF = 0, 1
        GCUM, GA, GNEG = (2, 3), (4, 5), (6, 7)
        GNM = GCUM

        def act_mix2(act, L, turn):
            act.wait_ge(S["wg_in"], at("wg_in", L))
            act.activation(wg_hi[:, :, :], wg32[:, :, :], ACT.Copy).then_inc(S["wg_hi"], 1)
            act.wait_ge(S["gates"], at("gates", L))
            act.activation(g_feat, bank[0:NG, 0, 0:T], ACT.Copy).then_inc(S["gates_out"], 1)
            split_hi(act, turn, range(4, 6))
            act.wait_ge(S["g_min"], at("g_min", L))
            act.activation(g_n, g_n, ACT.Exp).then_inc(S["g_exp"], 1)
            act.wait_ge(S["g_exp"], at("g_exp", L))
            act.activation(g_n, g_n, ACT.Ln, bias=1.0).then_inc(S["g_ln"], 1)
            split_hi(act, turn, range(6, 14))
            act.wait_ge(S["weights_used"], used_after(turn, 7))
            act.activation(xp[:, :, 2:2 + T], turned, ACT.Copy).then_inc(S["mqk_out"], 1)
            split_hi(act, turn, range(14, 22))
            act.wait_ge(S["g_cols_turned"], at("g_cols_turned", L))
            act.activation(g_cols, bank[:, 4, 0:64].rearrange("p (m d i r) -> p m d i r", m=2, d=2, i=NT), ACT.Copy)\
               .then_inc(S["g_cols"], 1)
            act.wait_ge(S["weights_used"], used_after(turn, 15))
            act.activation(va[:, :, :, 0:P], acc[:, :, 0:512].rearrange("p i (h e) -> p i h e", h=H), ACT.Copy)\
               .then_inc(S["mo_out"], 1)
            act.activation(gm, acc[:, :, 512:1024], ACT.Tanh, scale=0.5).then_inc(S["mo_out"], 1)
            act.wait_ge(S["conv"], at("conv", L))
            act.activation(conv_y[:, :, :], conv_y[:, :, :], ACT.Silu).then_inc(S["conv_silu"], 1)
            act.wait_ge(S["g_cols"], at("g_cols", L))
            act.activation(g_em, g_cols[:, 1], ACT.Exp).then_inc(S["g_em"], 1)
            for h in range(H):
                for d in range(2):
                    act.wait_ge(S["m_arg"], at("m_arg", L, 4 * h + 2 * d + 2))
                    act.activation(m_w[:, d, :], m_e[:, d, :], ACT.Exp).then_inc(S["m_exp"], 1)
                split_hi(act, turn, [22 + 2 * h, 23 + 2 * h])
            act.wait_ge(S["m_cell"], at("m_cell", L))
            for i in range(NT):
                for h in range(H):
                    n = i * H + h
                    act.activation(m_e[:, 0, 0:P] if n % 2 else m_e[:, 0, P:2 * P], cell[:, i, h * P:(h + 1) * P],
                                   ACT.Square, accum_out=ss[:, n:n + 1]).then_inc(S["m_ss"], 1)
                    act.wait_ge(S["m_ss"], at("m_ss", L, n + 1))
            act.wait_ge(S["weights_used"], used_after(turn, 23))
            act.activation(aqk[:, :, :], bank[:, 4:8, :].rearrange("p (t b) n -> p t (b n)", t=NT), ACT.Copy)\
               .then_inc(S["aqk_out"], 1)
            split_hi(act, turn, range(30, 34))
            act.wait_ge(S["weights_used"], used_after(turn, 27))
            act.activation(av, bank[:, 0:2, :], ACT.Copy).then_inc(S["av_out"], 1)
            act.wait_ge(S["a_turned"], at("a_turned", L))
            act.activation(aqk_t, turned, ACT.Copy).then_inc(S["a_t_out"], 1)
            for h in range(AH + 1):
                if h < AH:
                    for i in range(NT):
                        act.wait_ge(S["a_masked"], at("a_masked", L, 2 * h + i + 1))
                        if h >= 2:
                            act.wait_ge(S["a_p_turned"], at("a_p_turned", L, h - 1))
                        act.activation(a_p[:, h % 2, i, :], a_s[:, h % 2, i, :], ACT.Exp, scale=-1.0,
                                       bias=a_mx[:, h, i:i + 1], accum_out=a_sum[:, h, i:i + 1])\
                           .then_inc(S["a_exp"], 1)
                if h >= 1:
                    act.wait_ge(S["a_p_turned"], at("a_p_turned", L, h))
                    if h >= 3:
                        act.wait_ge(S["a_o"], at("a_o", L, h - 2))
                    act.activation(a_pt[:, (h - 1) % 2], bank[:, 6 + (h - 1) % 2, :]
                                   .rearrange("p (j i) -> p j i", j=NT), ACT.Copy).then_inc(S["a_p_out"], 1)
            act.wait_ge(S["merged_turned"], at("merged_turned", L))
            for a in range(2):
                act.activation(xt_hi[:, 4 * a:4 * a + 4, :], turned[:, 4 * a:4 * a + 4, :], ACT.Copy)\
                   .then_inc(S["m_hi"], 1)
            split_hi(act, turn, range(34, 36))

        def dve_mix2(dve, L, turn):
            dve.wait_ge(S["wg_hi"], at("wg_hi", L))
            dve.tensor_tensor(wg_lo[:, :, :], wg32[:, :, :], f32(wg_hi[:, :, :]), ALU.subtract).then_inc(S["wg_lo"], 1)
            split_lo(dve, turn, range(4, 6))
            dve.wait_ge(S["mixrows2"], at("mixrows2", L))
            dve.wait_ge(S["gates_turned"], at("gates_turned", L))
            gb = g_bank.rearrange("p i (d g r) -> p i d g r", d=2, g=2)
            bias = rows[:, 1, 512:512 + NG].rearrange("p (d g r) -> p d g r", d=2, g=2)
            for g, dst in enumerate((g_i, g_f)):
                for i in range(NT):
                    ins = dve.tensor_tensor(dst[:, i, :].rearrange("p (d r) -> p d r", d=2), gb[:, i, :, g, :],
                                            bias[:, :, g, :], ALU.add)
                ins.then_inc(S["g_biased"], 1)
            dve.wait_ge(S["g_biased"], at("g_biased", L))
            dve.scalar_tensor_tensor(g_n, g_f, -1.0, g_f, ALU.mult, ALU.min).then_inc(S["g_min"], 1)
            dve.tensor_scalar(g_lf, g_f, 0.0, None, ALU.min).then_inc(S["g_min"], 1)
            dve.wait_ge(S["g_min"], at("g_min", L))
            dve.wait_ge(S["g_ln"], at("g_ln", L))
            dve.tensor_tensor(g_lf, g_lf, g_n, ALU.subtract).then_inc(S["g_logf"], 1)
            split_lo(dve, turn, range(6, 10))
            dve.wait_ge(S["g_turned"], at("g_turned", L))
            dve.tensor_copy(grow[:, 0:2, :], bank[0:8, 1, :].rearrange("p (m t) -> p m t", m=2)).then_inc(S["g_rows"], 1)
            dve.wait_ge(S["g_rows"], at("g_rows", L))
            lf = grow[:, GLF, :]
            rev = (slice(None), slice(None, None, -1))
            dve.tensor_tensor_scan(grow[:, GCUM[0], :], ones8[:, :], lf, 0.0, ALU.mult, ALU.add).then_inc(S["g_cum"], 1)
            dve.tensor_tensor_scan(grow[:, GCUM[1], :][rev], ones8[:, :], lf[rev], 0.0, ALU.mult, ALU.add)\
               .then_inc(S["g_cum"], 1)
            for d in range(2):
                dve.wait_ge(S["g_cum"], at("g_cum", L, d + 1))
                dve.tensor_tensor(grow[:, GA[d], :], grow[:, GI, :], grow[:, GCUM[d], :], ALU.subtract)\
                   .then_inc(S["g_a"], 1)
            for d in range(2):
                o, a = grow[:, GNEG[d], :], grow[:, GA[d], :]
                if d:
                    o, a = o[rev], a[rev]
                dve.wait_ge(S["g_a"], at("g_a", L, d + 1))
                dve.tensor_tensor_scan(o, ones8[:, :], a, -1e30, ALU.mult, ALU.max).then_inc(S["g_max"], 1)
            for d in range(2):
                dve.wait_ge(S["g_max"], at("g_max", L, d + 1))
                dve.tensor_scalar(grow[:, GNEG[d], :], grow[:, GNEG[d], :], -1.0, None, ALU.mult).then_inc(S["g_neg"], 1)
            for d in range(2):
                dve.wait_ge(S["g_neg"], at("g_neg", L, d + 1))
                dve.tensor_tensor(grow[:, GNM[d], :], grow[:, GNEG[d], :], grow[:, GCUM[d], :], ALU.subtract)\
                   .then_inc(S["g_nm"], 1)
            split_lo(dve, turn, range(10, 14))
            dve.wait_ge(S["mqk_out"], at("mqk_out", L))
            dve.wait_ge(S["now2"], at("now2", L))
            dve.wait_ge(S["margins"], at("margins", L))
            for tap in range(CONV):
                for k in range(KD):
                    if tap == 0:
                        dve.tensor_scalar(conv_y[:, k, :], xp[:, k, 0:T], conv_now[:, 0, k:k + 1],
                                          conv_now[:, CONV, k:k + 1], ALU.mult, ALU.add).then_inc(S["conv"], 1)
                    else:
                        dve.wait_ge(S["conv"], at("conv", L, 8 * (tap - 1) + k + 1))
                        dve.scalar_tensor_tensor(conv_y[:, k, :], xp[:, k, tap:tap + T], conv_now[:, tap, k:k + 1],
                                                 conv_y[:, k, :], ALU.mult, ALU.add).then_inc(S["conv"], 1)
                split_lo(dve, turn, [14 + tap])
            split_lo(dve, turn, range(19, 22))
            dve.wait_ge(S["conv_silu"], at("conv_silu", L))
            dve.tensor_scalar(conv_y[:, 4:8, :], conv_y[:, 4:8, :], float(P) ** -0.5, None, ALU.mult)\
               .then_inc(S["k_scaled"], 1)
            dve.wait_ge(S["mo_out"], at("mo_out", L))
            dve.scalar_tensor_tensor(gm, gm, 1.0, rows[:, 1, 0:512].unsqueeze(1).broadcast_to([P, NT, 512]),
                                     ALU.add, ALU.mult).then_inc(S["mo_gain"], 1)
            dve.wait_ge(S["g_em"], at("g_em", L))
            for h in range(H):
                dve.wait_ge(S["m_scores"], at("m_scores", L, h + 1))
                for d in range(2):
                    mask = (fwd_mask, bwd_mask)[d]
                    for s in range(NT):
                        c0, c1, p0 = m_cols(d, s)
                        if d == 0:
                            mk = mask if s == 0 else mask[:, 0:P]
                        else:
                            mk = mask[:, P:2 * P] if s == 0 else mask
                        dve.scalar_tensor_tensor(m_e[:, d, p0:p0 + c1 - c0], m_bc[:, d, c0:c1],
                                                 g_cols[:, 0, d, s, d * H + h:d * H + h + 1], mk, ALU.add, ALU.min)\
                           .then_inc(S["m_arg"], 1)
                for d in range(2):
                    dve.wait_ge(S["m_exp"], at("m_exp", L, 2 * h + d + 1))
                    if h:
                        dve.wait_ge(S["m_num"], at("m_num", L, 2 * h - 1 + d))
                    for s in range(NT):
                        c0, c1, p0 = m_cols(d, s)
                        dve.tensor_tensor(m_pt[:, d, p0:p0 + c1 - c0], m_w[:, d, p0:p0 + c1 - c0],
                                          m_s[:, s, c0:c1], ALU.mult).then_inc(S["m_p"], 1)
                split_lo(dve, turn, [22 + 2 * h, 23 + 2 * h])
                nums = [bank[:, 2 + d, 0:258].rearrange("p (i e) -> p i e", i=NT) for d in range(2)]
                for d in range(2):
                    dve.wait_ge(S["m_num"], at("m_num", L, 2 * h + d + 1))
                    dve.tensor_tensor(m_den[:, h, d, :], nums[d][:, :, P], g_em[:, d, :, d * H + h], ALU.max)\
                       .then_inc(S["m_abs"], 1)
                for d in range(2):
                    dve.wait_ge(S["m_abs"], at("m_abs", L, 2 * h + d + 1))
                    dve.scalar_tensor_tensor(m_den[:, h, d, :], nums[d][:, :, P], -1.0, m_den[:, h, d, :],
                                             ALU.mult, ALU.max).then_inc(S["m_den"], 1)
                dve.wait_ge(S["m_den"], at("m_den", L, 2 * h + 2))
                dve.reciprocal(m_rd[:, h], m_den[:, h]).then_inc(S["m_rden"], 1)
                dve.wait_ge(S["m_rden"], at("m_rden", L, h + 1))
                for i in range(NT):
                    dve.tensor_scalar(cell[:, i, h * P:(h + 1) * P], nums[0][:, i, 0:P], m_rd[:, h, 0, i:i + 1], None,
                                      ALU.mult).then_inc(S["m_fwd"], 1)
                for i in range(NT):
                    dve.wait_ge(S["m_fwd"], at("m_fwd", L, 2 * h + i + 1))
                    dve.scalar_tensor_tensor(cell[:, i, h * P:(h + 1) * P], nums[1][:, i, 0:P],
                                             m_rd[:, h, 1, i:i + 1], cell[:, i, h * P:(h + 1) * P], ALU.mult, ALU.add)\
                       .then_inc(S["m_cell"], 1)
            dve.wait_ge(S["m_ss"], at("m_ss", L))
            dve.tensor_scalar(var[:, 0:8], ss[:, 0:8], 1.0 / P, NORM_EPS, ALU.mult, ALU.add).then_inc(S["m_var"], 1)
            dve.wait_ge(S["m_rstd"], at("m_rstd", L))
            dve.tensor_tensor(cell.rearrange("p i (h v) -> p (i h) v", h=H), cell.rearrange("p i (h v) -> p (i h) v", h=H),
                              rstd[:, 0:8].unsqueeze(2).broadcast_to([P, 8, P]), ALU.mult).then_inc(S["m_norm"], 1)
            dve.wait_ge(S["m_norm"], at("m_norm", L))
            dve.wait_ge(S["mo_gain"], at("mo_gain", L))
            dve.scalar_tensor_tensor(mlout, cell, 0.5, gm, ALU.mult, ALU.mult).then_inc(S["m_out"], 1)
            dve.wait_ge(S["aqk_out"], at("aqk_out", L))
            heads = 2 * AH
            n = 0
            for i in range(NT):
                v = aqk[:, i, :].rearrange("p (h c) -> p h c", c=DH)
                t1, t2 = v[:, :, 0:ROT], v[:, :, ROT:2 * ROT]
                cb, sb_ = (a[:, i:i + 1, :].broadcast_to([P, heads, ROT]) for a in (cos, sin))
                ra, rb, rc, rd = (b_[:, 0 + o * 128:128 + o * 128].rearrange("p (h c) -> p h c", c=ROT)
                                  for b_ in (rot_t, rot_u) for o in (2 * i, 2 * i + 1))
                for o, a, b in ((ra, t1, cb), (rb, t2, sb_), (rc, t2, cb), (rd, t1, sb_)):
                    dve.tensor_tensor(o, a, b, ALU.mult).then_inc(S["rot"], 1)
                    n += 1
                dve.wait_ge(S["rot"], at("rot", L, n))
                dve.tensor_tensor(t1, ra, rb, ALU.subtract).then_inc(S["rot"], 1)
                dve.tensor_tensor(t2, rc, rd, ALU.add).then_inc(S["rot"], 1)
                n += 2
            split_lo(dve, turn, range(30, 34))
            for h in range(AH):
                for i in range(NT):
                    dve_hold(dve, S["a_scores"], at("a_scores", L, h + 1))
                    if h >= 2:
                        dve_hold(dve, S["a_exp"], at("a_exp", L, 2 * h - 3 + i))
                    dve.tensor_tensor_reduce(a_s[:, h % 2, i, :], bank[:, 4 + h % 2, i * T:(i + 1) * T],
                                             at_mask[:, i, :], -float(DH) ** -0.5, 1e30, ALU.add, ALU.min,
                                             a_mx[:, h, i:i + 1]).then_inc(S["a_masked"], 1)
            dve.wait_ge(S["a_exp"], at("a_exp", L))
            dve.reciprocal(a_rs, a_sum).then_inc(S["a_rden"], 1)
            dve.wait_ge(S["a_rden"], at("a_rden", L))
            dve.wait_ge(S["m_out"], at("m_out", L))
            dve.wait_ge(S["a_o"], at("a_o", L))
            for i in range(NT):
                ins = dve.tensor_tensor(a_out[:, i, :].rearrange("p (h c) -> p h c", h=AH),
                                        bank[:, 2 + i, :].rearrange("p (h c) -> p h c", h=AH),
                                        a_rs[:, :, i:i + 1].broadcast_to([P, AH, DH]), ALU.mult)
            ins.then_inc(S["a_out"], 1)
            for a in range(2):
                dve.wait_ge(S["m_hi"], at("m_hi", L, a + 1))
                dve.tensor_tensor(xt_lo[:, 4 * a:4 * a + 4, :], turned[:, 4 * a:4 * a + 4, :],
                                  f32(xt_hi[:, 4 * a:4 * a + 4, :]), ALU.subtract).then_inc(S["m_lo"], 1)
            split_lo(dve, turn, range(34, 36))

        def pool_mix2(pool, L):
            pool.dma_start(rows[:, 1, 0:512], A["mlstm_norm_gain_2"][bass.ds(L, 1), :].rearrange("a n -> (a n)")
                           .partition_broadcast(P)).then_inc(S["mixrows2"], 16)
            pool.dma_start(rows[:, 1, 512:512 + NG], A["gate_bias_2"][bass.ds(L, 1), :, :]
                           .rearrange("a k h -> (a k h)").partition_broadcast(P)).then_inc(S["mixrows2"], 16)
            pool.memset(xp[:, :, 0:2], 0.0).then_inc(S["margins"], 1)
            pool.memset(xp[:, :, T + 2:T + 4], 0.0).then_inc(S["margins"], 1)
            pool.memset(va[:, :, :, P:P + 1], 1.0).then_inc(S["margins"], 1)
            pool.wait_ge(S["m_var"], at("m_var", L))
            pool.tensor_tensor(rstd[:, 0:8], var[:, 0:8], neg_half[:, :], ALU.pow).then_inc(S["m_rstd"], 1)

        block = ctx.enter_context(nc.Block())

        def turns1(L):
            t = L * LAYER1_TURNS
            return t, t + FFN_TURNS, t + (FFN_TURNS + MIX1_UNITS // RING)

        def turns2(L):
            t = L * LAYER2_TURNS + DEPTH * LAYER1_TURNS
            return t, t + FFN_TURNS, t + (FFN_TURNS + MIX2_UNITS // RING)

        def ln_cols(j):
            return ln_now[:, 0, j, :], ln_now[:, 1, j, :]

        def of_layer(w, L):
            return w[bass.ds(L, 1)].rearrange("l k c -> (l k) c")

        def of_half(w, L, j):
            return w[bass.ds(L, 1), j].rearrange("l k c -> (l k) c")

        @block.sync
        def _(sp):
            sp.dma_start(const[:, 0:P], A["shape_constants"][:, 0:P]).then_inc(S["const_in"], 16)
            for i in range(NT):
                sp.dma_start(xh[:, i, :], A["x"][0, i * P:(i + 1) * P, :]).then_inc(S["x_in"], 16)
            sp.wait_ge(S["tables_in"], 16 * 9)
            with sp.Fori(0, DEPTH) as L:
                t_ffn1, t_mix, t_ffn2 = turns1(L)
                sp_ffn(sp, t_ffn1, of_layer(A["ffn1_w13"], L), of_layer(A["ffn1_w2"], L))
                sp_mix1(sp, t_mix, of_layer(A["w_in"], L), of_layer(A["w_branch_a"], L),
                        of_layer(A["w_branch_b"], L), of_layer(A["w_out"], L))
                sp_ffn(sp, t_ffn2, of_layer(A["ffn2_w13"], L), of_layer(A["ffn2_w2"], L))
            with sp.Fori(0, DEPTH) as L:
                t_ffn1, t_mix, t_ffn2 = turns2(L)
                sp_ffn(sp, t_ffn1, of_half(A["ffn_w_in_2"], L, 0), of_half(A["ffn_w_out_2"], L, 0))
                sp_mix2(sp, t_mix, of_layer(A["mix_w_in_2"], L), of_layer(A["mix_w_out_2"], L))
                sp_ffn(sp, t_ffn2, of_half(A["ffn_w_in_2"], L, 1), of_half(A["ffn_w_out_2"], L, 1))
            for i in range(NT):
                sp.wait_ge(S["x_ready"], norm_done(6 * DEPTH - 1, i + 1))
                sp.dma_start(out[0, i * P:(i + 1) * P, :], x[:, i, :]).then_inc(S["x_out"], 16)
            sp.wait_ge(S["x_out"], 32)

        @block.gpsimd
        def _(pool):
            pool.memset(neg_half[:, :], -0.5).then_inc(S["ones_set"], 1)
            pool.memset(ones8[:, :], 1.0).then_inc(S["ones_set"], 1)
            pool.memset(ln_tab[:, 0, 0, :], 1.0).then_inc(S["ones_set"], 1)
            pool.memset(ln_tab[:, 1, 0, :], 0.0).then_inc(S["ones_set"], 1)
            for i in range(NT):
                pool.wait_ge(S["x_in"], 16 * NT)
                pool.tensor_copy(x[:, i, :], xh[:, i, :]).then_inc(S["x_ready"], 1)
            pool.wait_ge(S["hi_ready"], 6)
            pool.dma_start(sel[:, :, :], A["row_selectors"]).then_inc(S["rest_in"], 16)
            pool.dma_start(const[:, P:], A["shape_constants"][:, P:]).then_inc(S["rest_in"], 16)
            pool.wait_ge(S["ones_set"], 2)
            with pool.Fori(0, DEPTH) as L:
                pool_hold(pool, S["x_ready"], norm_done(3 * L - 1))
                load_ln_rows(pool, L, 0)
                pool_layer_norm(pool, 3 * L)
                pool_turn(pool, 3 * L + 1)
                pool_residual(pool, 3 * L)
                pool_mix1(pool, L)
                load_ln_rows(pool, L, 1)
                pool_layer_norm(pool, 3 * L + 1)
                pool_turn(pool, 3 * L + 2)
                pool_residual(pool, 3 * L + 1)
                pool_hold(pool, S["x_ready"], norm_done(3 * L + 1))
                load_ln_rows(pool, L, 2)
                pool_layer_norm(pool, 3 * L + 2)
                pool_residual(pool, 3 * L + 2)
            with pool.Fori(0, DEPTH) as L:
                pool_hold(pool, S["x_ready"], norm_done(3 * L + 5))
                for i in range(NT):
                    pool_pre(pool, 3 * L, i)
                pool_turn(pool, 3 * L + 6)
                load_post_row(pool, L, 1)
                pool.dma_start(wg32[:, :, :], A["mix_w_in_2"][bass.ds(L, 1), :, 3584:3600]
                               .rearrange("l (k p) c -> p (l k) c", p=P)).then_inc(S["wg_in"], 16)
                pool_post_pre(pool, 3 * L)
                pool_hold(pool, S["x_ready"], norm_done(3 * L + 6))
                load_post_row(pool, L, 3)
                pool_mix2(pool, L)
                pool_post_pre(pool, 3 * L + 1)
                pool_hold(pool, S["x_ready"], norm_done(3 * L + 7))
                load_post_row(pool, L, 5)
                for i in range(NT):
                    pool_post(pool, 3 * L + 2, i)

        @block.scalar
        def _(act):
            tab = lambda name, pat: A[name].rearrange(pat, p=P)
            for dst, src in ((t_rows[0:48, 0, :], tab("ln_g", "l j (k p) -> (l j k) p")),
                             (t_rows[48:96, 0, :], tab("ln_b", "l j (k p) -> (l j k) p")),
                             (t_rows[0:96, 1, :], tab("norm_gain_2", "l j (k p) -> (l j k) p")),
                             (t_rows[0:40, 2, :], tab("conv_w_2", "l j (k p) -> l (j k) p")[0]),
                             (t_rows[40:48, 2, :], tab("conv_b_2", "l (k p) -> l k p")[0]),
                             (t_rows[48:88, 2, :], tab("conv_w_2", "l j (k p) -> l (j k) p")[1]),
                             (t_rows[88:96, 2, :], tab("conv_b_2", "l (k p) -> l k p")[1]),
                             (t_rows[0:8, 3, :], tab("sg_bs", "l g p -> (l g) p")),
                             (t_rows[8:16, 3, :], tab("hg_lb", "l (k p) -> (l k) p"))):
                act.dma_start(dst, src).then_inc(S["tables_in"], 16)
            act.wait_ge(S["lb_step"], 3)
            act.activation(lb_tmp[:, 3:5, :], lb_tmp[:, 1:3, :], ACT.Exp).then_inc(S["lb_exp"], 1)
            with act.Fori(0, DEPTH) as L:
                t_ffn1, t_mix, t_ffn2 = turns1(L)
                split_hi(act, t_ffn1, range(2))
                act.wait_ge(S["now1"], at("now1", L))
                act_turn_both(act, 3 * L, *ln_cols(0))
                split_hi(act, t_ffn1, range(2, 4))
                act_ffn(act, t_ffn1, L * 2 * STEPS)
                split_hi(act, t_mix, range(2))
                act_layer_norm(act, 3 * L)
                act_turn_both(act, 3 * L + 1, *ln_cols(1))
                split_hi(act, t_mix, range(2, 4))
                act_mix1(act, L, t_mix)
                split_hi(act, t_ffn2, range(2))
                act_layer_norm(act, 3 * L + 1)
                act_turn_both(act, 3 * L + 2, *ln_cols(2))
                split_hi(act, t_ffn2, range(2, 4))
                act_ffn(act, t_ffn2, L * 2 * STEPS + STEPS)
                act_layer_norm(act, 3 * L + 2)
            with act.Fori(0, DEPTH) as L:
                t_ffn1, t_mix, t_ffn2 = turns2(L)
                split_hi(act, t_ffn1, [0])
                for i in range(NT):
                    act_pre(act, 3 * L, 3 * L + 5, i)
                act.wait_ge(S["now2"], at("now2", L))
                act_turn_both(act, 3 * L + 6, gain_now[:, 0, :], None)
                split_hi(act, t_ffn1, range(1, 4))
                act_ffn(act, t_ffn1, L * 2 * STEPS + 2 * DEPTH * STEPS)
                split_hi(act, t_mix, range(2))
                act_post_pre(act, 3 * L, 3 * L + 6, used_after(t_ffn1, FFN_UNITS - 1), gain_now[:, 2, :])
                split_hi(act, t_mix, range(2, 4))
                act_mix2(act, L, t_mix)
                split_hi(act, t_ffn2, range(2))
                act_post_pre(act, 3 * L + 1, 3 * L + 7, used_after(t_mix, MIX2_UNITS - 1), gain_now[:, 4, :])
                split_hi(act, t_ffn2, range(2, 4))
                act_ffn(act, t_ffn2, L * 2 * STEPS + (2 * DEPTH + 1) * STEPS)
                for i in range(NT):
                    act_post(act, 3 * L + 2, i, used_after(t_ffn2, FFN_UNITS - 1))

        @block.vector
        def _(dve):
            dve.sem_inc(S["lo_ready"], RING)
            dve.wait_ge(S["x_in"], 16 * NT)
            dve.sem_inc(S["ln_xhat"], NT)
            dve.wait_ge(S["tables_turned"], 1)
            c = [bank[:, 0, j * P:(j + 1) * P] for j in range(4)]
            for n, (dst, src) in enumerate((
                    (ln_tab[:, 0, 1:7, :], c[0][:, 0:48]), (ln_tab[:, 1, 1:7, :], c[0][:, 48:96]),
                    (gain_tab, c[1][:, 0:96]), (conv_tab, c[2][:, 0:96]),
                    (sgb_tab, c[3][:, 0:8]), (lbr_tab, c[3][:, 8:16]))):
                pat = {3: "p (a k) -> p a k", 4: "p (l j k) -> p l j k"}[len(dst.shape)]
                src = src.rearrange(pat, k=dst.shape[-1]) if len(dst.shape) == 3 else \
                    src.rearrange(pat, k=dst.shape[-1], j=dst.shape[-2])
                dve.tensor_copy(dst, src).then_inc(S["tables_out"], 1)
            dve.wait_ge(S["tables_out"], 6)
            mx, e = lb_tmp[:, 0, :], lb_tmp[:, 3:5, :]
            dve.tensor_tensor(mx, lbr_tab[:, 0, :], lbr_tab[:, 1, :], ALU.max).then_inc(S["lb_step"], 1)
            dve.wait_ge(S["lb_step"], 1)
            for l in range(2):
                dve.tensor_tensor(lb_tmp[:, 1 + l, :], lbr_tab[:, l, :], mx, ALU.subtract).then_inc(S["lb_step"], 1)
            dve.wait_ge(S["lb_exp"], 1)
            dve.tensor_tensor(lb_tmp[:, 5, :], e[:, 0, :], e[:, 1, :], ALU.add).then_inc(S["lb_step"], 1)
            dve.wait_ge(S["lb_step"], 4)
            dve.reciprocal(mx, lb_tmp[:, 5, :]).then_inc(S["lb_step"], 1)
            dve.wait_ge(S["lb_step"], 5)
            dve.tensor_tensor(lb_tab[:, 1, :], e[:, 1, :], mx, ALU.mult).then_inc(S["lb_step"], 1)
            dve.memset(lb_tab[:, 0, :], 0.0).then_inc(S["lb_step"], 1)
            dve.wait_ge(S["lb_step"], 7)
            dve.tensor_scalar(om_tab, lb_tab, -1.0, 1.0, ALU.mult, ALU.add).then_inc(S["lb_step"], 1)
            dve.wait_ge(S["lb_step"], 8)
            dve.wait_ge(S["ones_set"], 4)
            dve.wait_ge(S["const_in"], 16)
            with dve.Fori(0, DEPTH) as L:
                t_ffn1, t_mix, t_ffn2 = turns1(L)
                for g in range(2):
                    dve.tensor_copy(ln_now[:, g, :, :], ln_tab[:, g, bass.ds(3 * L, 3), :]).then_inc(S["now1"], 1)
                for dst, src in ((sgb_now, sgb_tab), (lb_now, lb_tab), (om_now, om_tab)):
                    dve.tensor_copy(dst.unsqueeze(1), src[:, bass.ds(L, 1), :]).then_inc(S["now1"], 1)
                split_lo(dve, t_ffn1, [0])
                dve_hold(dve, S["now1"], at("now1", L))
                for i in range(NT):
                    dve_turn(dve, 3 * L, i, *ln_cols(0), alone=True)
                split_lo(dve, t_ffn1, range(1, 4))
                dve_ffn(dve, t_ffn1, L * 2 * STEPS)
                split_lo(dve, t_mix, range(2))
                dve_layer_norm(dve, 3 * L, 3 * L + 1, used_after(t_ffn1, FFN_UNITS - 1), ln_cols(1))
                split_lo(dve, t_mix, range(2, 4))
                dve_mix1(dve, L, t_mix)
                split_lo(dve, t_ffn2, range(2))
                dve_layer_norm(dve, 3 * L + 1, 3 * L + 2, used_after(t_mix, MIX1_UNITS - 1), ln_cols(2))
                split_lo(dve, t_ffn2, range(2, 4))
                dve_ffn(dve, t_ffn2, L * 2 * STEPS + STEPS)
                dve_layer_norm(dve, 3 * L + 2, None, used_after(t_ffn2, FFN_UNITS - 1), None)
            with dve.Fori(0, DEPTH) as L:
                t_ffn1, t_mix, t_ffn2 = turns2(L)
                dve_hold(dve, S["x_ready"], norm_done(3 * L + 5))
                for dst, src in ((gain_now, gain_tab), (conv_now, conv_tab)):
                    dve.tensor_copy(dst.unsqueeze(1), src[:, bass.ds(L, 1), :, :]).then_inc(S["now2"], 1)
                split_lo(dve, t_ffn1, [0])
                dve_hold(dve, S["now2"], at("now2", L))
                dve_pre(dve, 3 * L, gain_now[:, 0, :])
                split_lo(dve, t_ffn1, range(1, 4))
                dve_ffn(dve, t_ffn1, L * 2 * STEPS + 2 * DEPTH * STEPS)
                split_lo(dve, t_mix, range(2))
                dve_post_pre(dve, 3 * L, 0.5, used_after(t_ffn1, FFN_UNITS - 1), gain_now[:, 2, :])
                split_lo(dve, t_mix, range(2, 4))
                dve_mix2(dve, L, t_mix)
                split_lo(dve, t_ffn2, range(2))
                dve_post_pre(dve, 3 * L + 1, 1.0, used_after(t_mix, MIX2_UNITS - 1), gain_now[:, 4, :])
                split_lo(dve, t_ffn2, range(2, 4))
                dve_ffn(dve, t_ffn2, L * 2 * STEPS + (2 * DEPTH + 1) * STEPS)
                for i in range(NT):
                    dve_post_scale(dve, 3 * L + 2, i, 0.5, used_after(t_ffn2, FFN_UNITS - 1))
                    dve_post_add(dve, 3 * L + 2, i)

        @block.tensor
        def _(pe):
            pe.sem_inc(S["weights_used"], RING)
            pe.wait_ge(S["const_in"], 16)
            pe.wait_ge(S["tables_in"], 16 * 9)
            for j in range(3):
                pe.transpose(bank[:, 0, j * P:j * P + 96], t_rows[0:96, j, :], ident[0:96, 0:96])
            pe.transpose(bank[:, 0, 3 * P:3 * P + 16], t_rows[0:16, 3, :], ident[0:16, 0:16])\
              .then_inc(S["tables_turned"], 1)
            with pe.Fori(0, DEPTH) as L:
                t_ffn1, t_mix, t_ffn2 = turns1(L)
                pe_turn(pe, S["ln_xhat"], lambda i: xhat_done(3 * L - 1, i + 1))
                pe_ffn(pe, t_ffn1, L * 2 * STEPS, 3 * L)
                pe_turn(pe, S["ln_xhat"], lambda i: xhat_done(3 * L, i + 1))
                pe_mix1(pe, L, t_mix, 3 * L + 1)
                pe_turn(pe, S["ln_xhat"], lambda i: xhat_done(3 * L + 1, i + 1))
                pe_ffn(pe, t_ffn2, L * 2 * STEPS + STEPS, 3 * L + 2)
            with pe.Fori(0, DEPTH) as L:
                t_ffn1, t_mix, t_ffn2 = turns2(L)
                pe_turn(pe, S["pre_xhat"], lambda i: at("pre_xhat", 3 * L, i + 1))
                pe_ffn(pe, t_ffn1, L * 2 * STEPS + 2 * DEPTH * STEPS, 3 * L + 6)
                pe_turn(pe, S["pre_xhat"], lambda i: at("pre_xhat", 3 * L + 1, i + 1))
                pe_mix2(pe, L, t_mix, 3 * L + 7)
                pe_turn(pe, S["pre_xhat"], lambda i: at("pre_xhat", 3 * L + 2, i + 1))
                pe_ffn(pe, t_ffn2, L * 2 * STEPS + (2 * DEPTH + 1) * STEPS, 3 * L + 8)


def shape_constants():
    import numpy as np
    s = np.arange(P)[:, None]
    t = np.arange(P)[None, :]
    hg = [(s == t)]
    for b in LEVELS[1:6]:
        hg.append((s // (2 * b) == t // (2 * b)) & (s % (2 * b) < b) & (t % (2 * b) >= b))
    i = np.arange(T)[:, None]
    j = np.arange(T)[None, :]
    count = np.zeros((T, T))
    for window, dilation in ((128, 1), (512, 4), (2048, 16)):
        side = (window // 2) // dilation
        count += ((i - j) % dilation == 0) & (np.abs(i // dilation - j // dilation) <= side)
    logs = np.where(count > 0, np.log(np.maximum(count, 1)) * DH ** 0.5, -1e30)
    logs = logs.reshape(NT, P, T).transpose(1, 0, 2).reshape(P, NT * T)
    none = np.zeros((P, P))
    fwd = np.concatenate([np.where(s <= t, 0.0, -1e30), none], 1)
    bwd = np.concatenate([none, np.where(s >= t, 0.0, -1e30)], 1)
    freq = np.float32(500000.0) ** (-np.arange(ROT, dtype=np.float32) / np.float32(ROT))
    ang = (np.arange(T, dtype=np.float32)[:, None] * freq[None, :]).astype(np.float32)
    turn = [f(ang).reshape(NT, P, ROT).transpose(1, 0, 2).reshape(P, NT * ROT) for f in (np.cos, np.sin)]
    table = np.concatenate([np.eye(P), *[m.astype(float) for m in hg], logs, fwd, bwd, *turn], 1).astype(np.float32)
    rows = np.zeros((2 * H, 2 * H, P), np.float32)
    for k in range(2 * H):
        rows[k, k, :] = 1.0
    return table, rows


_INS = ["x", "ffn1_w13", "ffn1_w2", "ffn2_w13", "ffn2_w2", "ln_g", "ln_b", "w_in", "hg_lb", "hg_norm_g",
        "sg_ln_g", "sg_ln_b", "sg_ws", "sg_bs", "w_branch_a", "w_branch_b", "w_out", "norm_gain_2",
        "ffn_w_in_2", "ffn_w_out_2", "mix_w_in_2", "conv_w_2", "conv_b_2", "gate_bias_2",
        "mlstm_norm_gain_2", "mix_w_out_2"]


def kernel(**inputs):
    import numpy as _np
    import concourse.bacc as _bacc
    from concourse import mybir as _mybir
    from concourse.bass_utils import run_bass_kernel_spmd as _run

    nc = _bacc.Bacc("TRN2", target_bir_lowering=False, num_devices=1)
    arrays = {name: _np.ascontiguousarray(inputs[name]) for name in _INS}
    arrays["shape_constants"], arrays["row_selectors"] = shape_constants()
    aps = {name: nc.dram_tensor("in_" + name, a.shape, _mybir.dt.from_np(a.dtype), kind="ExternalInput").ap()
           for name, a in arrays.items()}
    out = nc.dram_tensor("out", (1, T, D), F32, kind="ExternalOutput").ap()
    build(nc, aps, out)
    r = _run(nc, [{"in_" + name: a for name, a in arrays.items()}], core_ids=[0])
    return r.results[0]["out"]
```
